# Optimizing a Trainium2 kernel written in Bass

```python
import math
import jax, jax.numpy as jnp
from jax import lax
import numpy as np

D_MODEL = 1024
BATCH = 1
SEQ = 1024
DEPTH = 2

N_MIXERS = 4
CONV_WIDTH = 3
CONV_DIM = D_MODEL
DIL_WINDOWS = (128, 512, 2048)
DIL_RATES = (1, 4, 16)
DIL_HEADS = 8
DIL_HEAD_DIM = D_MODEL // DIL_HEADS
DIL_DIM = DIL_HEADS * DIL_HEAD_DIM
SWA_HALF = 128
SWA_Q_HEADS = 16
SWA_KV_HEADS = 4
SWA_HEAD_DIM = 64
SWA_DIM = SWA_Q_HEADS * SWA_HEAD_DIM
DIFF_HEADS = 8
DIFF_HEAD_DIM = D_MODEL // (2 * DIFF_HEADS)
DIFF_DIM = DIFF_HEADS * 2 * DIFF_HEAD_DIM
Q_BLOCK = 128

ROPE_THETA = 10000.0
NORM_EPS = 1e-6
SUBLN_EPS = 1e-5
NEG_INF = -1e30


def _layers_of_type(t):
    return len(range(t, DEPTH, N_MIXERS))

def rms_norm(x, g, eps):
    xf = x.astype(jnp.float32)
    y = xf * lax.rsqrt(jnp.mean(xf * xf, axis=-1, keepdims=True) + eps)
    return (y * g.astype(jnp.float32)).astype(x.dtype)

def rope_tables(seq, dim):
    inv = ROPE_THETA ** (-jnp.arange(0, dim, 2, dtype=jnp.float32) / dim)
    ang = jnp.arange(seq, dtype=jnp.float32)[:, None] * inv[None, :]
    return jnp.cos(ang), jnp.sin(ang)

def apply_rope(x, cos, sin):
    shp = (cos.shape[0],) + (1,) * (x.ndim - 3) + (cos.shape[1],)
    cos, sin = cos.reshape(shp), sin.reshape(shp)
    x1, x2 = jnp.split(x.astype(jnp.float32), 2, axis=-1)
    return jnp.concatenate([x1 * cos - x2 * sin, x2 * cos + x1 * sin], axis=-1).astype(x.dtype)

def adaln_pre_norm(x, c, g, w_mod, b_mod):
    mod = jax.nn.silu(c) @ w_mod + b_mod
    shift, scale, gate = jnp.split(mod, 3, axis=-1)
    h = rms_norm(x, g, NORM_EPS) * (1.0 + scale[:, None, :]) + shift[:, None, :]
    return h, gate

def banded_attention(q, k, v, half, sink=None):
    N, L, Hk, G, D = q.shape
    Dv = v.shape[-1]
    blk = half
    nb = -(-L // blk)
    Lp = nb * blk
    qp = jnp.pad(q, ((0, 0), (0, Lp - L), (0, 0), (0, 0), (0, 0))).reshape(N, nb, blk, Hk, G, D)
    kv_pad = ((0, 0), (blk, Lp - L + blk), (0, 0), (0, 0))
    kp = jnp.pad(k, kv_pad).reshape(N, nb + 2, blk, Hk, D)
    vp = jnp.pad(v, kv_pad).reshape(N, nb + 2, blk, Hk, Dv)
    band = lambda t: jnp.concatenate([t[:, :-2], t[:, 1:-1], t[:, 2:]], axis=2)
    kw, vw = band(kp), band(vp)
    qpos = jnp.arange(Lp).reshape(nb, blk)
    kpos = (jnp.arange(nb)[:, None] - 1) * blk + jnp.arange(3 * blk)[None, :]
    kk = kpos[:, None, :]
    valid = (jnp.abs(kk - qpos[:, :, None]) <= half) & (kk >= 0) & (kk < L)
    scale = D ** -0.5
    sink_f = None if sink is None else sink.astype(jnp.float32)[None, :, :, None]

    def one(args):
        qs, ks, vs = args
        s = jnp.einsum('bqhgd,bkhd->bhgqk', qs, ks, preferred_element_type=jnp.float32) * scale
        s = jnp.where(valid[:, None, None], s, NEG_INF)
        m = jnp.max(s, axis=-1)
        if sink_f is not None:
            m = jnp.maximum(m, sink_f)
        p = jnp.exp(s - m[..., None])
        l = jnp.sum(p, axis=-1)
        if sink_f is not None:
            l = l + jnp.exp(sink_f - m)
        o = jnp.einsum('bhgqk,bkhe->bqhge', p, vs.astype(jnp.float32))
        l_t = jnp.moveaxis(l, -1, 1)
        return o / l_t[..., None], jnp.moveaxis(m, -1, 1) + jnp.log(l_t)

    o, lse = lax.map(one, (qp, kw, vw))
    o = o.reshape(N, Lp, Hk, G, Dv)[:, :L]
    lse = lse.reshape(N, Lp, Hk, G)[:, :L]
    return o, lse

def to_strided(x, r):
    B, S = x.shape[:2]
    rest = x.shape[2:]
    x = x.reshape((B, S // r, r) + rest)
    return jnp.moveaxis(x, 2, 1).reshape((B * r, S // r) + rest)

def from_strided(x, r, B):
    L = x.shape[1]
    rest = x.shape[2:]
    x = x.reshape((B, r, L) + rest)
    return jnp.moveaxis(x, 1, 2).reshape((B, L * r) + rest)

def short_conv_mixer(h, w_in, conv_k, w_out):
    b_gate, c_gate, xin, z = jnp.split(h @ w_in, 4, axis=-1)
    t = c_gate * xin
    E = t.shape[-1]
    pad = (CONV_WIDTH - 1) // 2
    conv = lax.conv_general_dilated(
        t, conv_k.astype(t.dtype)[:, None, :], window_strides=(1,), padding=[(pad, pad)],
        dimension_numbers=('NWC', 'WIO', 'NWC'), feature_group_count=E)
    return (b_gate * conv * jax.nn.silu(z)) @ w_out

def dilated_mixer(h, w_in, w_out, cos, sin):
    B, S, _ = h.shape
    G, H, Dh = len(DIL_RATES), DIL_HEADS, DIL_HEAD_DIM
    E = H * Dh
    q, k, v, z = jnp.split(h @ w_in, [G * E, 2 * G * E, 2 * G * E + E], axis=-1)
    q = apply_rope(q.reshape(B, S, G, H, Dh), cos, sin)
    k = apply_rope(k.reshape(B, S, G, H, Dh), cos, sin)
    v = v.reshape(B, S, H, Dh)
    outs, lses = [], []
    for g in range(G):
        r = DIL_RATES[g]
        half = DIL_WINDOWS[g] // (2 * r)
        o, lse = banded_attention(to_strided(q[:, :, g], r)[:, :, :, None],
                                  to_strided(k[:, :, g], r), to_strided(v, r), half)
        outs.append(from_strided(o[:, :, :, 0], r, B))
        lses.append(from_strided(lse[..., 0], r, B))
    wts = jax.nn.softmax(jnp.stack(lses, axis=0), axis=0)
    o = jnp.sum(wts[..., None] * jnp.stack(outs, axis=0), axis=0)
    y = o.reshape(B, S, E).astype(h.dtype) * jax.nn.silu(z)
    return y @ w_out

def window_gqa_mixer(h, w_in, sink, w_out, cos, sin):
    B, S, _ = h.shape
    Hq, Hk, Dh = SWA_Q_HEADS, SWA_KV_HEADS, SWA_HEAD_DIM
    G = Hq // Hk
    q, k, v, z = jnp.split(h @ w_in, [Hq * Dh, Hq * Dh + Hk * Dh, Hq * Dh + 2 * Hk * Dh], axis=-1)
    q = apply_rope(q.reshape(B, S, Hk, G, Dh), cos, sin)
    k = apply_rope(k.reshape(B, S, Hk, Dh), cos, sin)
    v = v.reshape(B, S, Hk, Dh)
    o, _ = banded_attention(q, k, v, SWA_HALF, sink.reshape(Hk, G))
    y = o.reshape(B, S, Hq * Dh).astype(h.dtype) * jax.nn.silu(z)
    return y @ w_out

def diff_attention_mixer(h, w_in, lam_vecs, subln_g, w_out, cos, sin, layer_idx):
    B, S, _ = h.shape
    H, d = DIFF_HEADS, DIFF_HEAD_DIM
    q, k, v, z = jnp.split(h @ w_in, 4, axis=-1)
    q = apply_rope(q.reshape(B, S, H, 2, d), cos, sin)
    k = apply_rope(k.reshape(B, S, H, 2, d), cos, sin)
    v = v.reshape(B, S, H, 2 * d).astype(jnp.float32)
    lam_init = 0.8 - 0.6 * math.exp(-0.3 * layer_idx)
    lv = lam_vecs.astype(jnp.float32)
    lam = jnp.exp(jnp.sum(lv[0] * lv[1])) - jnp.exp(jnp.sum(lv[2] * lv[3])) + lam_init
    nb = S // Q_BLOCK
    qb = jnp.moveaxis(q.reshape(B, nb, Q_BLOCK, H, 2, d), 1, 0)
    scale = d ** -0.5

    def block(qs):
        s = jnp.einsum('bqhcd,bkhcd->bhcqk', qs, k, preferred_element_type=jnp.float32) * scale
        p = jax.nn.softmax(s, axis=-1)
        a = p[:, :, 0] - lam * p[:, :, 1]
        return jnp.einsum('bhqk,bkhe->bqhe', a, v)

    o = jnp.moveaxis(lax.map(block, qb), 0, 1).reshape(B, S, H, 2 * d)
    o = rms_norm(o, subln_g, SUBLN_EPS) * (1.0 - lam_init)
    y = o.reshape(B, S, H * 2 * d).astype(h.dtype) * jax.nn.silu(z)
    return y @ w_out

def first_inputs(seed: int = 0) -> dict:
    key = jax.random.key(seed)
    ks = iter(jax.random.split(key, 32))
    nrm = lambda shape, s: jax.random.normal(next(ks), shape, jnp.float32) * s
    D = D_MODEL
    nA, nB, nC, nD = (_layers_of_type(t) for t in range(N_MIXERS))
    G = len(DIL_RATES)
    swa_in = 2 * SWA_DIM + 2 * SWA_KV_HEADS * SWA_HEAD_DIM
    return dict(
        x=nrm((BATCH, SEQ, D), 1.0),
        c=nrm((BATCH, D), 1.0),
        norm_g=1.0 + nrm((DEPTH, D), 0.02),
        w_mod=nrm((DEPTH, D, 3 * D), 0.5 * D ** -0.5),
        b_mod=nrm((DEPTH, 3 * D), 0.02),
        conv_w_in=nrm((nA, D, 4 * CONV_DIM), D ** -0.5),
        conv_k=nrm((nA, CONV_WIDTH, CONV_DIM), CONV_WIDTH ** -0.5),
        conv_w_out=nrm((nA, CONV_DIM, D), CONV_DIM ** -0.5),
        dil_w_in=nrm((nB, D, (2 * G + 2) * DIL_DIM), D ** -0.5),
        dil_w_out=nrm((nB, DIL_DIM, D), DIL_DIM ** -0.5),
        swa_w_in=nrm((nC, D, swa_in), D ** -0.5),
        swa_sink=nrm((nC, SWA_Q_HEADS), 1.0),
        swa_w_out=nrm((nC, SWA_DIM, D), SWA_DIM ** -0.5),
        diff_w_in=nrm((nD, D, 4 * DIFF_DIM), D ** -0.5),
        diff_lambda=nrm((nD, 4, DIFF_HEAD_DIM), 0.1),
        diff_subln_g=1.0 + nrm((nD, 2 * DIFF_HEAD_DIM), 0.02),
        diff_w_out=nrm((nD, DIFF_DIM, D), DIFF_DIM ** -0.5),
        final_g=1.0 + nrm((D,), 0.02),
    )

def first_block(x, c, norm_g, w_mod, b_mod, conv_w_in, conv_k, conv_w_out, dil_w_in, dil_w_out,
              swa_w_in, swa_sink, swa_w_out, diff_w_in, diff_lambda, diff_subln_g, diff_w_out,
              final_g):
    S = x.shape[1]
    cos_dil, sin_dil = rope_tables(S, DIL_HEAD_DIM)
    cos_swa, sin_swa = rope_tables(S, SWA_HEAD_DIM)
    cos_diff, sin_diff = rope_tables(S, DIFF_HEAD_DIM)
    for i in range(DEPTH):
        kind, j = i % N_MIXERS, i // N_MIXERS
        h, gate = adaln_pre_norm(x, c, norm_g[i], w_mod[i], b_mod[i])
        if kind == 0:
            y = short_conv_mixer(h, conv_w_in[j], conv_k[j], conv_w_out[j])
        elif kind == 1:
            y = dilated_mixer(h, dil_w_in[j], dil_w_out[j], cos_dil, sin_dil)
        elif kind == 2:
            y = window_gqa_mixer(h, swa_w_in[j], swa_sink[j], swa_w_out[j], cos_swa, sin_swa)
        else:
            y = diff_attention_mixer(h, diff_w_in[j], diff_lambda[j], diff_subln_g[j],
                                     diff_w_out[j], cos_diff, sin_diff, i)
        x = x + gate[:, None, :] * y
    return rms_norm(x, final_g, NORM_EPS)


DEPTH_2 = 1

N_MIXERS_2 = 2
N_A_LAYERS = (DEPTH_2 + N_MIXERS_2 - 1) // N_MIXERS_2
N_B_LAYERS = DEPTH_2 // N_MIXERS_2

A_HEADS = D_MODEL // 128
A_HEAD_DIM = 128
A_V_DIM = 128
Q_RANK = 256
KV_RANK = 256
IDX_HEADS = 8
IDX_DIM = 64
TOPK_MAX = 256
A_IN = Q_RANK + KV_RANK + IDX_DIM + IDX_HEADS

NUM_BUCKETS = 32
MAX_DISTANCE = 128

G_HEADS = 4
G_KD = D_MODEL // 2
G_VD = D_MODEL
G_DK = G_KD // G_HEADS
G_DV = G_VD // G_HEADS
G_RANK = 16
GATE_TAU = 16.0
CHUNK = 64
B_IN = 2 * G_KD + 2 * G_VD + G_RANK

D_FF = 2816

EPS = 1e-6


def rmsnorm(x, g):
    xf = x.astype(jnp.float32)
    y = xf * lax.rsqrt(jnp.mean(xf * xf, axis=-1, keepdims=True) + EPS)
    return (y * g.astype(jnp.float32)).astype(x.dtype)

def t5_bucket(dist):
    n = jnp.maximum(dist, 0)
    exact = NUM_BUCKETS // 2
    log_ratio = jnp.log(jnp.maximum(n, 1).astype(jnp.float32) / exact) / math.log(MAX_DISTANCE / exact)
    large = exact + (log_ratio * (NUM_BUCKETS - exact)).astype(jnp.int32)
    return jnp.where(n < exact, n, jnp.minimum(large, NUM_BUCKETS - 1))

def dsa_mixer(h, rel_bias, w_in, g_cq, g_ckv, w_uq, w_uk, w_uv, w_qi, w_o):
    B, T, _ = h.shape
    c_q, c_kv, k_idx, w_idx = jnp.split(
        h @ w_in, [Q_RANK, Q_RANK + KV_RANK, Q_RANK + KV_RANK + IDX_DIM], axis=-1)
    c_q = rmsnorm(c_q, g_cq)
    c_kv = rmsnorm(c_kv, g_ckv)
    q = (c_q @ w_uq).reshape(B, T, A_HEADS, A_HEAD_DIM)
    q_lat = jnp.einsum('bthd,hdc->bthc', q, w_uk) * (A_HEAD_DIM ** -0.5)
    q_idx = (c_q @ w_qi).reshape(B, T, IDX_HEADS, IDX_DIM)
    w_idx = w_idx * (IDX_HEADS ** -0.5 * IDX_DIM ** -0.5)

    n_sel = min(TOPK_MAX, T // 4)
    n_blk = T // Q_BLOCK
    key_pos = jnp.arange(T, dtype=jnp.int32)

    def to_blocks(a):
        return a.reshape(B, n_blk, Q_BLOCK, *a.shape[2:]).swapaxes(0, 1)

    def attend_block(args):
        qb_lat, qb_idx, wb, start = args
        q_pos = start + jnp.arange(Q_BLOCK, dtype=jnp.int32)
        rel = jax.nn.relu(jnp.einsum('bqhd,bsd->bqhs', qb_idx, k_idx))
        score = jnp.einsum('bqh,bqhs->bqs', wb, rel).astype(jnp.float32)
        score = jnp.where(key_pos[None, None, :] <= q_pos[None, :, None], score, -jnp.inf)
        _, sel = lax.top_k(score, n_sel)
        kv_sel = jax.vmap(lambda a, i: a[i])(c_kv, sel.reshape(B, -1))
        kv_sel = kv_sel.reshape(B, Q_BLOCK, n_sel, KV_RANK)
        dist = q_pos[None, :, None] - sel
        bias = rel_bias[t5_bucket(dist)].transpose(0, 1, 3, 2)
        logits = (jnp.einsum('bqhc,bqkc->bqhk', qb_lat, kv_sel).astype(jnp.float32)
                  + bias.astype(jnp.float32))
        logits = jnp.where((dist >= 0)[:, :, None, :], logits, -jnp.inf)
        p = jax.nn.softmax(logits, axis=-1).astype(kv_sel.dtype)
        return jnp.einsum('bqhk,bqkc->bqhc', p, kv_sel)

    starts = jnp.arange(n_blk, dtype=jnp.int32) * Q_BLOCK
    o_lat = lax.map(attend_block, (to_blocks(q_lat), to_blocks(q_idx), to_blocks(w_idx), starts))
    o_lat = o_lat.swapaxes(0, 1).reshape(B, T, A_HEADS, KV_RANK)
    o = jnp.einsum('bthc,hcv->bthv', o_lat, w_uv).reshape(B, T, A_HEADS * A_V_DIM)
    return o @ w_o

def gla_mixer(h, w_in, w_g2, b_g, g_norm, w_o):
    B, T, _ = h.shape
    q, k, v, r, g_lr = jnp.split(
        h @ w_in, [G_KD, 2 * G_KD, 2 * G_KD + G_VD, 2 * G_KD + 2 * G_VD], axis=-1)
    log_a = jax.nn.log_sigmoid((g_lr @ w_g2 + b_g).astype(jnp.float32)) / GATE_TAU
    n_chk = T // CHUNK

    def heads_chunks(a, d):
        return a.astype(jnp.float32).reshape(B, n_chk, CHUNK, G_HEADS, d).transpose(1, 0, 3, 2, 4)

    qc = heads_chunks(q * (G_DK ** -0.5), G_DK)
    kc = heads_chunks(k, G_DK)
    vc = heads_chunks(v, G_DV)
    gc = heads_chunks(log_a, G_DK)
    idx = jnp.arange(CHUNK)
    causal = (idx[:, None] >= idx[None, :])[None, None, :, :, None]

    def step(S, inp):
        q_c, k_c, v_c, g_c = inp
        b = jnp.cumsum(g_c, axis=2)
        o_inter = jnp.einsum('bhik,bhkv->bhiv', q_c * jnp.exp(b), S)
        diff = jnp.where(causal, b[:, :, :, None, :] - b[:, :, None, :, :], -jnp.inf)
        attn = jnp.einsum('bhik,bhjk,bhijk->bhij', q_c, k_c, jnp.exp(diff))
        o_intra = jnp.einsum('bhij,bhjv->bhiv', attn, v_c)
        b_last = b[:, :, -1:, :]
        S = (S * jnp.exp(b_last[:, :, 0, :])[..., None]
             + jnp.einsum('bhjk,bhjv->bhkv', k_c * jnp.exp(b_last - b), v_c))
        return S, o_inter + o_intra

    S0 = jnp.zeros((B, G_HEADS, G_DK, G_DV), jnp.float32)
    _, o = lax.scan(step, S0, (qc, kc, vc, gc))
    o = o.transpose(1, 0, 3, 2, 4).reshape(B, T, G_HEADS, G_DV)
    o = rmsnorm(o, g_norm.reshape(G_HEADS, G_DV)).reshape(B, T, G_VD).astype(h.dtype)
    return (o * jax.nn.silu(r)) @ w_o

def conv_ffn(h, w_in, conv_w, conv_b, w_out):
    u, v = jnp.split(h @ w_in, 2, axis=-1)
    u = lax.conv_general_dilated(
        u, conv_w[:, None, :], window_strides=(1,), padding=[(CONV_WIDTH - 1, 0)],
        dimension_numbers=('NWC', 'WIO', 'NWC'), feature_group_count=D_FF) + conv_b
    return (jax.nn.gelu(u, approximate=False) * v) @ w_out

def second_inputs(seed: int = 0) -> dict:
    key = jax.random.key(seed)
    ks = iter(jax.random.split(key, 40))
    f32 = jnp.float32

    def w(shape, fan_in):
        return jax.random.normal(next(ks), shape, f32) * fan_in ** -0.5

    def gain(shape):
        return 1.0 + 0.05 * jax.random.normal(next(ks), shape, f32)

    def small(shape, s=0.02):
        return s * jax.random.normal(next(ks), shape, f32)

    nA, nB = N_A_LAYERS, N_B_LAYERS
    return {
        "x": jax.random.normal(next(ks), (BATCH, SEQ, D_MODEL), f32),
        "c": jax.random.normal(next(ks), (BATCH, D_MODEL), f32),
        "rel_bias": small((NUM_BUCKETS, A_HEADS), 0.2),
        "a_w_in": w((nA, D_MODEL, A_IN), D_MODEL),
        "a_g_cq": gain((nA, Q_RANK)),
        "a_g_ckv": gain((nA, KV_RANK)),
        "a_w_uq": w((nA, Q_RANK, A_HEADS * A_HEAD_DIM), Q_RANK),
        "a_w_uk": w((nA, A_HEADS, A_HEAD_DIM, KV_RANK), A_HEAD_DIM),
        "a_w_uv": w((nA, A_HEADS, KV_RANK, A_V_DIM), KV_RANK),
        "a_w_qi": w((nA, Q_RANK, IDX_HEADS * IDX_DIM), Q_RANK),
        "a_w_o": w((nA, A_HEADS * A_V_DIM, D_MODEL), A_HEADS * A_V_DIM),
        "b_w_in": w((nB, D_MODEL, B_IN), D_MODEL),
        "b_w_g2": w((nB, G_RANK, G_KD), G_RANK),
        "b_b_g": small((nB, G_KD)),
        "b_g_norm": gain((nB, G_VD)),
        "b_w_o": w((nB, G_VD, D_MODEL), G_VD),
        "ada_w": w((DEPTH_2, D_MODEL, 6 * D_MODEL), D_MODEL),
        "ada_b": small((DEPTH_2, 6 * D_MODEL)),
        "g_mix": gain((DEPTH_2, D_MODEL)),
        "g_ffn": gain((DEPTH_2, D_MODEL)),
        "f_w_in": w((DEPTH_2, D_MODEL, 2 * D_FF), D_MODEL),
        "f_conv_w": w((DEPTH_2, CONV_WIDTH, D_FF), CONV_WIDTH),
        "f_conv_b": small((DEPTH_2, D_FF)),
        "f_w_out": w((DEPTH_2, D_FF, D_MODEL), D_FF),
        "g_final": gain((D_MODEL,)),
    }

def second_block(x, c, rel_bias, a_w_in, a_g_cq, a_g_ckv, a_w_uq, a_w_uk, a_w_uv, a_w_qi, a_w_o,
              b_w_in, b_w_g2, b_b_g, b_g_norm, b_w_o, ada_w, ada_b, g_mix, g_ffn,
              f_w_in, f_conv_w, f_conv_b, f_w_out, g_final):
    cond = jax.nn.silu(c)
    for i in range(DEPTH_2):
        mod = cond @ ada_w[i] + ada_b[i]
        sh_m, sc_m, gt_m, sh_f, sc_f, gt_f = jnp.split(mod[:, None, :], 6, axis=-1)
        h = rmsnorm(x, g_mix[i]) * (1 + sc_m) + sh_m
        j = i // N_MIXERS_2
        if i % N_MIXERS_2 == 0:
            y = dsa_mixer(h, rel_bias, a_w_in[j], a_g_cq[j], a_g_ckv[j], a_w_uq[j],
                          a_w_uk[j], a_w_uv[j], a_w_qi[j], a_w_o[j])
        else:
            y = gla_mixer(h, b_w_in[j], b_w_g2[j], b_b_g[j], b_g_norm[j], b_w_o[j])
        x = x + gt_m * y
        h = rmsnorm(x, g_ffn[i]) * (1 + sc_f) + sh_f
        x = x + gt_f * conv_ffn(h, f_w_in[i], f_conv_w[i], f_conv_b[i], f_w_out[i])
    return rmsnorm(x, g_final)


def setup_inputs(seed=0):
    out = dict(first_inputs(seed))
    for name, value in second_inputs(seed + 1).items():
        if name != "x":
            out[name + "_2"] = value
    return out


def reference(
    x, c, norm_g, w_mod, b_mod, conv_w_in, conv_k, conv_w_out, dil_w_in, dil_w_out, swa_w_in,
    swa_sink, swa_w_out, diff_w_in, diff_lambda, diff_subln_g, diff_w_out, final_g, c_2,
    rel_bias_2, a_w_in_2, a_g_cq_2, a_g_ckv_2, a_w_uq_2, a_w_uk_2, a_w_uv_2, a_w_qi_2, a_w_o_2,
    b_w_in_2, b_w_g2_2, b_b_g_2, b_g_norm_2, b_w_o_2, ada_w_2, ada_b_2, g_mix_2, g_ffn_2,
    f_w_in_2, f_conv_w_2, f_conv_b_2, f_w_out_2, g_final_2,
):
    x = first_block(
        x, c, norm_g, w_mod, b_mod, conv_w_in, conv_k, conv_w_out, dil_w_in, dil_w_out,
        swa_w_in, swa_sink, swa_w_out, diff_w_in, diff_lambda, diff_subln_g, diff_w_out,
        final_g,
    )
    return second_block(
        x, c_2, rel_bias_2, a_w_in_2, a_g_cq_2, a_g_ckv_2, a_w_uq_2, a_w_uk_2, a_w_uv_2,
        a_w_qi_2, a_w_o_2, b_w_in_2, b_w_g2_2, b_b_g_2, b_g_norm_2, b_w_o_2, ada_w_2, ada_b_2,
        g_mix_2, g_ffn_2, f_w_in_2, f_conv_w_2, f_conv_b_2, f_w_out_2, g_final_2,
    )


_drawn_inputs = setup_inputs


def setup_inputs(seed=0):
    import zlib

    import numpy as np

    out = dict(_drawn_inputs(seed))
    spreads = {}
    factors = {'norm_g': 4.194,
     'rel_bias_2': 4.321,
     'a_g_cq_2': 4.285,
     'a_g_ckv_2': 3.426,
     'g_mix_2': 3.22,
     'f_conv_b_2': 6.746}
    for name, (base, spread) in spreads.items():
        noise = np.random.default_rng([zlib.crc32(name.encode()), seed]).standard_normal(out[name].shape)
        drawn = base * np.exp(spread * noise) if base else spread * noise
        out[name] = __import__('jax').numpy.asarray(drawn.astype(out[name].dtype))
    for name, factor in factors.items():
        out[name] = (out[name] * factor).astype(out[name].dtype)
    return out
```

```python
from contextlib import ExitStack

import numpy as np

import concourse.bass as bass
from concourse import mybir

P = 128
F32 = mybir.dt.float32
F32R = mybir.dt.float32r
ALU = mybir.AluOpType
ACT = mybir.ActivationFunctionType
AX = mybir.AxisListType

T = 1024
D = 1024
KD = D // P
NT = T // P
HALF = 512
NH = T // HALF
CONV_TAPS = 3
HEADS = 8
DH = D // HEADS
RATES = (1, 4, 16)
STRIDES = (1, 4, 8)
REACH = 64
Q_RANK = 256
KV_RANK = 256
IDX_HEADS = 8
IDX_DIM = 64
TOPK = 256
NUM_BUCKETS = 32
MAX_DISTANCE = 128
D_FF = 2816
KF = D_FF // P
EPS = 1e-6
MASKED = -1e30
TAKEN = -3e38
LOWEST = -3.4e38

PACK_A = [("c", KD), ("c_2", KD), ("norm_g", 2 * KD), ("final_g", KD), ("conv_k", CONV_TAPS * KD),
          ("b_mod", 2 * 3 * KD), ("g_mix_2", KD), ("g_ffn_2", KD)]
PACK_B = [("ada_b_2", 6 * KD), ("f_conv_w_2", CONV_TAPS * KF), ("g_final_2", KD),
          ("a_g_cq_2", Q_RANK // P), ("a_g_ckv_2", KV_RANK // P)]
PACK_C = [("f_conv_b_2", KF)]


def shape_constants():
    f = np.float32
    half = DH // 2
    inv = (f(10000.0) ** (-np.arange(0, DH, 2, dtype=f) / f(DH))).astype(f)
    angle = (np.arange(T, dtype=f)[:, None] * inv[None, :]).astype(f)
    cos, sin = np.cos(angle).astype(f).T, np.sin(angle).astype(f).T
    p = np.arange(P)[:, None]
    j = np.arange(3 * P)[None, :]
    band = np.where(np.abs(j - P - p) <= REACH, 0.0, MASKED).astype(f)
    k = np.arange(P)[None, :]
    pair = np.where(p % 2 == k % 2, 0.0, MASKED).astype(f)
    causal = np.where(k <= p, 0.0, MASKED).astype(f)
    dist = np.arange(-127, 256)
    n = np.maximum(dist, 0)
    exact = NUM_BUCKETS // 2
    ratio = np.log(np.maximum(n, 1).astype(f) / f(exact)) / f(np.log(MAX_DISTANCE / exact))
    large = exact + (ratio * f(NUM_BUCKETS - exact)).astype(np.int32)
    bucket = np.where(n < exact, n, np.minimum(large, NUM_BUCKETS - 1))
    assert (bucket[dist >= P] == NUM_BUCKETS - 1).all()
    hot = np.zeros((NUM_BUCKETS, dist.size + 1), f)
    hot[bucket, np.arange(dist.size)] = 1.0
    hot[NUM_BUCKETS - 1, :dist.size] -= 1.0
    hot[:, :dist.size][:, dist < 0] = 0.0
    return {
        "rope_cos": np.ascontiguousarray(np.concatenate([cos, cos], 0)),
        "rope_sin": np.ascontiguousarray(np.concatenate([-sin, sin], 0)),
        "band_mask": band, "pair_mask": pair, "causal_mask": causal,
        "bucket_hot": hot, "identity": np.eye(P, dtype=f),
    }


class Line:

    def __init__(self, name, sem):
        self.name, self.sem, self.count, self.steps, self.seen = name, sem, 0, [], {}

    def wait(self, *tokens):
        for token in tokens:
            if isinstance(token, list):
                self.wait(*token)
            elif token is not None:
                sem, value = token
                if self.seen.get(sem, 0) < value:
                    self.seen[sem] = value
                    self.steps.append(lambda e, s=sem, v=value: e.wait_ge(s, v))

    def do(self, emit, *after, mark=True):
        self.wait(*after)
        if not mark:
            self.steps.append(emit)
            return None
        self.count += 1
        self.steps.append(lambda e: emit(e).then_inc(self.sem, 1))
        return (self.sem, self.count)

    @property
    def last(self):
        return (self.sem, self.count) if self.count else None


class DmaSlot:

    def __init__(self, sem):
        self.sem, self.count = sem, 0


def build(nc, ins, out):
    ctx = ExitStack()
    with ctx:
        named = {}

        def sb(name, shape, dt=F32, where=ctx):
            named[name] = named.get(name, 0) + 1
            return where.enter_context(nc.sbuf_tensor(f"{name}_{named[name]}", shape, dt))

        def ps(name, shape, where):
            return where.enter_context(nc.psum_tensor(name, shape, F32))

        def sem(name):
            return ctx.enter_context(nc.semaphore(name))

        PE, V, S, G = (Line(n, sem("done_" + n)) for n in ("pe", "dve", "act", "pool"))
        SP = Line("sp", sem("done_sp"))
        LINES = (PE, V, S, G, SP)
        slots = {}

        def dma(name, dst, src, *after):
            if name not in slots:
                slots[name] = DmaSlot(sem("dma_" + name))
            slot = slots[name]
            SP.wait(*after)
            slot.count += 16
            SP.steps.append(lambda e: e.dma_start(dst, src).then_inc(slot.sem, 16))
            return (slot.sem, slot.count)

        def barrier():
            last = [line.last for line in LINES] + [(s.sem, s.count) for s in slots.values()]
            for line in LINES:
                line.wait(*last)

        x = sb("x", [P, KD, T])
        ident = sb("ident", [P, P])
        ones = sb("ones", [P, P])
        eps = sb("eps", [P, 1])
        par_a = sb("par_a", [P, P])
        par_b = sb("par_b", [P, P])
        par_c = sb("par_c", [P, sum(n for _, n in PACK_C)])
        silu_c = sb("silu_c", [P, 2 * KD])
        mod = sb("mod", [P, 12 * KD])
        gain = sb("gain", [P, 4 * KD])
        x_park = nc.dram_tensor("x_park", (P, KD, T), F32).ap()

        col, at = {}, 0
        for tile, pack in ((par_a, PACK_A), (par_b, PACK_B), (par_c, PACK_C)):
            at = 0
            for name, rows in pack:
                col[name] = (tile, at, rows)
                at += rows

        def par(name, j):
            tile, a, _ = col[name]
            return tile[:, a + j:a + j + 1]

        class Weights:

            def __init__(self, where, items, raw=3, split=2, kt=KD):
                self.items, self.raw, self.split = items, raw, split
                self.room = sb("w_raw", [P, raw, kt, P], F32, where)
                self.hi = sb("w_hi", [P, split, kt, P], F32R, where)
                self.lo = sb("w_lo", [P, split, kt, P], F32R, where)
                self.raw_free, self.split_free = {}, [None] * split
                self.loaded, self.ready, self.taken, self.splits = {}, {}, 0, 0
                self.n_loaded = self.n_split = 0

            def load_next(self):
                n = self.n_loaded
                if n >= len(self.items) or (n >= self.raw and n - self.raw not in self.raw_free):
                    return False
                self.n_loaded += 1
                r = n % self.raw
                parts, kt, _ = self.items[n]
                for a, b, src in parts:
                    self.loaded[n] = dma(f"w{r}", self.room[:, r, 0:kt, a:b], src, self.raw_free.get(n - self.raw))
                return True

            def split_next(self):
                n = self.n_split
                if n >= len(self.items):
                    return
                while n >= self.n_loaded:
                    assert self.load_next()
                self.n_split += 1
                r = n % self.raw
                _, kt, split = self.items[n]
                if not split:
                    self.ready[n] = (None, r, self.loaded[n])
                    return
                s = self.splits % self.split
                self.splits += 1
                raw, hi, lo = self.room[:, r, 0:kt, :], self.hi[:, s, 0:kt, :], self.lo[:, s, 0:kt, :]
                t_hi = S.do(lambda e: e.activation(hi, raw, ACT.Copy), self.loaded[n], self.split_free[s])
                t_lo = G.do(lambda e: e.tensor_tensor(lo, raw, hi.bitcast(F32), ALU.subtract), t_hi)
                self.raw_free[n] = t_lo
                self.ready[n] = (s, r, t_lo)

            def take(self):
                n = self.taken
                self.taken += 1
                while self.n_split <= min(n + 1, len(self.items) - 1):
                    self.split_next()
                while self.load_next():
                    pass
                return (n,) + self.ready[n]

        class Banks:

            def __init__(self, tiles):
                self.tiles, self.free, self.n = tiles, [None] * len(tiles), 0

            def take(self):
                b = self.n % len(self.tiles)
                self.n += 1
                PE.wait(self.free[b])
                return b, self.tiles[b]

        tasks = []

        def run_task():
            if tasks:
                tasks.pop(0)[1]()

        def queue_task(room, task):
            tasks.append((room, task))

        def drain(room):
            while any(name == room for name, _ in tasks):
                run_task()

        def product(w, banks, a_hi, a_lo, a_ready, evac, slot=True):
            n, s, _, t_w = w.take()
            kt = w.items[n][1]
            for h in range(NH):
                b, bank = banks.take()
                PE.wait(t_w)
                cols = slice(h * HALF, (h + 1) * HALF)
                for k in range(kt):
                    PE.wait(a_ready[k])
                    for i, (wp, ap) in enumerate(((w.hi, a_hi), (w.hi, a_lo), (w.lo, a_hi))):
                        first, end = k == 0 and i == 0, k == kt - 1 and i == 2
                        t = PE.do(lambda e, o=bank[:, :], l=wp[:, s, k, :], r=ap[:, k, cols], f=first, z=end:
                                  e.matmul(o, l, r, start=f, stop=z), mark=end)
                banks.free[b] = evac(h, cols, bank, t)
                if slot:
                    run_task()
            w.split_free[s] = t

        def modulation(w, banks, c_col, mod_col, bias_ap):
            n, _, r, t_w = w.take()
            b, bank = banks.take()
            PE.wait(t_w)
            for k in range(KD):
                t = PE.do(lambda e, k=k: e.matmul(bank[:, 0:1], w.room[:, r, k, :], silu_c[:, c_col + k:c_col + k + 1],
                                                  start=(k == 0), stop=(k == KD - 1)), mark=(k == KD - 1))
            w.raw_free[n] = t
            t_m = V.do(lambda e: e.tensor_tensor(mod[:, mod_col:mod_col + 1], bank[:, 0:1], bias_ap, ALU.add), t)
            banks.free[b] = t_m
            return t_m

        def gains(first, scale_col, g_name, g_first, *after):
            return V.do(lambda e: e.scalar_tensor_tensor(
                out=gain[:, first:first + KD], in0=mod[:, scale_col:scale_col + KD], scalar=1.0,
                in1=col[g_name][0][:, col[g_name][1] + g_first:col[g_name][1] + g_first + KD],
                op0=ALU.add, op1=ALU.mult), *after)

        def inverse_rms(src, ready, n_features, banks, sq, acc, r_out):
            t_sq, t_acc = [None, None], None
            for k, tile in enumerate(src):
                dst = acc if k == 0 else sq[:, k % 2, :]
                t = S.do(lambda e, d=dst, i=tile: e.activation(d[:, :] if d is acc else d, i, ACT.Square),
                         ready[k], t_sq[k % 2])
                if k:
                    t = t_sq[k % 2] = V.do(lambda e, k=k: e.tensor_tensor(acc[:, :], acc[:, :], sq[:, k % 2, :], ALU.add),
                                           t, t_acc)
                t_acc = t
            for h in range(NH):
                b, bank = banks.take()
                cols = slice(h * HALF, (h + 1) * HALF)
                t = PE.do(lambda e, o=bank[:, :], a=acc[:, cols]: e.matmul(o, ones[:, :], a, start=True, stop=True), t_acc)
                t = S.do(lambda e, o=r_out[:, cols], i=bank[:, :]: e.activation(
                    o, i, ACT.Sqrt, bias=eps[:, 0:1], scale=1.0 / n_features), t)
                banks.free[b] = t
                t = V.do(lambda e, o=r_out[:, cols]: e.reciprocal(o, o), t)
            return t

        def split_into(hi, lo, src, *after):
            t = S.do(lambda e: e.activation(hi, src, ACT.Copy), *after)
            return G.do(lambda e: e.tensor_tensor(lo, src, hi.bitcast(F32), ALU.subtract), t, *after)

        def modulated_norm(where, banks, x_ready, gain_col, shift_col, h_hi, h_lo, *after):
            sq = sb("norm_sq", [P, 2, T], F32, where)
            acc = sb("norm_acc", [P, T], F32, where)
            r = sb("norm_r", [P, T], F32, where)
            t_r = inverse_rms([x[:, k, :] for k in range(KD)], x_ready, D, banks, sq, acc, r)
            ready, used = [], [None, None]
            for k in range(KD):
                xn = sq[:, k % 2, :]
                shift = mod[:, shift_col + k:shift_col + k + 1]
                t = V.do(lambda e, k=k, xn=xn: e.scalar_tensor_tensor(
                    out=xn, in0=x[:, k, :], scalar=gain[:, gain_col + k:gain_col + k + 1], in1=r[:, :],
                    op0=ALU.mult, op1=ALU.mult), t_r, used[k % 2], *after)
                t_hi = S.do(lambda e, k=k, xn=xn, shift=shift: e.activation(h_hi[:, k, :], xn, ACT.Identity, bias=shift), t)
                t = used[k % 2] = V.do(lambda e, k=k, xn=xn, shift=shift: e.scalar_tensor_tensor(
                    out=h_lo[:, k, :], in0=xn, scalar=shift, in1=h_hi[:, k, :].bitcast(F32),
                    op0=ALU.add, op1=ALU.subtract), t_hi)
                ready.append(t)
            return ready

        def out_projection(w, banks, y_hi, y_lo, y_ready, gate_col, x_ready):
            for d in range(KD):
                def evac(h, cols, bank, t, d=d):
                    x_ready[d] = [V.do(lambda e: e.scalar_tensor_tensor(
                        out=x[:, d, cols], in0=bank[:, :], scalar=mod[:, gate_col + d:gate_col + d + 1],
                        in1=x[:, d, cols], op0=ALU.mult, op1=ALU.add), t, x_ready[d])]
                    return x_ready[d]
                product(w, banks, y_hi, y_lo, y_ready, evac)

        def block_of(w2d, n):
            return w2d.rearrange("(k p) n -> p k n", p=P)[:, :, n * P:(n + 1) * P]

        def item(w2d, n, split=True):
            src = block_of(w2d, n)
            return ([(0, P, src)], src.shape[1], split)

        w_mod, ada_w = ins["w_mod"], ins["ada_w_2"][0]

        x_ready = [[] for _ in range(KD)]

        def stage_setup():
            with ExitStack() as st:
                banks = Banks([ps(f"s0_bank{i}", [P, HALF], st) for i in range(8)])
                rows = sb("par_rows", [P, 3, P], F32, st)
                x_rows = sb("x_rows", [P, NT, D], F32, st)
                t_id = dma("ident", ident[:, :], ins["identity"])
                t_par = []
                for p_i, pack in enumerate((PACK_A, PACK_B, PACK_C)):
                    a = 0
                    for name, n in pack:
                        flat = ins[name]
                        names = " ".join("abcd"[:len(flat.shape)])
                        flat = flat.rearrange(f"{names} -> ({names})") if len(flat.shape) > 1 else flat
                        t_par.append(dma("par", rows[a:a + n, p_i, :], flat.rearrange("(j p) -> j p", p=P)))
                        a += n
                t_x = [dma(f"x{i}", x_rows[:, i, :], ins["x"][0, i * P:(i + 1) * P, :]) for i in range(NT)]
                t_ones = V.do(lambda e: e.memset(ones[:, :], 1.0))
                t_ones = V.do(lambda e: e.memset(eps[:, :], EPS))
                for p_i, (tile, pack) in enumerate(((par_a, PACK_A), (par_b, PACK_B), (par_c, PACK_C))):
                    n = sum(r for _, r in pack)
                    b, bank = banks.take()
                    t = PE.do(lambda e, n=n, p_i=p_i, bank=bank: e.transpose(bank[:, 0:n], rows[0:n, p_i, :], ident[0:n, 0:n]),
                              t_id, t_par[-1])
                    t_vec = banks.free[b] = V.do(lambda e, n=n, tile=tile, bank=bank: e.tensor_copy(tile[:, 0:n], bank[:, 0:n]), t)
                t_silu = S.do(lambda e: e.activation(silu_c[:, :], par_a[:, 0:2 * KD], ACT.Silu), t_vec)
                for i in range(NT):
                    for q in range(2):
                        b, bank = banks.take()
                        PE.wait(t_x[i])
                        for k in range(4):
                            t = PE.do(lambda e, i=i, k=k, q=q, bank=bank: e.transpose(
                                bank[:, k * P:(k + 1) * P], x_rows[:, i, (4 * q + k) * P:(4 * q + k + 1) * P], ident[:, :]),
                                mark=(k == 3))
                        dst = x[:, 4 * q:4 * q + 4, i * P:(i + 1) * P]
                        src = bank[:, :].rearrange("p (k n) -> p k n", k=4)
                        if q:
                            t = S.do(lambda e, dst=dst, src=src: e.activation(dst, src, ACT.Copy), t)
                        else:
                            t = V.do(lambda e, dst=dst, src=src: e.tensor_copy(dst, src), t)
                        banks.free[b] = t
                        for k in range(4):
                            x_ready[4 * q + k].append(t)
                barrier()

        def stage_conv():
            GROUP = 4
            with ExitStack() as st:
                w_in, w_out = ins["conv_w_in"][0], ins["conv_w_out"][0]
                items = [item(w_mod[0], j, False) for j in range(3 * KD)]
                for g in range(KD // GROUP):
                    for e_ in range(GROUP * g, GROUP * (g + 1)):
                        items += [item(w_in, KD * part + e_) for part in (1, 2, 3, 0)]
                        items += [item(w_mod[1], 3 * e_ + j, False) for j in range(3)]
                    rows_g = w_out[GROUP * g * P:GROUP * (g + 1) * P, :]
                    items += [item(rows_g, d) for d in range(KD)]
                w = Weights(st, items, raw=4)
                banks = Banks([ps(f"s1_bank{i}", [P, HALF], st) for i in range(8)])
                h_hi, h_lo = sb("h_hi", [P, KD, T], F32R, st), sb("h_lo", [P, KD, T], F32R, st)
                y_hi, y_lo = sb("y_hi", [P, GROUP, T], F32R, st), sb("y_lo", [P, GROUP, T], F32R, st)
                for j in range(3 * KD):
                    t_mod = modulation(w, banks, 0, j, par("b_mod", j))
                t_gain = gains(0, KD, "norm_g", 0, t_mod)
                with ExitStack() as st2:
                    h_ready = modulated_norm(st2, banks, x_ready, 0, 0, h_hi, h_lo, t_gain)
                    for line in LINES:
                        line.wait(h_ready[-1])
                c_sb = sb("c_sb", [P, T], F32, st)
                t_pad = sb("t_pad", [P, T + 2], F32, st)
                cv = sb("cv", [P, T], F32, st)
                zs = sb("zs", [P, T], F32, st)
                yv = sb("yv", [P, T], F32, st)
                t_edge = V.do(lambda e: e.memset(t_pad[:, 0:1], 0.0))
                t_edge = V.do(lambda e: e.memset(t_pad[:, T + 1:T + 2], 0.0))
                y_free = t_cfree = t_tfree = t_cvfree = t_yfree = None
                for g in range(KD // GROUP):
                    y_ready = []
                    for e_ in range(GROUP * g, GROUP * (g + 1)):
                        tk = [None] * NH
                        tc = [None] * NH

                        def evac_c(h, cols, bank, t):
                            tc[h] = S.do(lambda e: e.activation(c_sb[:, cols], bank[:, :], ACT.Copy), t, t_cfree)
                            return tc[h]
                        product(w, banks, h_hi, h_lo, h_ready, evac_c)

                        def evac_x(h, cols, bank, t):
                            a = 1 + h * HALF
                            tk[h] = V.do(lambda e: e.tensor_tensor(t_pad[:, a:a + HALF], bank[:, :], c_sb[:, cols], ALU.mult),
                                         t, tc[h], t_tfree)
                            return tk[h]
                        product(w, banks, h_hi, h_lo, h_ready, evac_x)
                        t_cfree = tk[1]
                        t0 = V.do(lambda e, e_=e_: e.tensor_scalar(cv[:, :], t_pad[:, 0:T], par("conv_k", e_), None, ALU.mult),
                                  tk, t_edge, t_cvfree)
                        for tap in (1, 2):
                            t0 = V.do(lambda e, e_=e_, tap=tap: e.scalar_tensor_tensor(
                                out=cv[:, :], in0=t_pad[:, tap:tap + T], scalar=par("conv_k", tap * KD + e_),
                                in1=cv[:, :], op0=ALU.mult, op1=ALU.add), t0)
                        t_tfree = t_cv = t0
                        tz = [None] * NH

                        def evac_z(h, cols, bank, t):
                            t1 = S.do(lambda e: e.activation(zs[:, cols], bank[:, :], ACT.Silu), t, t_cvfree)
                            tz[h] = V.do(lambda e: e.tensor_tensor(cv[:, cols], cv[:, cols], zs[:, cols], ALU.mult), t1, t_cv)
                            return t1
                        product(w, banks, h_hi, h_lo, h_ready, evac_z)
                        ty = [None] * NH

                        def evac_b(h, cols, bank, t):
                            ty[h] = V.do(lambda e: e.tensor_tensor(yv[:, cols], bank[:, :], cv[:, cols], ALU.mult),
                                         t, tz[h], t_yfree)
                            return ty[h]
                        product(w, banks, h_hi, h_lo, h_ready, evac_b)
                        t_cvfree = ty[1]
                        i = e_ - GROUP * g
                        t_yfree = split_into(y_hi[:, i, :], y_lo[:, i, :], yv[:, :], ty, y_free)
                        y_ready.append(t_yfree)
                        for j in range(3):
                            t_mod = modulation(w, banks, 0, 3 * KD + 3 * e_ + j, par("b_mod", 3 * KD + 3 * e_ + j))
                    out_projection(w, banks, y_hi, y_lo, y_ready, 2 * KD, x_ready)
                    y_free = PE.last
                barrier()

        def stage_dilated():
            SCALE = float(DH) ** -0.5
            G_RATES = len(RATES)
            with ExitStack() as st:
                w_in, w_out = ins["dil_w_in"][0], ins["dil_w_out"][0]
                items = []
                for hd in range(HEADS):
                    blocks = [2 * G_RATES * HEADS + hd, (2 * G_RATES + 1) * HEADS + hd]
                    for g in range(G_RATES):
                        blocks += [g * HEADS + hd, (G_RATES + g) * HEADS + hd]
                    items += [item(w_in, n) for n in blocks[0:2]]
                    for g in range(G_RATES):
                        items += [item(w_in, n) for n in blocks[2 + 2 * g:4 + 2 * g]]
                        items += [item(ada_w, 6 * hd + 2 * g + j, False) for j in range(2)]
                items += [item(w_out, d) for d in range(KD)]
                w = Weights(st, items)
                banks = Banks([ps(f"s2_bank{i}", [P, HALF], st) for i in range(3)])
                s_banks = Banks([ps(f"s2_score{i}", [P, 2, 256], st) for i in range(2)])
                t_banks = Banks([ps(f"s2_turn{i}", [P, 4, P], st) for i in range(2)])
                o_banks = Banks([ps("s2_o", [P, 4, P], st)])
                h_hi, h_lo = sb("h_hi", [P, KD, T], F32R, st), sb("h_lo", [P, KD, T], F32R, st)
                t_gain = gains(KD, 4 * KD, "norm_g", KD)
                with ExitStack() as st2:
                    h_ready = modulated_norm(st2, banks, x_ready, KD, 3 * KD, h_hi, h_lo, t_gain)
                    for line in LINES:
                        line.wait(h_ready[-1])
                t_park = dma("park", x_park, x[:, :, :], x_ready)
                cos, sin = sb("cos", [P, T], F32, st), sb("sin", [P, T], F32, st)
                band, pair_m = sb("band", [P, 3 * P], F32, st), sb("pair_m", [P, P], F32, st)
                dma("tables", cos[:, :], ins["rope_cos"])
                dma("tables", sin[:, :], ins["rope_sin"])
                dma("tables", band[:, :], ins["band_mask"])
                t_tab = dma("tables", pair_m[:, :], ins["pair_mask"])
                qk = sb("qk", [P, 2, 2, T], F32, st)
                v_t = sb("v_t", [P, T], F32, st)
                v_tok = [sb(f"v_tok{g}", [P, NT + (g == 0), P], F32, st) for g in range(G_RATES)]
                o_g = [sb(f"o_g{g}", [P, T], F32, st) for g in range(G_RATES)]
                l_g = [sb(f"l_g{g}", [P, T], F32, st) for g in range(G_RATES)]
                rot = sb("rot", [P, HALF], F32, st)
                swp = sb("swp", [P, HALF], F32, st)
                prob = sb("prob", [P, 2, 2, 256], F32, st)
                prob_t = sb("prob_t", [P, 2, 4, P], F32, st)
                diag = sb("diag", [P, 4, P], F32, st)
                mx = diag[:, :, :].rearrange("p a b -> p (a b)")
                stat = sb("stat", [P, 2, 3, G_RATES * NT], F32, st)
                used = {}
                y_done = [None] * HEADS

                def natural(ap, r):
                    return ap.rearrange("p (i c) -> p i c", c=r)

                def rope_evac(dst, g, ready):
                    r = STRIDES[g]

                    def evac(h, cols, bank, t):
                        t1 = V.do(lambda e: e.tensor_tensor(rot[:, :], bank[:, :], cos[:, cols], ALU.mult), t, t_tab, used.get("rot"))
                        S.do(lambda e: e.activation(swp[0:DH // 2, :], bank[DH // 2:DH, :], ACT.Copy), t1, used.get("swp"))
                        t2 = S.do(lambda e: e.activation(swp[DH // 2:DH, :], bank[0:DH // 2, :], ACT.Copy))
                        t3 = G.do(lambda e: e.tensor_tensor(swp[:, :], swp[:, :], sin[:, cols], ALU.mult), t2)
                        per = HALF // r
                        to = dst.rearrange("p (c i) -> p i c", c=r)[:, h * per:(h + 1) * per, :]
                        t4 = V.do(lambda e: e.tensor_tensor(to, natural(rot[:, :], r), natural(swp[:, :], r), ALU.add), t3)
                        used["rot"] = used["swp"] = t4
                        ready.append(t4)
                        return t2
                    return evac

                def tile_plan(g, t):
                    if g == 0:
                        lo, hi = max(0, P * t - REACH), min(T, P * t + P + REACH)
                        off = lo - (P * t - REACH)
                        chunks = [(max(off, 0), P - off, t), (P, min(P, hi - P * t - REACH), t + 1)]
                        return lo, hi - lo, off, band[:, REACH + off:REACH + off + hi - lo], chunks
                    if g == 1:
                        c, u = divmod(t, 2)
                        return 256 * c, 256, 0, band[:, P * (1 - u):P * (1 - u) + 256], [(0, P, 2 * c), (P, P, 2 * c + 1)]
                    return P * t, P, 0, pair_m[:, :], [(0, P, t)]

                def turn_values(hd, t_v):
                    plans = [[v_t[:, max(0, P * j - REACH):min(T, P * j + REACH)] for j in range(NT + 1)]]
                    s4 = v_t[:, :].rearrange("p (i c) -> p c i", c=STRIDES[1])
                    plans.append([s4[:, j // 2, P * (j % 2):P * (j % 2) + P] for j in range(NT)])
                    s8 = v_t[:, :].rearrange("p (i c) -> p c i", c=STRIDES[2])
                    plans.append([s8[:, j, :] for j in range(NT)])

                    def turn(g, js):
                        b, bank = t_banks.take()
                        PE.wait(t_v)
                        t = None
                        for n, j in enumerate(js):
                            src = plans[g][j]
                            rows = src.free_size()
                            t = PE.do(lambda e, o=bank[0:rows, n, :], i=src: e.transpose(o, i, ident[:, :]), mark=True)
                        runs = []
                        for n, j in enumerate(js):
                            rows = plans[g][j].free_size()
                            if runs and runs[-1][2] == rows:
                                runs[-1][1] = n + 1
                            else:
                                runs.append([n, n + 1, rows])
                        for a, z, rows in runs:
                            te = S.do(lambda e, o=v_tok[g][0:rows, js[a]:js[a] + z - a, :], i=bank[0:rows, a:z, :]:
                                      e.activation(o, i, ACT.Copy), t, used.get(("v_tok", g)))
                        t_banks.free[b] = te
                        v_ready[g] = te
                        used["v_t"] = t

                    for g in range(G_RATES):
                        n = len(plans[g])
                        todo = [list(range(a, min(a + 4, n))) for a in range(0, n, 4)]
                        for i in range(0, len(todo), 2):
                            queue_task("v_t", lambda g=g, part=todo[i:i + 2]: [turn(g, js) for js in part])

                v_ready = [None] * G_RATES

                def attend(hd, g, q, k, qk_ready, qk_name):
                    par_ = hd % 2
                    keep = {}

                    def scores(p):
                        b, bank = s_banks.take()
                        PE.wait(qk_ready)
                        i = p % 2
                        room = prob[:, i, :, :]
                        ts = []
                        for u in range(2):
                            t = 2 * p + u
                            lo, n, off, mask, _ = tile_plan(g, t)
                            tt = PE.do(lambda e, o=bank[:, u, off:off + n], l=q[:, P * t:P * t + P], r=k[:, lo:lo + n]:
                                       e.matmul(o, l, r, start=True, stop=True))
                        for u in range(2):
                            t = 2 * p + u
                            lo, n, off, mask, _ = tile_plan(g, t)
                            c = g * NT + t
                            ts.append(V.do(lambda e, o=room[:, u, off:off + n], a=bank[:, u, off:off + n], m=mask, c=c:
                                           e.tensor_tensor_reduce(o, a, m, 1.0, LOWEST, ALU.add, ALU.max, stat[:, par_, 0, c:c + 1]),
                                           tt, used.get(("prob", i)), used.get(("stat", par_))))
                        used[qk_name] = tt
                        s_banks.free[b] = ts[-1]
                        c = g * NT + 2 * p
                        t1 = V.do(lambda e: e.tensor_scalar(stat[:, par_, 1, c:c + 2], stat[:, par_, 0, c:c + 2], -SCALE, None, ALU.mult), ts)
                        te = []
                        for u in range(2):
                            _, n, off, _, _ = tile_plan(g, 2 * p + u)
                            te.append(S.do(lambda e, a=room[:, u, off:off + n], c=c + u: e.activation(
                                a, a, ACT.Exp, bias=stat[:, par_, 1, c:c + 1], scale=SCALE, accum_out=stat[:, par_, 2, c:c + 1]), t1))
                        t2 = V.do(lambda e: e.reciprocal(stat[:, par_, 1, c:c + 2], stat[:, par_, 2, c:c + 2]), te)
                        for u in range(2):
                            _, n, off, _, _ = tile_plan(g, 2 * p + u)
                            t3 = V.do(lambda e, a=room[:, u, off:off + n], c=c + u: e.tensor_scalar(
                                a, a, stat[:, par_, 1, c:c + 1], None, ALU.mult), t2)
                        keep[p] = [t3, None]

                    def turn(p):
                        b, bank = t_banks.take()
                        i = p % 2
                        PE.wait(keep[p][0])
                        slots_ = []
                        n_ = 0
                        for u in range(2):
                            for (a, n, ch) in tile_plan(g, 2 * p + u)[4]:
                                tt = PE.do(lambda e, o=bank[0:n, n_, :], s=prob[:, i, u, a:a + n]: e.transpose(o, s, ident[:, :]))
                                slots_.append((u, n_, n, ch))
                                n_ += 1
                        used[("prob", i)] = tt
                        runs = []
                        for (_, s_, n, _) in slots_:
                            if runs and runs[-1][2] == n:
                                runs[-1][1] = s_ + 1
                            else:
                                runs.append([s_, s_ + 1, n])
                        for a, z, n in runs:
                            te = S.do(lambda e, o=prob_t[0:n, i, a:z, :], s=bank[0:n, a:z, :]: e.activation(o, s, ACT.Copy),
                                      tt, used.get(("prob_t", i)))
                        t_banks.free[b] = te
                        keep[p] = [te, slots_]

                    def values(p):
                        i = p % 2
                        if i == 0:
                            keep["o"] = o_banks.take()
                        b, bank = keep["o"]
                        te, slots_ = keep[p]
                        PE.wait(te, v_ready[g])
                        for n_, (u, s_, n, ch) in enumerate(slots_):
                            first = n_ == 0 or slots_[n_ - 1][0] != u
                            last = n_ == len(slots_) - 1 or slots_[n_ + 1][0] != u
                            tt = PE.do(lambda e, o=bank[:, 2 * i + u, :], l=v_tok[g][0:n, ch, :], r=prob_t[0:n, i, s_, :], f=first, z=last:
                                       e.matmul(o, l, r, start=f, stop=z))
                        used[("prob_t", i)] = used[("v_tok", g)] = tt
                        if i == 1:
                            r = STRIDES[g]
                            half = p // 2
                            src = bank[:, :, :].rearrange("p a b -> p (a b)")
                            if r == 1:
                                src, to = src, o_g[g][:, half * HALF:(half + 1) * HALF]
                            else:
                                src = src.rearrange("p (c i) -> p c i", i=T // r)
                                to = o_g[g][:, :].rearrange("p (i c) -> p c i", c=r)[:, half * r // 2:(half + 1) * r // 2, :]
                            t = S.do(lambda e: e.activation(to, src, ACT.Copy), tt, used.get(("o_g", g)))
                            o_banks.free[b] = t
                            o_ready[g] = t

                    queue_task(qk_name, lambda: (scores(0), scores(1)))
                    queue_task(qk_name, lambda: (turn(0), scores(2), turn(1), scores(3)))
                    queue_task(qk_name, lambda: (values(0), values(1), turn(2), turn(3)))
                    queue_task(qk_name, lambda: (values(2), values(3)))

                o_ready = [None] * G_RATES

                def combine(hd):
                    par_ = hd % 2
                    l_ready = [[None] * NH for _ in range(G_RATES)]

                    def spread(g, half):
                        c = g * NT + 4 * half
                        lse = stat[:, par_, 1, c:c + 4].unsqueeze(2).to_broadcast([P, 4, P])
                        eye = ident[:, :].unsqueeze(1).to_broadcast([P, 4, P])
                        td = V.do(lambda e: e.tensor_tensor(diag[:, :, :], eye, lse, ALU.mult), t_lse[0], used.get("diag"), used.get("mx"))
                        used[("stat", par_)] = td
                        b, bank = t_banks.take()
                        flat = bank[:, :, :].rearrange("p a b -> p (a b)")
                        tt = PE.do(lambda e: e.matmul(flat, ones[:, :], diag[:, :, :].rearrange("p a b -> p (a b)"),
                                                      start=True, stop=True), td)
                        used["diag"] = tt
                        r = STRIDES[g]
                        if r == 1:
                            src, to = flat, l_g[g][:, half * HALF:(half + 1) * HALF]
                        else:
                            src = flat.rearrange("p (c i) -> p c i", i=T // r)
                            to = l_g[g][:, :].rearrange("p (i c) -> p c i", c=r)[:, half * r // 2:(half + 1) * r // 2, :]
                        t = S.do(lambda e: e.activation(to, src, ACT.Copy), tt, used.get(("l_g", g)))
                        t_banks.free[b] = t
                        l_ready[g][half] = t

                    t_lse = [None]

                    def start():
                        t = S.do(lambda e: e.activation(stat[:, par_, 1, :], stat[:, par_, 2, :], ACT.Ln), used.get(("lse", par_)), o_ready)
                        t_lse[0] = V.do(lambda e: e.scalar_tensor_tensor(
                            out=stat[:, par_, 1, :], in0=stat[:, par_, 0, :], scalar=SCALE, in1=stat[:, par_, 1, :],
                            op0=ALU.mult, op1=ALU.add), t)
                        for g in range(G_RATES):
                            for half in range(NH):
                                spread(g, half)
                        used[("lse", par_)] = used["diag"]

                    def blend_half(cols):
                        L = [l[:, cols] for l in l_g]
                        O = [o[:, cols] for o in o_g]
                        y = x[:, hd, cols]
                        t = V.do(lambda e: e.tensor_tensor(mx, L[0], L[1], ALU.max), l_ready, used.get("mx"), used.get("diag"))
                        t = V.do(lambda e: e.tensor_tensor(mx, mx, L[2], ALU.max), t)
                        te = []
                        for g in range(G_RATES):
                            tg = G.do(lambda e, l=L[g]: e.tensor_tensor(l, l, mx, ALU.subtract), t)
                            te.append(S.do(lambda e, l=L[g]: e.activation(l, l, ACT.Exp), tg))
                        t = G.do(lambda e: e.tensor_tensor(mx, L[0], L[1], ALU.add), te)
                        t = G.do(lambda e: e.tensor_tensor(mx, mx, L[2], ALU.add), t)
                        tm = V.do(lambda e: e.reciprocal(mx, mx), t)
                        to = [V.do(lambda e, o=O[g], l=L[g]: e.tensor_tensor(o, o, l, ALU.mult), te[g], o_ready[g])
                              for g in range(G_RATES)]
                        t = V.do(lambda e: e.tensor_tensor(O[0], O[0], O[1], ALU.add), to)
                        t = V.do(lambda e: e.tensor_tensor(O[0], O[0], O[2], ALU.add), t)
                        t = V.do(lambda e: e.tensor_tensor(O[0], O[0], mx, ALU.mult), t, tm)
                        used["mx"] = V.do(lambda e: e.tensor_tensor(y, O[0], y, ALU.mult), t, z_ready[hd])

                    def blend():
                        for half in range(NH):
                            blend_half(slice(half * HALF, (half + 1) * HALF))
                        for g in range(G_RATES):
                            used[("l_g", g)] = used[("o_g", g)] = used["mx"]
                        y_done[hd] = used["mx"]

                    queue_task(None, start)
                    queue_task(None, blend)

                z_ready = [None] * HEADS
                for hd in range(HEADS):
                    tv = []
                    drain("v_t")

                    def evac_v(h, cols, bank, t):
                        tv.append(S.do(lambda e: e.activation(v_t[:, cols], bank[:, :], ACT.Copy), t, used.get("v_t")))
                        return tv[-1]
                    product(w, banks, h_hi, h_lo, h_ready, evac_v)
                    turn_values(hd, tv)

                    def evac_z(h, cols, bank, t, hd=hd):
                        z_ready[hd] = S.do(lambda e: e.activation(x[:, hd, cols], bank[:, :], ACT.Silu), t, t_park)
                        return z_ready[hd]
                    product(w, banks, h_hi, h_lo, h_ready, evac_z)
                    for g in range(G_RATES):
                        which = (hd * G_RATES + g) % 2
                        name = ("qk", which)
                        ready = []
                        drain(name)
                        for n in range(2):
                            dst = qk[:, which, n, :]
                            wait_for = name
                            ev = rope_evac(dst, g, ready)

                            def evac(h, cols, bank, t, ev=ev, wait_for=wait_for):
                                V.wait(used.get(wait_for))
                                return ev(h, cols, bank, t)
                            product(w, banks, h_hi, h_lo, h_ready, evac)
                        attend(hd, g, qk[:, which, 0, :], qk[:, which, 1, :], ready, name)
                        for j in (2 * g, 2 * g + 1):
                            modulation(w, banks, KD, 6 * KD + 6 * hd + j, par("ada_b_2", 6 * hd + j))
                            run_task()
                    combine(hd)
                y_ready = [None] * KD
                t_h_free = PE.last
                todo = list(range(KD))

                def split_y():
                    k = todo.pop(0)
                    y_ready[k] = split_into(h_hi[:, k, :], h_lo[:, k, :], x[:, k, :], y_done[k], t_h_free)
                    x_ready[k] = [dma(f"x{k}", x[:, k, :], x_park[:, k, :], y_ready[k], t_park)]
                while tasks:
                    run_task()
                    if len(todo) > 1 and y_done[todo[0]]:
                        split_y()
                while todo:
                    split_y()
                out_projection(w, banks, h_hi, h_lo, y_ready, 5 * KD, x_ready)
                barrier()
        def stage_between():
            with ExitStack() as st:
                banks = Banks([ps(f"s2n_bank{i}", [P, HALF], st) for i in range(4)])
                sq, acc, r = sb("norm_sq", [P, 2, T], F32, st), sb("norm_acc", [P, T], F32, st), sb("norm_r", [P, T], F32, st)
                t_r = inverse_rms([x[:, k, :] for k in range(KD)], x_ready, D, banks, sq, acc, r)
                for k in range(KD):
                    x_ready[k] = [V.do(lambda e, k=k: e.scalar_tensor_tensor(
                        out=x[:, k, :], in0=x[:, k, :], scalar=par("final_g", k), in1=r[:, :],
                        op0=ALU.mult, op1=ALU.mult), t_r, x_ready[k])]
                barrier()

        def stage_latent():
            KQ, KC = Q_RANK // P, KV_RANK // P
            w_in = ins["a_w_in_2"][0]
            i_kidx, i_widx = Q_RANK + KV_RANK, Q_RANK + KV_RANK + IDX_DIM
            with ExitStack() as st:
                ckv_t = sb("ckv_t", [P, KC, T], F32, st)
                ckv_tok = sb("ckv_tok", [P, NT, KV_RANK], F32, st)
                k_idx = sb("k_idx", [P, T], F32, st)
                w_idx = sb("w_idx", [P, NT, IDX_HEADS], F32, st)
                q_idx = sb("q_idx", [P, IDX_HEADS * IDX_DIM // P, T], F32, st)
                bias = sb("bias", [P, HEADS, 2 * P], F32, st)
                t_park = [None]
                with ExitStack() as sa:
                    items = [item(w_in, n) for n in range(KQ + KC)]
                    kcols = w_in.rearrange("(k p) n -> p k n", p=P)[:, :, i_kidx:i_widx]
                    items.append(([(0, IDX_DIM, kcols), (IDX_DIM, P, kcols)], KD, True))
                    w = Weights(sa, items)
                    banks = Banks([ps(f"s3_bank{i}", [P, HALF], sa) for i in range(8)])
                    h_hi, h_lo = sb("h_hi", [P, KD, T], F32R, sa), sb("h_lo", [P, KD, T], F32R, sa)
                    wi = sb("wi", [P, KD, IDX_HEADS], F32, sa)
                    wi_hi, wi_lo = sb("wi_hi", [P, KD, IDX_HEADS], F32R, sa), sb("wi_lo", [P, KD, IDX_HEADS], F32R, sa)
                    rel = sb("rel", [NUM_BUCKETS, IDX_HEADS], F32, sa)
                    hot = sb("hot", [NUM_BUCKETS, 3 * P], F32, sa)
                    t_rel = dma("rel", rel[:, :], ins["rel_bias_2"])
                    t_hot = dma("hot", hot[:, :], ins["bucket_hot"])
                    t_wi = dma("wi", wi[:, :, :], w_in.rearrange("(k p) n -> p k n", p=P)[:, :, i_widx:i_widx + IDX_HEADS])
                    t_gain = gains(2 * KD, 7 * KD, "g_mix_2", 0)
                    with ExitStack() as st2:
                        h_ready = modulated_norm(st2, banks, x_ready, 2 * KD, 6 * KD, h_hi, h_lo, t_gain)
                        for line in LINES:
                            line.wait(h_ready[-1])
                    t_park[0] = dma("park", x_park, x[:, :, :], x_ready)
                    t_wi = split_into(wi_hi[:, :, :], wi_lo[:, :, :], wi[:, :, :], t_wi)
                    PE.wait(t_rel, t_hot)
                    for part in range(4):
                        b, bank = banks.take()
                        for n in range(64):
                            a = 2 * P - 1 - (64 * part + n)
                            t = PE.do(lambda e, o=bank[:, 8 * n:8 * n + 8], l=hot[:, a:a + P]:
                                      e.matmul(o, l, rel[:, :], start=True, stop=True), mark=(n == 63))
                        banks.free[b] = V.do(lambda e, o=bias[:, :, 64 * part:64 * part + 64].rearrange("p h s -> p s h"),
                                             i=bank[:, :].rearrange("p (s h) -> p s h", h=HEADS): e.tensor_copy(o, i), t)
                    c_room = x[:, :, :]
                    c_ready = [[] for _ in range(KQ + KC)]
                    for n in range(KQ + KC):
                        def evac(h, cols, bank, t, n=n):
                            c_ready[n].append(S.do(lambda e: e.activation(c_room[:, n, cols], bank[:, :], ACT.Copy), t, t_park[0]))
                            return c_ready[n][-1]
                        product(w, banks, h_hi, h_lo, h_ready, evac)

                    def evac_k(h, cols, bank, t):
                        return S.do(lambda e: e.activation(k_idx[:, cols], bank[:, :], ACT.Copy), t)
                    product(w, banks, h_hi, h_lo, h_ready, evac_k)
                    b, bank = banks.take()
                    PE.wait(t_wi)
                    for i in range(NT):
                        for k in range(KD):
                            for n, (hp, wp) in enumerate(((h_hi, wi_hi), (h_hi, wi_lo), (h_lo, wi_hi))):
                                first, end = k == 0 and n == 0, k == KD - 1 and n == 2
                                t = PE.do(lambda e, o=bank[:, 8 * i:8 * i + 8], l=hp[:, k, i * P:(i + 1) * P], r=wp[:, k, :], f=first, z=end:
                                          e.matmul(o, l, r, start=f, stop=z), mark=end)
                    w_scale = float(IDX_HEADS) ** -0.5 * float(IDX_DIM) ** -0.5
                    banks.free[b] = V.do(lambda e, bank=bank: e.tensor_scalar(w_idx[:, :, :].rearrange("p a b -> p (a b)"), bank[:, 0:NT * IDX_HEADS],
                                                                   w_scale, None, ALU.mult), t)
                    sq, acc, r = sb("norm_sq", [P, 2, T], F32, sa), sb("norm_acc", [P, T], F32, sa), sb("norm_r", [P, T], F32, sa)
                    t_r = inverse_rms([c_room[:, k, :] for k in range(KQ)], c_ready[:KQ], Q_RANK, banks, sq, acc, r)
                    for k in range(KQ):
                        t_cq = V.do(lambda e, k=k: e.scalar_tensor_tensor(
                            out=c_room[:, k, :], in0=c_room[:, k, :], scalar=par("a_g_cq_2", k), in1=r[:, :],
                            op0=ALU.mult, op1=ALU.mult), t_r)
                    t_r = inverse_rms([c_room[:, KQ + k, :] for k in range(KC)], [c + [t_cq] for c in c_ready[KQ:]], KV_RANK, banks, sq, acc, r)
                    t_kv = []
                    for k in range(KC):
                        t_kv.append(V.do(lambda e, k=k: e.scalar_tensor_tensor(
                            out=ckv_t[:, k, :], in0=c_room[:, KQ + k, :], scalar=par("a_g_ckv_2", k), in1=r[:, :],
                            op0=ALU.mult, op1=ALU.mult), t_r))
                    for i in range(0, NT, 2):
                        b, bank = banks.take()
                        for u in range(2):
                            for k in range(KC):
                                c = (u * KC + k) * P
                                t = PE.do(lambda e, o=bank[:, c:c + P], s=ckv_t[:, k, (i + u) * P:(i + u + 1) * P]:
                                          e.transpose(o, s, ident[:, :]), t_kv[k])
                        banks.free[b] = S.do(lambda e, o=ckv_tok[:, i:i + 2, :].rearrange("p a b -> p (a b)"), s=bank[:, :]:
                                             e.activation(o, s, ACT.Copy), t)
                    barrier()

                q_lat = sb("q_lat", [P, HEADS, KC, T], F32, st)
                with ExitStack() as sq_:
                    w_uq, w_qi = ins["a_w_uq_2"][0], ins["a_w_qi_2"][0]
                    items = [item(w_uq, n) for n in range(HEADS)] + [item(w_qi, n) for n in range(IDX_HEADS * IDX_DIM // P)]
                    w = Weights(sq_, items, kt=KQ)
                    banks = Banks([ps(f"s3b_bank{i}", [P, HALF], sq_) for i in range(8)])
                    cq_hi, cq_lo = sb("cq_hi", [P, KQ, T], F32R, sq_), sb("cq_lo", [P, KQ, T], F32R, sq_)
                    w_uk = sb("w_uk", [P, HEADS, KV_RANK], F32, sq_)
                    qh = sb("qh", [P, 2, T], F32, sq_)
                    t_uk = dma("w_uk", w_uk[:, :, :], ins["a_w_uk_2"][0].rearrange("h d c -> d h c"))
                    cq_ready = [split_into(cq_hi[:, k, :], cq_lo[:, k, :], x[:, k, :]) for k in range(KQ)]
                    q_free = [None, None]
                    q_scale = float(DH) ** -0.5
                    for hd in range(HEADS):
                        tq = []

                        def evac_q(h, cols, bank, t, hd=hd):
                            tq.append(V.do(lambda e: e.tensor_copy(qh[:, hd % 2, cols], bank[:, :]), t, q_free[hd % 2]))
                            return tq[-1]
                        product(w, banks, cq_hi, cq_lo, cq_ready, evac_q)
                        for ch in range(KC):
                            for h in range(NH):
                                b, bank = banks.take()
                                cols = slice(h * HALF, (h + 1) * HALF)
                                PE.wait(t_uk)
                                t = PE.do(lambda e, o=bank[:, :], l=w_uk[:, hd, ch * P:(ch + 1) * P], s=qh[:, hd % 2, cols]:
                                          e.matmul(o, l, s, start=True, stop=True), tq[h])
                                q_free[hd % 2] = t
                                banks.free[b] = S.do(lambda e, o=q_lat[:, hd, ch, cols], s=bank[:, :]:
                                                     e.activation(o, s, ACT.Copy, scale=q_scale), t)
                    for n in range(IDX_HEADS * IDX_DIM // P):
                        def evac(h, cols, bank, t, n=n):
                            return V.do(lambda e: e.tensor_copy(q_idx[:, n, cols], bank[:, :]), t)
                        product(w, banks, cq_hi, cq_lo, cq_ready, evac)
                    barrier()

                with ExitStack() as sc_:
                    s_banks = Banks([ps(f"s3_s{i}", [P, 2, HALF], sc_) for i in range(2)])
                    t_banks = Banks([ps(f"s3_t{i}", [P, 4, P], sc_) for i in range(2)])
                    o_banks = Banks([ps("s3_o", [P, KC, P], sc_)])
                    y_banks = Banks([ps("s3_y", [P, P], sc_)])
                    w_uv = sb("w_uv", [P, HEADS, KC, P], F32, sc_)
                    causal = sb("causal", [P, P], F32, sc_)
                    work = sb("work", [P, T], F32, sc_)
                    relu = sb("relu", [P, 2, HALF], F32, sc_)
                    top8 = sb("top8", [P, 8], F32, sc_)
                    keep = sb("keep", [P, 2, T], F32, sc_)
                    near = sb("near", [P, 2, 2 * P], F32, sc_)
                    prob = sb("prob", [P, 2, T], F32, sc_)
                    prob_t = sb("prob_t", [P, 2, NT, P], F32, sc_)
                    o_lat = sb("o_lat", [P, 2, KC, P], F32, sc_)
                    stat = sb("stat", [P, 2, 5], F32, sc_)
                    t_uv = dma("w_uv", w_uv[:, :, :, :].rearrange("p h k v -> p (h k) v"),
                               ins["a_w_uv_2"][0].rearrange("h (k p) v -> p (h k) v", p=P))
                    t_causal = dma("causal", causal[:, :], ins["causal_mask"])
                    used = {}
                    keep_ready = [None, None]

                    def pick(i):
                        n = P * (i + 1)
                        steps = []
                        room = keep[:, i % 2, :]

                        def whole():
                            t = V.do(lambda e: e.tensor_copy(room[:, n - P:n], causal[:, :]), t_causal, used.get(("keep", i % 2)))
                            if n > P:
                                t = V.do(lambda e: e.memset(room[:, 0:n - P], 0.0))
                            keep_ready[i % 2] = t
                        if n <= TOPK:
                            return [whole]
                        last = [None]

                        def score(hh):
                            rows = slice(64 * (hh % 2), 64 * (hh % 2) + 64)
                            b, bank = s_banks.take()
                            flat = bank[:, :, :].rearrange("p a b -> p (a b)")
                            for a in range(0, n, HALF):
                                z = min(a + HALF, n)
                                t = PE.do(lambda e, o=flat[:, a:z], l=q_idx[rows, hh // 2, i * P:(i + 1) * P], r=k_idx[rows, a:z]:
                                          e.matmul(o, l, r, start=True, stop=True))
                            ends = []
                            for u, a in enumerate(range(0, n, HALF)):
                                z = min(a + HALF, n)
                                ta = S.do(lambda e, o=relu[:, u, 0:z - a], s=flat[:, a:z]: e.activation(o, s, ACT.Relu),
                                          t, used.get(("relu", u)))
                                wcol = w_idx[:, i, hh:hh + 1]
                                if hh == 0:
                                    tv = V.do(lambda e, o=work[:, a:z], s=relu[:, u, 0:z - a]: e.tensor_scalar(o, s, wcol, None, ALU.mult),
                                              ta, used.get("work"))
                                else:
                                    tv = V.do(lambda e, o=work[:, a:z], s=relu[:, u, 0:z - a]: e.scalar_tensor_tensor(
                                        out=o, in0=s, scalar=wcol, in1=o, op0=ALU.mult, op1=ALU.add), ta, last[0])
                                used[("relu", u)] = tv
                                ends.append(tv)
                            s_banks.free[b] = ta
                            last[0] = ends

                        def bound():
                            last[0] = V.do(lambda e: e.tensor_tensor(work[:, n - P:n], work[:, n - P:n], causal[:, :], ALU.add),
                                           last[0], t_causal)

                        def take8():
                            t = V.do(lambda e: e.max(top8[:, :], work[:, 0:n]), last[0])
                            last[0] = V.do(lambda e: e.match_replace(work[:, 0:n], top8[:, :], work[:, 0:n], TAKEN), t)

                        def finish():
                            t = V.do(lambda e: e.tensor_scalar(room[:, 0:n], work[:, 0:n], TAKEN / 2, MASKED, ALU.is_gt, ALU.mult),
                                     last[0], used.get(("keep", i % 2)))
                            used["work"] = keep_ready[i % 2] = t
                        steps = [lambda hh=hh: score(hh) for hh in range(IDX_HEADS)] + [bound]
                        steps += [take8] * (TOPK // 8) + [finish]
                        return steps

                    def weigh(i, hd):
                        n = P * (i + 1)
                        i2, h2 = i % 2, hd % 2
                        m = min(n, 2 * P)
                        t_near = G.do(lambda e: e.tensor_tensor(near[:, h2, 0:m], keep[:, i2, n - m:n], bias[:, hd, 2 * P - m:2 * P], ALU.add),
                                      keep_ready[i2], used.get(("near", h2)))
                        b, bank = s_banks.take()
                        flat = bank[:, :, :].rearrange("p a b -> p (a b)")
                        for a in range(0, n, HALF):
                            z = min(a + HALF, n)
                            for k in range(KC):
                                t = PE.do(lambda e, o=flat[:, a:z], l=q_lat[:, hd, k, i * P:(i + 1) * P], r=ckv_t[:, k, a:z], f=(k == 0), s=(k == KC - 1):
                                          e.matmul(o, l, r, start=f, stop=s), mark=(k == KC - 1))
                        row = prob[:, h2, :]
                        tm = [V.do(lambda e: e.tensor_tensor_reduce(row[:, n - m:n], flat[:, n - m:n], near[:, h2, 0:m], 1.0, LOWEST,
                                                                    ALU.add, ALU.max, stat[:, h2, 0:1]),
                                   t, t_near, used.get(("prob", h2)), used.get(("stat", h2)))]
                        used[("near", h2)] = tm[0]
                        if n > m:
                            tm.append(V.do(lambda e: e.tensor_tensor_reduce(row[:, 0:n - m], flat[:, 0:n - m], keep[:, i2, 0:n - m], 1.0, LOWEST,
                                                                            ALU.add, ALU.max, stat[:, h2, 1:2])))
                            t = V.do(lambda e: e.tensor_scalar(stat[:, h2, 2:3], stat[:, h2, 0:1], stat[:, h2, 1:2], -1.0, ALU.max, ALU.mult), tm)
                        else:
                            t = V.do(lambda e: e.tensor_scalar(stat[:, h2, 2:3], stat[:, h2, 0:1], -1.0, None, ALU.mult), tm)
                        used[("keep", i2)] = s_banks.free[b] = tm[-1]
                        t = S.do(lambda e: e.activation(row[:, 0:n], row[:, 0:n], ACT.Exp, bias=stat[:, h2, 2:3], accum_out=stat[:, h2, 3:4]), t)
                        t = V.do(lambda e: e.reciprocal(stat[:, h2, 4:5], stat[:, h2, 3:4]), t)
                        t = V.do(lambda e: e.tensor_scalar(row[:, 0:n], row[:, 0:n], stat[:, h2, 4:5], None, ALU.mult), t)
                        used[("stat", h2)] = t
                        return t

                    def gather(i, hd, t_prob):
                        h2 = hd % 2
                        ends = []
                        for a in range(0, i + 1, 4):
                            z = min(a + 4, i + 1)
                            b, bank = t_banks.take()
                            PE.wait(t_prob)
                            for j in range(a, z):
                                t = PE.do(lambda e, o=bank[:, j - a, :], s=prob[:, h2, j * P:(j + 1) * P]: e.transpose(o, s, ident[:, :]),
                                          mark=(j == z - 1))
                            te = S.do(lambda e, o=prob_t[:, h2, a:z, :], s=bank[:, 0:z - a, :]: e.activation(o, s, ACT.Copy),
                                      t, used.get(("prob_t", h2)))
                            t_banks.free[b] = te
                            ends.append(te)
                        used[("prob", h2)] = t
                        b, bank = o_banks.take()
                        PE.wait(ends)
                        for k in range(KC):
                            for j in range(i + 1):
                                t = PE.do(lambda e, o=bank[:, k, :], l=ckv_tok[:, j, k * P:(k + 1) * P], r=prob_t[:, h2, j, :], f=(j == 0), s=(j == i):
                                          e.matmul(o, l, r, start=f, stop=s), mark=(j == i))
                        used[("prob_t", h2)] = t
                        te = o_banks.free[b] = V.do(lambda e, s=bank[:, :, :]: e.tensor_copy(o_lat[:, h2, :, :], s), t, used.get(("o_lat", h2)))
                        b, bank2 = y_banks.take()
                        PE.wait(te, t_uv)
                        for k in range(KC):
                            t = PE.do(lambda e, l=w_uv[:, hd, k, :], r=o_lat[:, h2, k, :], f=(k == 0), s=(k == KC - 1):
                                      e.matmul(bank2[:, :], l, r, start=f, stop=s), mark=(k == KC - 1))
                        used[("o_lat", h2)] = t
                        y_banks.free[b] = S.do(lambda e: e.activation(x[:, hd, i * P:(i + 1) * P], bank2[:, :], ACT.Copy), t)

                    for step in pick(0) + pick(1):
                        step()
                    behind = None
                    for i in range(NT):
                        ahead = pick(i + 1) if 1 <= i < NT - 1 else []
                        per = -(-len(ahead) // HEADS)
                        for hd in range(HEADS):
                            t = weigh(i, hd)
                            if behind:
                                gather(*behind)
                            behind = (i, hd, t)
                            for step in ahead[hd * per:(hd + 1) * per]:
                                step()
                    gather(*behind)
                    barrier()

            with ExitStack() as st:
                w = Weights(st, [item(ins["a_w_o_2"][0], d) for d in range(KD)])
                banks = Banks([ps(f"s3d_bank{i}", [P, HALF], st) for i in range(8)])
                y_hi, y_lo = sb("y_hi", [P, KD, T], F32R, st), sb("y_lo", [P, KD, T], F32R, st)
                y_ready = []
                for k in range(KD):
                    y_ready.append(split_into(y_hi[:, k, :], y_lo[:, k, :], x[:, k, :]))
                    x_ready[k] = [dma(f"x{k}", x[:, k, :], x_park[:, k, :], y_ready[k])]
                out_projection(w, banks, y_hi, y_lo, y_ready, 8 * KD, x_ready)
                barrier()

        def stage_ffn():
            w_in, w_out = ins["f_w_in_2"][0], ins["f_w_out_2"][0]
            groups = [range(0, 6), range(6, 12), range(12, 17), range(17, KF)]
            with ExitStack() as st:
                items = []
                for grp in groups:
                    for n in grp:
                        items += [item(w_in, n), item(w_in, KF + n)]
                    rows_g = w_out[grp[0] * P:(grp[-1] + 1) * P, :]
                    items += [item(rows_g, d) for d in range(KD)]
                w = Weights(st, items)
                banks = Banks([ps(f"s4_bank{i}", [P, HALF], st) for i in range(8)])
                h_hi, h_lo = sb("h_hi", [P, KD, T], F32R, st), sb("h_lo", [P, KD, T], F32R, st)
                t_gain = gains(3 * KD, 10 * KD, "g_ffn_2", 0)
                with ExitStack() as st2:
                    h_ready = modulated_norm(st2, banks, x_ready, 3 * KD, 9 * KD, h_hi, h_lo, t_gain)
                    for line in LINES:
                        line.wait(h_ready[-1])
                y_hi, y_lo = sb("y_hi", [P, 6, T], F32R, st), sb("y_lo", [P, 6, T], F32R, st)
                u_pad = sb("u_pad", [P, T + 2], F32, st)
                cv = sb("cv", [P, T], F32, st)
                yv = sb("yv", [P, T], F32, st)
                t_edge = V.do(lambda e: e.memset(u_pad[:, 0:2], 0.0))
                y_free = u_free = cv_free = yv_free = None
                for grp in groups:
                    y_ready = []
                    for i, n in enumerate(grp):
                        tu = []

                        def evac_u(h, cols, bank, t):
                            a = 2 + h * HALF
                            tu.append(S.do(lambda e: e.activation(u_pad[:, a:a + HALF], bank[:, :], ACT.Copy), t, u_free))
                            return tu[-1]
                        product(w, banks, h_hi, h_lo, h_ready, evac_u)
                        t0 = V.do(lambda e, n=n: e.tensor_scalar(cv[:, :], u_pad[:, 0:T], par("f_conv_w_2", n), None, ALU.mult),
                                  tu, t_edge, cv_free)
                        for tap in (1, 2):
                            t0 = V.do(lambda e, n=n, tap=tap: e.scalar_tensor_tensor(
                                out=cv[:, :], in0=u_pad[:, tap:tap + T], scalar=par("f_conv_w_2", tap * KF + n),
                                in1=cv[:, :], op0=ALU.mult, op1=ALU.add), t0)
                        u_free = t0
                        tg = S.do(lambda e, n=n: e.activation(cv[:, :], cv[:, :], ACT.Gelu, bias=par("f_conv_b_2", n)), t0)
                        ty = []

                        def evac_v(h, cols, bank, t):
                            ty.append(V.do(lambda e: e.tensor_tensor(yv[:, cols], bank[:, :], cv[:, cols], ALU.mult), t, tg, yv_free))
                            return ty[-1]
                        product(w, banks, h_hi, h_lo, h_ready, evac_v)
                        cv_free = ty[-1]
                        yv_free = split_into(y_hi[:, i, :], y_lo[:, i, :], yv[:, :], ty, y_free)
                        y_ready.append(yv_free)
                    out_projection(w, banks, y_hi, y_lo, y_ready, 11 * KD, x_ready)
                    y_free = PE.last
                barrier()

        def stage_end():
            with ExitStack() as st:
                banks = Banks([ps(f"s9_bank{i}", [P, HALF], st) for i in range(8)])
                o_rows = sb("o_rows", [P, NT, D], F32, st)
                sq = sb("norm_sq", [P, 2, T], F32, st)
                acc = sb("norm_acc", [P, T], F32, st)
                r = sb("norm_r", [P, T], F32, st)
                t_n = [None] * KD
                t_r = inverse_rms([x[:, k, :] for k in range(KD)], [None] * KD, D, banks, sq, acc, r)
                for k in range(KD):
                    t_n[k] = V.do(lambda e, k=k: e.scalar_tensor_tensor(
                        out=x[:, k, :], in0=x[:, k, :], scalar=par("g_final_2", k), in1=r[:, :],
                        op0=ALU.mult, op1=ALU.mult), t_r)
                t_out = []
                for i in range(NT):
                    ends = []
                    for q in range(2):
                        b, bank = banks.take()
                        for k in range(4):
                            t = PE.do(lambda e, i=i, k=k, q=q, bank=bank: e.transpose(
                                bank[:, k * P:(k + 1) * P], x[:, 4 * q + k, i * P:(i + 1) * P], ident[:, :]),
                                t_n[4 * q + k], mark=(k == 3))
                        dst = o_rows[:, i, 4 * q * P:(4 * q + 4) * P]
                        if q:
                            t = S.do(lambda e, dst=dst, bank=bank: e.activation(dst, bank[:, :], ACT.Copy), t)
                        else:
                            t = V.do(lambda e, dst=dst, bank=bank: e.tensor_copy(dst, bank[:, :]), t)
                        banks.free[b] = t
                        ends.append(t)
                    t_out.append(dma("out", out[0, i * P:(i + 1) * P, :], o_rows[:, i, :], ends))
                SP.wait(t_out[-1])

        stage_setup()
        stage_conv()
        stage_dilated()
        stage_between()
        stage_latent()
        stage_ffn()
        stage_end()

        block = ctx.enter_context(nc.Block())

        @block.tensor
        def _(e):
            for step in PE.steps:
                step(e)

        @block.vector
        def _(e):
            for step in V.steps:
                step(e)

        @block.scalar
        def _(e):
            for step in S.steps:
                step(e)

        @block.gpsimd
        def _(e):
            for step in G.steps:
                step(e)

        @block.sync
        def _(e):
            for step in SP.steps:
                step(e)


_INS = ["x", "c", "norm_g", "w_mod", "b_mod", "conv_w_in", "conv_k", "conv_w_out", "dil_w_in", "dil_w_out",
        "final_g", "c_2", "rel_bias_2", "a_w_in_2", "a_g_cq_2", "a_g_ckv_2", "a_w_uq_2", "a_w_uk_2",
        "a_w_uv_2", "a_w_qi_2", "a_w_o_2", "ada_w_2", "ada_b_2", "g_mix_2", "g_ffn_2", "f_w_in_2",
        "f_conv_w_2", "f_conv_b_2", "f_w_out_2", "g_final_2"]


def kernel(**inputs):
    import concourse.bacc as bacc
    from concourse.bass_utils import run_bass_kernel_spmd

    nc = bacc.Bacc("TRN2", target_bir_lowering=False, num_devices=1)
    arrays = {f"in_{n}": np.ascontiguousarray(inputs[n]) for n in _INS}
    arrays.update({f"in_{n}": a for n, a in shape_constants().items()})
    aps = {n[3:]: nc.dram_tensor(n, a.shape, F32, kind="ExternalInput").ap() for n, a in arrays.items()}
    out = nc.dram_tensor("out_x", (1, T, D), F32, kind="ExternalOutput").ap()
    build(nc, aps, out)
    r = run_bass_kernel_spmd(nc, [arrays], core_ids=[0])
    return r.results[0]["out_x"]
```

```python
from contextlib import ExitStack

import numpy as np

import concourse.bass as bass
from concourse import mybir

P = 128
F32 = mybir.dt.float32
F32R = mybir.dt.float32r
ALU = mybir.AluOpType
ACT = mybir.ActivationFunctionType
AX = mybir.AxisListType

T = 1024
D = 1024
KD = D // P
NT = T // P
HALF = 512
NH = T // HALF
CONV_TAPS = 3
HEADS = 8
DH = D // HEADS
RATES = (1, 4, 16)
STRIDES = (1, 4, 8)
REACH = 64
Q_RANK = 256
KV_RANK = 256
IDX_HEADS = 8
IDX_DIM = 64
TOPK = 256
NUM_BUCKETS = 32
MAX_DISTANCE = 128
D_FF = 2816
KF = D_FF // P
EPS = 1e-6
MASKED = -1e30
TAKEN = -3e38
LOWEST = -3.4e38

PACK_A = [("c", KD), ("c_2", KD), ("norm_g", 2 * KD), ("final_g", KD), ("conv_k", CONV_TAPS * KD),
          ("b_mod", 2 * 3 * KD), ("g_mix_2", KD), ("g_ffn_2", KD)]
PACK_B = [("ada_b_2", 6 * KD), ("f_conv_w_2", CONV_TAPS * KF), ("g_final_2", KD),
          ("a_g_cq_2", Q_RANK // P), ("a_g_ckv_2", KV_RANK // P)]
PACK_C = [("f_conv_b_2", KF)]


def shape_constants():
    f = np.float32
    half = DH // 2
    inv = (f(10000.0) ** (-np.arange(0, DH, 2, dtype=f) / f(DH))).astype(f)
    angle = (np.arange(T, dtype=f)[:, None] * inv[None, :]).astype(f)
    cos, sin = np.cos(angle).astype(f).T, np.sin(angle).astype(f).T
    p = np.arange(P)[:, None]
    j = np.arange(3 * P)[None, :]
    band = np.where(np.abs(j - P - p) <= REACH, 0.0, MASKED).astype(f)
    k = np.arange(P)[None, :]
    pair = np.where(p % 2 == k % 2, 0.0, MASKED).astype(f)
    causal = np.where(k <= p, 0.0, MASKED).astype(f)
    dist = np.arange(-127, 256)
    n = np.maximum(dist, 0)
    exact = NUM_BUCKETS // 2
    ratio = np.log(np.maximum(n, 1).astype(f) / f(exact)) / f(np.log(MAX_DISTANCE / exact))
    large = exact + (ratio * f(NUM_BUCKETS - exact)).astype(np.int32)
    bucket = np.where(n < exact, n, np.minimum(large, NUM_BUCKETS - 1))
    assert (bucket[dist >= P] == NUM_BUCKETS - 1).all()
    hot = np.zeros((NUM_BUCKETS, dist.size + 1), f)
    hot[bucket, np.arange(dist.size)] = 1.0
    hot[NUM_BUCKETS - 1, :dist.size] -= 1.0
    hot[:, :dist.size][:, dist < 0] = 0.0
    return {
        "rope_cos": np.ascontiguousarray(np.concatenate([cos, cos], 0)),
        "rope_sin": np.ascontiguousarray(np.concatenate([-sin, sin], 0)),
        "band_mask": band, "pair_mask": pair, "causal_mask": causal,
        "bucket_hot": hot, "identity": np.eye(P, dtype=f),
    }


class Line:

    def __init__(self, name, sem):
        self.name, self.sem, self.count, self.steps, self.seen = name, sem, 0, [], {}

    def wait(self, *tokens):
        for token in tokens:
            if isinstance(token, list):
                self.wait(*token)
            elif token is not None:
                sem, value = token
                if self.seen.get(sem, 0) < value:
                    self.seen[sem] = value
                    self.steps.append(lambda e, s=sem, v=value: e.wait_ge(s, v))

    def do(self, emit, *after, mark=True):
        self.wait(*after)
        if not mark:
            self.steps.append(emit)
            return None
        self.count += 1
        self.steps.append(lambda e: emit(e).then_inc(self.sem, 1))
        return (self.sem, self.count)

    @property
    def last(self):
        return (self.sem, self.count) if self.count else None


class DmaSlot:

    def __init__(self, sem):
        self.sem, self.count = sem, 0


def build(nc, ins, out):
    ctx = ExitStack()
    with ctx:
        named = {}

        class Area:

            def __init__(self, start, size):
                self.at, self.end = start, start + size

            def sb(self, name, shape, dt=F32):
                size = 4 * int(np.prod(shape[1:]))
                assert self.at + size <= self.end, (name, self.at, size, self.end)
                named[name] = named.get(name, 0) + 1
                tile = nc.alloc_sbuf_tensor_at(f"{name}_{named[name]}", shape, dt, offset=self.at)
                self.at += -(-size // 32) * 32
                return tile

            def rest(self):
                return self.end - self.at

        def sem(name):
            return ctx.enter_context(nc.semaphore(name))

        PE, V, S, G = (Line(n, sem("done_" + n)) for n in ("pe", "dve", "act", "pool"))
        SP = Line("sp", sem("done_sp"))
        LINES = (PE, V, S, G, SP)
        slots = {}

        def dma(name, dst, src, *after):
            if name not in slots:
                slots[name] = DmaSlot(sem("dma_" + name))
            slot = slots[name]
            SP.wait(*after)
            slot.count += 16
            SP.steps.append(lambda e: e.dma_start(dst, src).then_inc(slot.sem, 16))
            return (slot.sem, slot.count)

        def everything():
            return [line.last for line in LINES] + [(s.sem, s.count) for s in slots.values()]

        def change_rooms(*after):
            for line in LINES:
                line.wait(*after)

        base = -(-nc.sbuf_base // 32) * 32
        whole = Area(base, nc.sbuf_usable_end - base)
        x = whole.sb("x", [P, KD, T])
        ident = whole.sb("ident", [P, P])
        ones = whole.sb("ones", [P, P])
        eps = whole.sb("eps", [P, 1])
        par_a = whole.sb("par_a", [P, P])
        par_b = whole.sb("par_b", [P, P])
        par_c = whole.sb("par_c", [P, sum(n for _, n in PACK_C)])
        silu_c = whole.sb("silu_c", [P, 2 * KD])
        mod = whole.sb("mod", [P, 12 * KD])
        gain = whole.sb("gain", [P, 4 * KD])
        factor = whole.sb("factor", [P, 3, NT])
        RAW, SPLIT = 3, 2
        w_raw = whole.sb("w_raw", [P, RAW, KD, P])
        w_hi = whole.sb("w_hi", [P, SPLIT, KD, P], F32R)
        w_lo = whole.sb("w_lo", [P, SPLIT, KD, P], F32R)
        H_AT = whole.at
        h_hi = whole.sb("h_hi", [P, KD, T], F32R)
        h_lo = whole.sb("h_lo", [P, KD, T], F32R)
        STAGE_AT, STAGE_SIZE = whole.at, whole.rest()
        NORM_SIZE = 4 * 4 * T
        NORM_AT = (STAGE_AT + STAGE_SIZE - NORM_SIZE) // 32 * 32
        norm_area = Area(NORM_AT, NORM_SIZE)
        acc = norm_area.sb("norm_acc", [P, 2, T])
        wide = norm_area.sb("norm_wide", [P, 2, 2, HALF])
        x_park = nc.dram_tensor("x_park", (P, KD, T), F32).ap()
        psum = ctx.enter_context(nc.psum_tensor("psum", [P, 8, HALF], F32))

        col = {}
        for tile, pack in ((par_a, PACK_A), (par_b, PACK_B), (par_c, PACK_C)):
            at = 0
            for name, rows in pack:
                col[name] = (tile, at, rows)
                at += rows

        def par(name, j):
            tile, a, _ = col[name]
            return tile[:, a + j:a + j + 1]

        bank_free = [None] * 8

        class Banks:

            def __init__(self, groups, shape=None):
                self.groups, self.shape, self.n = groups, shape, 0

            def take(self):
                group = self.groups[self.n % len(self.groups)]
                self.n += 1
                for b in group:
                    PE.wait(bank_free[b])
                tile = psum[:, group[0]:group[-1] + 1, :].rearrange("p a b -> p (a b)")
                if self.shape:
                    tile = tile[:, 0:self.shape[0] * self.shape[1]].rearrange("p (a b) -> p a b", a=self.shape[0])
                return group, tile

            def release(self, group, token):
                for b in group:
                    bank_free[b] = token

        class Weights:

            def __init__(self):
                self.items, self.room, self.hi, self.lo = [], w_raw, w_hi, w_lo
                self.raw_free, self.split_free = {}, [None] * SPLIT
                self.loaded, self.ready, self.taken, self.splits = {}, {}, 0, 0
                self.n_loaded = self.n_split = 0

            def load_next(self):
                n = self.n_loaded
                if n >= len(self.items) or (n >= RAW and n - RAW not in self.raw_free):
                    return False
                self.n_loaded += 1
                r = n % RAW
                parts, kt, _ = self.items[n]
                for a, b, src in parts:
                    self.loaded[n] = dma(f"w{r}", self.room[:, r, 0:kt, a:b], src, self.raw_free.get(n - RAW))
                return True

            def hand_on(self):
                n = self.n_split
                while n >= self.n_loaded:
                    assert self.load_next()
                self.n_split += 1
                r = n % RAW
                _, kt, split = self.items[n]
                if not split:
                    self.ready[n] = (None, r, self.loaded[n])
                    return
                s = self.splits % SPLIT
                self.splits += 1
                raw, hi, lo = self.room[:, r, 0:kt, :], self.hi[:, s, 0:kt, :], self.lo[:, s, 0:kt, :]
                t_hi = S.do(lambda e: e.activation(hi, raw, ACT.Copy), self.loaded[n], self.split_free[s])
                t_lo = G.do(lambda e: e.tensor_tensor(lo, raw, hi.bitcast(F32), ALU.subtract), t_hi)
                self.raw_free[n] = t_lo
                self.ready[n] = (s, r, t_lo)

            def take(self):
                n = self.taken
                self.taken += 1
                while self.n_split <= n or (self.n_split < min(n + 3, len(self.items)) and
                                            not any(self.items[m][2] for m in range(n + 1, self.n_split))):
                    self.hand_on()
                while self.load_next():
                    pass
                return (n,) + self.ready[n]

        w = Weights()
        tasks = []

        def run_task():
            if tasks:
                tasks.pop(0)[1]()

        def queue_task(room, task):
            tasks.append((room, task))

        def drain(room):
            while any(name == room for name, _ in tasks):
                run_task()

        def product(banks, a_hi, a_lo, a_ready, evac):
            n, s, _, t_w = w.take()
            kt = w.items[n][1]
            for h in range(NH):
                b, bank = banks.take()
                PE.wait(t_w)
                cols = slice(h * HALF, (h + 1) * HALF)
                for k in range(kt):
                    PE.wait(a_ready[h][k])
                    for i, (wp, ap) in enumerate(((w.hi, a_hi), (w.hi, a_lo), (w.lo, a_hi))):
                        first, end = k == 0 and i == 0, k == kt - 1 and i == 2
                        t = PE.do(lambda e, o=bank, l=wp[:, s, k, :], r=ap[:, k, cols], f=first, z=end:
                                  e.matmul(o, l, r, start=f, stop=z), mark=end)
                    if k == kt // 2 - 1:
                        run_task()
                banks.release(b, evac(h, cols, bank, t))
                run_task()
            w.split_free[s] = t

        def modulation(banks, c_col, mod_col, bias_ap):
            n, _, r, t_w = w.take()
            b, bank = banks.take()
            PE.wait(t_w, t_silu[0])
            for k in range(KD):
                t = PE.do(lambda e, k=k: e.matmul(bank[:, 0:1], w.room[:, r, k, :], silu_c[:, c_col + k:c_col + k + 1],
                                                  start=(k == 0), stop=(k == KD - 1)), mark=(k == KD - 1))
            w.raw_free[n] = t
            t_m = V.do(lambda e: e.tensor_tensor(mod[:, mod_col:mod_col + 1], bank[:, 0:1], bias_ap, ALU.add), t)
            banks.release(b, t_m)
            return t_m

        def gains(first, scale_col, g_name, g_first, *after):
            return V.do(lambda e: e.scalar_tensor_tensor(
                out=gain[:, first:first + KD], in0=mod[:, scale_col:scale_col + KD], scalar=1.0,
                in1=col[g_name][0][:, col[g_name][1] + g_first:col[g_name][1] + g_first + KD],
                op0=ALU.add, op1=ALU.mult), *after)

        acc_ready = [[None, None], [None, None]]
        wide_free = [None, None]

        def add_squares(src, h, first, which=0, scale=None, *after):
            cols = slice(h * HALF, (h + 1) * HALF)
            kw = {} if scale is None else {"scale": scale}
            if first:
                acc_ready[which][h] = S.do(lambda e: e.activation(acc[:, which, cols], src, ACT.Square, **kw), *after)
                return
            t = S.do(lambda e: e.activation(wide[:, which, 0, :], src, ACT.Square, **kw), *after, wide_free[which])
            acc_ready[which][h] = wide_free[which] = V.do(
                lambda e: e.tensor_tensor(acc[:, which, cols], acc[:, which, cols], wide[:, which, 0, :], ALU.add),
                t, acc_ready[which][h])

        def token_sums(banks, which, h):
            b, bank = banks.take()
            for j in range(4):
                a = h * HALF + j * P
                t = PE.do(lambda e, o=bank[:, j:j + 1], l=acc[:, which, a:a + P]: e.matmul(o, l, ones[:, 0:1], start=True, stop=True),
                          acc_ready[which][h], mark=(j == 3))
            return b, bank, t

        def inverse_root(banks, got, h, n_features, to):
            b, bank, t = got
            f = factor[:, to, 4 * h:4 * h + 4]
            t = S.do(lambda e: e.activation(f, bank[:, 0:4], ACT.Sqrt, bias=eps[:, 0:1], scale=1.0 / n_features), t)
            banks.release(b, t)
            return V.do(lambda e: e.reciprocal(f, f), t)

        def spread(banks, h, which, diag, *after):
            f = factor[:, which, 4 * h:4 * h + 4].unsqueeze(2).to_broadcast([P, 4, P])
            eye = ident[:, :].unsqueeze(1).to_broadcast([P, 4, P])
            t = V.do(lambda e: e.tensor_tensor(diag.rearrange("p (a b) -> p a b", a=4), eye, f, ALU.mult), *after)
            b, bank = banks.take()
            t = PE.do(lambda e: e.matmul(bank, ones[:, :], diag, start=True, stop=True), t)
            return b, bank, t

        def norm_half(banks, h, gain_col, shift_col, x_ready, factor_row, t_factor, *after):
            cols = slice(h * HALF, (h + 1) * HALF)
            diag = wide[:, h, 1, :]
            b, r, t_r = spread(banks, h, factor_row, diag, t_factor, wide_free[h])
            ready, used = [], [wide_free[h], t_r]
            for k in range(KD):
                xn = wide[:, h, k % 2, :]
                shift = mod[:, shift_col + k:shift_col + k + 1]
                t = V.do(lambda e, k=k, xn=xn: e.scalar_tensor_tensor(
                    out=xn, in0=x[:, k, cols], scalar=gain[:, gain_col + k:gain_col + k + 1], in1=r,
                    op0=ALU.mult, op1=ALU.mult), t_r, used[k % 2], x_ready[k], *after)
                t_hi = S.do(lambda e, k=k, xn=xn, shift=shift: e.activation(h_hi[:, k, cols], xn, ACT.Identity, bias=shift), t)
                t = used[k % 2] = V.do(lambda e, k=k, xn=xn, shift=shift: e.scalar_tensor_tensor(
                    out=h_lo[:, k, cols], in0=xn, scalar=shift, in1=h_hi[:, k, cols].bitcast(F32),
                    op0=ALU.add, op1=ALU.subtract), t_hi)
                ready.append(t)
            banks.release(b, t)
            wide_free[h] = t
            return ready

        def modulated_norm(banks, gain_col, shift_col, x_ready, *after):
            h_ready = []
            sums = [token_sums(banks, 0, h) for h in range(NH)]
            for h in range(NH):
                t = inverse_root(banks, sums[h], h, D, 0)
                h_ready.append(norm_half(banks, h, gain_col, shift_col, x_ready, 0, t, *after))
            return h_ready

        def split_halves(hi, lo, src, ready, after):
            for h in range(NH):
                cols = slice(h * HALF, (h + 1) * HALF)
                t = S.do(lambda e, c=cols: e.activation(hi[:, c], src[:, c], ACT.Copy), after[h])
                ready[h].append(G.do(lambda e, c=cols: e.tensor_tensor(lo[:, c], src[:, c], hi[:, c].bitcast(F32), ALU.subtract), t))

        def out_projection(banks, y_hi, y_lo, y_ready, gate_col, x_ready, squares=(), before_squares=()):
            for d in range(KD):
                def evac(h, cols, bank, t, d=d):
                    t = V.do(lambda e: e.scalar_tensor_tensor(
                        out=x[:, d, cols], in0=bank, scalar=mod[:, gate_col + d:gate_col + d + 1],
                        in1=x[:, d, cols], op0=ALU.mult, op1=ALU.add), t, x_ready[d])
                    x_last[d][h] = t
                    for which, scale in enumerate(squares):
                        add_squares(x[:, d, cols], h, d == 0, which, scale and par(scale, d), t, *before_squares)
                    return t
                x_last = x_lasts
                product(banks, y_hi, y_lo, y_ready, evac)
            for d in range(KD):
                x_ready[d] = list(x_lasts[d])

        x_lasts = [[None, None] for _ in range(KD)]

        def block_of(w2d, n):
            return w2d.rearrange("(k p) n -> p k n", p=P)[:, :, n * P:(n + 1) * P]

        def item(w2d, n, split=True):
            src = block_of(w2d, n)
            return ([(0, P, src)], src.shape[1], split)

        w_mod, ada_w = ins["w_mod"], ins["ada_w_2"][0]
        x_ready = [[] for _ in range(KD)]
        t_silu = [None]
        all_banks = [(b,) for b in range(8)]

        def stage_setup():
            banks = Banks(all_banks)
            area = Area(H_AT, 4 * (3 * P + NT * D))
            x_rows = area.sb("x_rows", [P, NT, D])
            rows = area.sb("par_rows", [P, 3, P])
            t_id = dma("ident", ident[:, :], ins["identity"])
            t_par = []
            for p_i, pack in enumerate((PACK_A, PACK_B, PACK_C)):
                a = 0
                for name, n in pack:
                    flat = ins[name]
                    names = " ".join("abcd"[:len(flat.shape)])
                    flat = flat.rearrange(f"{names} -> ({names})") if len(flat.shape) > 1 else flat
                    t_par.append(dma("par", rows[a:a + n, p_i, :], flat.rearrange("(j p) -> j p", p=P)))
                    a += n
            t_x = [dma(f"x{i}", x_rows[:, i, :], ins["x"][0, i * P:(i + 1) * P, :]) for i in range(NT)]
            t_ones = V.do(lambda e: e.memset(ones[:, :], 1.0))
            V.do(lambda e: e.memset(eps[:, :], EPS))
            for p_i, (tile, pack) in enumerate(((par_a, PACK_A), (par_b, PACK_B), (par_c, PACK_C))):
                n = sum(r for _, r in pack)
                b, bank = banks.take()
                t = PE.do(lambda e, n=n, p_i=p_i, bank=bank: e.transpose(bank[:, 0:n], rows[0:n, p_i, :], ident[0:n, 0:n]),
                          t_id, t_par[-1])
                t = V.do(lambda e, n=n, tile=tile, bank=bank: e.tensor_copy(tile[:, 0:n], bank[:, 0:n]), t)
                banks.release(b, t)
            t_silu[0] = S.do(lambda e: e.activation(silu_c[:, :], par_a[:, 0:2 * KD], ACT.Silu), t)
            PE.wait(t_ones)
            for h in range(NH):
                got = [[] for _ in range(KD)]
                for i in range(4 * h, 4 * h + 4):
                    for q in range(2):
                        b, bank = banks.take()
                        PE.wait(t_x[i])
                        for k in range(4):
                            t = PE.do(lambda e, i=i, k=k, q=q, bank=bank: e.transpose(
                                bank[:, k * P:(k + 1) * P], x_rows[:, i, (4 * q + k) * P:(4 * q + k + 1) * P], ident[:, :]),
                                mark=(k == 3))
                        dst = x[:, 4 * q:4 * q + 4, i * P:(i + 1) * P]
                        src = bank.rearrange("p (k n) -> p k n", k=4)
                        if q:
                            t = S.do(lambda e, dst=dst, src=src: e.activation(dst, src, ACT.Copy), t)
                        else:
                            t = V.do(lambda e, dst=dst, src=src: e.tensor_copy(dst, src), t)
                        banks.release(b, t)
                        for k in range(4):
                            got[4 * q + k].append(t)
                            x_ready[4 * q + k].append(t)
                for k in range(KD):
                    add_squares(x[:, k, h * HALF:(h + 1) * HALF], h, k == 0, 0, None, got[k])
                for j in range(KD * h, KD * (h + 1)):
                    t_mod = modulation(banks, 0, j, par("b_mod", j))
            return gains(0, KD, "norm_g", 0, t_mod)

        GROUP = 4

        def conv_items():
            w_in, w_out = ins["conv_w_in"][0], ins["conv_w_out"][0]
            items = [item(w_mod[0], j, False) for j in range(2 * KD)]
            mods = [item(w_mod[0], j, False) for j in range(2 * KD, 3 * KD)] + [item(w_mod[1], j, False) for j in range(3 * KD)]
            for g in range(KD // GROUP):
                for e_ in range(GROUP * g, GROUP * (g + 1)):
                    for part in (1, 2, 3, 0):
                        items += [item(w_in, KD * part + e_), mods.pop(0)]
                items += [item(w_out[GROUP * g * P:GROUP * (g + 1) * P, :], d) for d in range(KD)]
            assert not mods
            return items

        def stage_conv(t_gain):
            banks = Banks(all_banks)
            area = Area(STAGE_AT, NORM_AT - STAGE_AT)
            y_hi, y_lo = area.sb("y_hi", [P, GROUP, T], F32R), area.sb("y_lo", [P, GROUP, T], F32R)
            c_sb, cv, zs = area.sb("c_sb", [P, T]), area.sb("cv", [P, T]), area.sb("zs", [P, T])
            t_pad, yv = area.sb("t_pad", [P, T + 2]), area.sb("yv", [P, T])
            change_rooms(x_ready)
            h_ready = modulated_norm(banks, 0, 0, x_ready, t_gain)
            V.do(lambda e: e.memset(t_pad[:, 0:1], 0.0))
            t_edge = V.do(lambda e: e.memset(t_pad[:, T + 1:T + 2], 0.0))
            y_free = t_cfree = t_tfree = t_cvfree = None
            t_yfree = [None, None]
            todo = list(range(2 * KD, 6 * KD))

            def one_modulation():
                j = todo.pop(0)
                modulation(banks, 0, j, par("b_mod", j))

            for g in range(KD // GROUP):
                y_ready = [[], []]
                for e_ in range(GROUP * g, GROUP * (g + 1)):
                    tk, tc, tz, ty = [None] * NH, [None] * NH, [None] * NH, [None] * NH

                    def evac_c(h, cols, bank, t):
                        tc[h] = S.do(lambda e: e.activation(c_sb[:, cols], bank, ACT.Copy), t, t_cfree)
                        return tc[h]
                    product(banks, h_hi, h_lo, h_ready, evac_c)
                    one_modulation()

                    def evac_x(h, cols, bank, t):
                        a = 1 + h * HALF
                        tk[h] = V.do(lambda e: e.tensor_tensor(t_pad[:, a:a + HALF], bank, c_sb[:, cols], ALU.mult),
                                     t, tc[h], t_tfree)
                        return tk[h]
                    product(banks, h_hi, h_lo, h_ready, evac_x)
                    one_modulation()
                    t_cfree = tk[1]
                    t0 = V.do(lambda e, e_=e_: e.tensor_scalar(cv[:, :], t_pad[:, 0:T], par("conv_k", e_), None, ALU.mult),
                              tk, t_edge, t_cvfree)
                    for tap in (1, 2):
                        t0 = V.do(lambda e, e_=e_, tap=tap: e.scalar_tensor_tensor(
                            out=cv[:, :], in0=t_pad[:, tap:tap + T], scalar=par("conv_k", tap * KD + e_),
                            in1=cv[:, :], op0=ALU.mult, op1=ALU.add), t0)
                    t_tfree = t_cv = t0

                    def evac_z(h, cols, bank, t):
                        t1 = S.do(lambda e: e.activation(zs[:, cols], bank, ACT.Silu), t, t_cvfree)
                        tz[h] = V.do(lambda e: e.tensor_tensor(cv[:, cols], cv[:, cols], zs[:, cols], ALU.mult), t1, t_cv)
                        return t1
                    product(banks, h_hi, h_lo, h_ready, evac_z)
                    one_modulation()

                    def evac_b(h, cols, bank, t):
                        ty[h] = V.do(lambda e: e.tensor_tensor(yv[:, cols], bank, cv[:, cols], ALU.mult),
                                     t, tz[h], t_yfree)
                        return ty[h]
                    product(banks, h_hi, h_lo, h_ready, evac_b)
                    one_modulation()
                    t_cvfree = ty[1]
                    i = e_ - GROUP * g
                    S.wait(y_free)
                    split_halves(y_hi[:, i, :], y_lo[:, i, :], yv, y_ready, ty)
                    t_yfree = [y_ready[0][-1], y_ready[1][-1]]
                out_projection(banks, y_hi, y_lo, y_ready, 2 * KD, x_ready, (None,) if g else ())
                y_free = PE.last
            return gains(KD, 4 * KD, "norm_g", KD)

        def dilated_items():
            w_in, w_out = ins["dil_w_in"][0], ins["dil_w_out"][0]
            n_g, items = len(RATES), []
            for hd in range(HEADS):
                items += [item(w_in, 2 * n_g * HEADS + hd), item(w_in, (2 * n_g + 1) * HEADS + hd)]
                for g in range(n_g):
                    for n, block in enumerate((g * HEADS + hd, (n_g + g) * HEADS + hd)):
                        items += [item(w_in, block), item(ada_w, 6 * hd + 2 * g + n, False)]
            return items + [item(w_out, d) for d in range(KD)]

        def stage_dilated(t_gain):
            SCALE = float(DH) ** -0.5
            G_RATES = len(RATES)
            banks = Banks([(0,), (1,), (2,)])
            s_banks = Banks([(3,), (4,)], (2, 256))
            t_banks = Banks([(5,), (6,)], (4, P))
            o_banks = Banks([(7,)], (4, P))
            area = Area(STAGE_AT, STAGE_SIZE)
            release = everything()
            h_ready = modulated_norm(Banks(all_banks), KD, 3 * KD, x_ready, t_gain)
            change_rooms(release, h_ready[0], h_ready[1])
            t_park = dma("park", x_park, x[:, :, :], x_ready)
            cos, sin = area.sb("cos", [P, T]), area.sb("sin", [P, T])
            band, pair_m = area.sb("band", [P, 3 * P]), area.sb("pair_m", [P, P])
            dma("tables", cos[:, :], ins["rope_cos"])
            dma("tables", sin[:, :], ins["rope_sin"])
            dma("tables", band[:, :], ins["band_mask"])
            t_tab = dma("tables", pair_m[:, :], ins["pair_mask"])
            qk = area.sb("qk", [P, 2, 2, T])
            v_t = area.sb("v_t", [P, T])
            v_tok = [area.sb(f"v_tok{g}", [P, NT + (g == 0), P]) for g in range(G_RATES)]
            o_g = [area.sb(f"o_g{g}", [P, T]) for g in range(G_RATES)]
            l_g = [area.sb(f"l_g{g}", [P, T]) for g in range(G_RATES)]
            rot, swp = area.sb("rot", [P, HALF]), area.sb("swp", [P, HALF])
            prob = area.sb("prob", [P, 2, 2, 256])
            prob_t = area.sb("prob_t", [P, 2, 4, P])
            mx = area.sb("mx", [P, HALF])[:, :]
            stat = area.sb("stat", [P, 2, 3, G_RATES * NT])
            used = {}
            y_done = [None] * HEADS

            def natural(ap, r):
                return ap.rearrange("p (i c) -> p i c", c=r)

            def rope_evac(dst, g, ready):
                r = STRIDES[g]

                def evac(h, cols, bank, t):
                    t1 = V.do(lambda e: e.tensor_tensor(rot[:, :], bank, cos[:, cols], ALU.mult), t, t_tab, used.get("rot"))
                    S.do(lambda e: e.activation(swp[0:DH // 2, :], bank[DH // 2:DH, :], ACT.Copy), t1, used.get("swp"))
                    t2 = S.do(lambda e: e.activation(swp[DH // 2:DH, :], bank[0:DH // 2, :], ACT.Copy))
                    t3 = V.do(lambda e: e.tensor_tensor(swp[:, :], swp[:, :], sin[:, cols], ALU.mult), t2)
                    per = HALF // r
                    to = dst.rearrange("p (c i) -> p i c", c=r)[:, h * per:(h + 1) * per, :]
                    t4 = V.do(lambda e: e.tensor_tensor(to, natural(rot[:, :], r), natural(swp[:, :], r), ALU.add), t3)
                    used["rot"] = used["swp"] = t4
                    ready.append(t4)
                    return t2
                return evac

            def tile_plan(g, t):
                if g == 0:
                    lo, hi = max(0, P * t - REACH), min(T, P * t + P + REACH)
                    off = lo - (P * t - REACH)
                    chunks = [(max(off, 0), P - off, t), (P, min(P, hi - P * t - REACH), t + 1)]
                    return lo, hi - lo, off, band[:, REACH + off:REACH + off + hi - lo], chunks
                if g == 1:
                    c, u = divmod(t, 2)
                    return 256 * c, 256, 0, band[:, P * (1 - u):P * (1 - u) + 256], [(0, P, 2 * c), (P, P, 2 * c + 1)]
                return P * t, P, 0, pair_m[:, :], [(0, P, t)]

            def turn_values(hd, t_v):
                plans = [[v_t[:, max(0, P * j - REACH):min(T, P * j + REACH)] for j in range(NT + 1)]]
                s4 = v_t[:, :].rearrange("p (i c) -> p c i", c=STRIDES[1])
                plans.append([s4[:, j // 2, P * (j % 2):P * (j % 2) + P] for j in range(NT)])
                s8 = v_t[:, :].rearrange("p (i c) -> p c i", c=STRIDES[2])
                plans.append([s8[:, j, :] for j in range(NT)])

                def turn(g, js):
                    b, bank = t_banks.take()
                    PE.wait(t_v)
                    t = None
                    for n, j in enumerate(js):
                        src = plans[g][j]
                        rows = src.free_size()
                        t = PE.do(lambda e, o=bank[0:rows, n, :], i=src: e.transpose(o, i, ident[:, :]), mark=True)
                    runs = []
                    for n, j in enumerate(js):
                        rows = plans[g][j].free_size()
                        if runs and runs[-1][2] == rows:
                            runs[-1][1] = n + 1
                        else:
                            runs.append([n, n + 1, rows])
                    for a, z, rows in runs:
                        te = S.do(lambda e, o=v_tok[g][0:rows, js[a]:js[a] + z - a, :], i=bank[0:rows, a:z, :]:
                                  e.activation(o, i, ACT.Copy), t, used.get(("v_tok", g)))
                    t_banks.release(b, te)
                    v_ready[g] = te
                    used["v_t"] = t

                for g in range(G_RATES):
                    n = len(plans[g])
                    todo = [list(range(a, min(a + 4, n))) for a in range(0, n, 4)]
                    for js in todo:
                        queue_task("v_t", lambda g=g, js=js: turn(g, js))

            v_ready = [None] * G_RATES

            def attend(hd, g, q, k, qk_ready, qk_name):
                par_ = hd % 2
                keep = {}

                def scores(p):
                    b, bank = s_banks.take()
                    PE.wait(qk_ready)
                    i = p % 2
                    room = prob[:, i, :, :]
                    ts = []
                    for u in range(2):
                        t = 2 * p + u
                        lo, n, off, mask, _ = tile_plan(g, t)
                        tt = PE.do(lambda e, o=bank[:, u, off:off + n], l=q[:, P * t:P * t + P], r=k[:, lo:lo + n]:
                                   e.matmul(o, l, r, start=True, stop=True))
                    for u in range(2):
                        t = 2 * p + u
                        lo, n, off, mask, _ = tile_plan(g, t)
                        c = g * NT + t
                        ts.append(V.do(lambda e, o=room[:, u, off:off + n], a=bank[:, u, off:off + n], m=mask, c=c:
                                       e.tensor_tensor_reduce(o, a, m, 1.0, LOWEST, ALU.add, ALU.max, stat[:, par_, 0, c:c + 1]),
                                       tt, used.get(("prob", i)), used.get(("stat", par_))))
                    used[qk_name] = tt
                    s_banks.release(b, ts[-1])
                    c = g * NT + 2 * p
                    t1 = V.do(lambda e: e.tensor_scalar(stat[:, par_, 1, c:c + 2], stat[:, par_, 0, c:c + 2], -SCALE, None, ALU.mult), ts)
                    te = []
                    for u in range(2):
                        _, n, off, _, _ = tile_plan(g, 2 * p + u)
                        te.append(S.do(lambda e, a=room[:, u, off:off + n], c=c + u: e.activation(
                            a, a, ACT.Exp, bias=stat[:, par_, 1, c:c + 1], scale=SCALE, accum_out=stat[:, par_, 2, c:c + 1]), t1))
                    t2 = V.do(lambda e: e.reciprocal(stat[:, par_, 1, c:c + 2], stat[:, par_, 2, c:c + 2]), te)
                    for u in range(2):
                        _, n, off, _, _ = tile_plan(g, 2 * p + u)
                        t3 = V.do(lambda e, a=room[:, u, off:off + n], c=c + u: e.tensor_scalar(
                            a, a, stat[:, par_, 1, c:c + 1], None, ALU.mult), t2)
                    keep[p] = [t3, None]

                def turn(p):
                    b, bank = t_banks.take()
                    i = p % 2
                    PE.wait(keep[p][0])
                    slots_ = []
                    n_ = 0
                    for u in range(2):
                        for (a, n, ch) in tile_plan(g, 2 * p + u)[4]:
                            tt = PE.do(lambda e, o=bank[0:n, n_, :], s=prob[:, i, u, a:a + n]: e.transpose(o, s, ident[:, :]))
                            slots_.append((u, n_, n, ch))
                            n_ += 1
                    used[("prob", i)] = tt
                    runs = []
                    for (_, s_, n, _) in slots_:
                        if runs and runs[-1][2] == n:
                            runs[-1][1] = s_ + 1
                        else:
                            runs.append([s_, s_ + 1, n])
                    for a, z, n in runs:
                        te = S.do(lambda e, o=prob_t[0:n, i, a:z, :], s=bank[0:n, a:z, :]: e.activation(o, s, ACT.Copy),
                                  tt, used.get(("prob_t", i)))
                    t_banks.release(b, te)
                    keep[p] = [te, slots_]

                def values(p):
                    i = p % 2
                    if i == 0:
                        keep["o"] = o_banks.take()
                    b, bank = keep["o"]
                    te, slots_ = keep[p]
                    PE.wait(te, v_ready[g])
                    for n_, (u, s_, n, ch) in enumerate(slots_):
                        first = n_ == 0 or slots_[n_ - 1][0] != u
                        last = n_ == len(slots_) - 1 or slots_[n_ + 1][0] != u
                        tt = PE.do(lambda e, o=bank[:, 2 * i + u, :], l=v_tok[g][0:n, ch, :], r=prob_t[0:n, i, s_, :], f=first, z=last:
                                   e.matmul(o, l, r, start=f, stop=z))
                    used[("prob_t", i)] = used[("v_tok", g)] = tt
                    if i == 1:
                        r = STRIDES[g]
                        half = p // 2
                        src = bank.rearrange("p a b -> p (a b)")
                        if r == 1:
                            src, to = src, o_g[g][:, half * HALF:(half + 1) * HALF]
                        else:
                            src = src.rearrange("p (c i) -> p c i", i=T // r)
                            to = o_g[g][:, :].rearrange("p (i c) -> p c i", c=r)[:, half * r // 2:(half + 1) * r // 2, :]
                        t = S.do(lambda e: e.activation(to, src, ACT.Copy), tt, used.get(("o_g", g)))
                        o_banks.release(b, t)
                        o_ready[g] = t

                queue_task(qk_name, lambda: scores(0))
                queue_task(qk_name, lambda: scores(1))
                queue_task(qk_name, lambda: (turn(0), scores(2)))
                queue_task(qk_name, lambda: (turn(1), scores(3)))
                queue_task(None, lambda: (values(0), turn(2)))
                queue_task(None, lambda: (values(1), turn(3)))
                queue_task(None, lambda: values(2))
                queue_task(None, lambda: values(3))

            o_ready = [None] * G_RATES

            def combine(hd):
                par_ = hd % 2
                l_ready = [[None] * NH for _ in range(G_RATES)]

                eye = ident[:, :].unsqueeze(1).to_broadcast([P, 4, P])
                t_diag = [None] * (G_RATES * NH)

                def diagonal(n):
                    c = 4 * n
                    lse = stat[:, par_, 1, c:c + 4].unsqueeze(2).to_broadcast([P, 4, P])
                    room = prob[:, n % 2, :, :].rearrange("p a (b c) -> p (a b) c", c=P)
                    t_diag[n] = used[("stat", par_)] = used[("lse", par_)] = G.do(
                        lambda e: e.tensor_tensor(room, eye, lse, ALU.mult), t_lse[0], used.get(("prob", n % 2)))

                def spread(n):
                    g, half = divmod(n, NH)
                    b, bank = t_banks.take()
                    flat = bank.rearrange("p a b -> p (a b)")
                    room = prob[:, n % 2, :, :].rearrange("p a b -> p (a b)")
                    tt = used[("prob", n % 2)] = PE.do(lambda e: e.matmul(flat, ones[:, :], room, start=True, stop=True), t_diag[n])
                    if n + 2 < G_RATES * NH:
                        diagonal(n + 2)
                    r = STRIDES[g]
                    if r == 1:
                        src, to = flat, l_g[g][:, half * HALF:(half + 1) * HALF]
                    else:
                        src = flat.rearrange("p (c i) -> p c i", i=T // r)
                        to = l_g[g][:, :].rearrange("p (i c) -> p c i", c=r)[:, half * r // 2:(half + 1) * r // 2, :]
                    t = S.do(lambda e: e.activation(to, src, ACT.Copy), tt, used.get(("l_g", g)))
                    t_banks.release(b, t)
                    l_ready[g][half] = t

                t_lse = [None]

                def start():
                    t = S.do(lambda e: e.activation(stat[:, par_, 1, :], stat[:, par_, 2, :], ACT.Ln), used.get(("lse", par_)), o_ready)
                    t_lse[0] = V.do(lambda e: e.scalar_tensor_tensor(
                        out=stat[:, par_, 1, :], in0=stat[:, par_, 0, :], scalar=SCALE, in1=stat[:, par_, 1, :],
                        op0=ALU.mult, op1=ALU.add), t)
                    diagonal(0)
                    diagonal(1)

                t_sub, t_exp, t_sum, t_o = {}, {}, {}, {}
                halves = [slice(half * HALF, (half + 1) * HALF) for half in range(NH)]

                def less_maximum(half):
                    for cols in (halves[half],):
                        L = [l[:, cols] for l in l_g]
                        t = V.do(lambda e, L=L: e.tensor_tensor(mx, L[0], L[1], ALU.max), l_ready, used.get("mx"))
                        t = V.do(lambda e, L=L: e.tensor_tensor(mx, mx, L[2], ALU.max), t)
                        for g in range(G_RATES):
                            used["mx"] = t_sub[half, g] = V.do(lambda e, l=L[g]: e.tensor_tensor(l, l, mx, ALU.subtract), t)

                def weigh(half):
                    for cols in (halves[half],):
                        L, O = [l[:, cols] for l in l_g], [o[:, cols] for o in o_g]
                        for g in range(G_RATES):
                            te = S.do(lambda e, l=L[g]: e.activation(l, l, ACT.Exp), t_sub[half, g])
                            t_exp[g] = V.do(lambda e, o=O[g], l=L[g]: e.tensor_tensor(o, o, l, ALU.mult), te, o_ready[g])
                        t = V.do(lambda e, L=L: e.tensor_tensor(L[0], L[0], L[1], ALU.add), te, t_exp[0])
                        t_sum[half] = V.do(lambda e, L=L: e.tensor_tensor(L[0], L[0], L[2], ALU.add), t)
                        t = V.do(lambda e, O=O: e.tensor_tensor(O[0], O[0], O[1], ALU.add), t_exp[1])
                        t_o[half] = V.do(lambda e, O=O: e.tensor_tensor(O[0], O[0], O[2], ALU.add), t, t_exp[2])

                def gate():
                    total = l_g[0][:, :]
                    t = S.do(lambda e: e.activation(total, total, ACT.Ln), t_sum[0], t_sum[1])
                    t_r = S.do(lambda e: e.activation(total, total, ACT.Exp, scale=-1.0), t)
                    for half, cols in enumerate(halves):
                        l, o, y = l_g[0][:, cols], o_g[0][:, cols], x[:, hd, cols]
                        t = V.do(lambda e, l=l, o=o: e.tensor_tensor(o, o, l, ALU.mult), t_r, t_o[half])
                        t = V.do(lambda e, y=y, o=o: e.tensor_tensor(y, o, y, ALU.mult), t, z_ready[hd])
                    for g in range(G_RATES):
                        used[("l_g", g)] = used[("o_g", g)] = t
                    y_done[hd] = t

                last_task = tasks.pop()
                queue_task(last_task[0], lambda: (last_task[1](), start()))
                for n in range(0, G_RATES * NH, 2):
                    queue_task(None, lambda n=n: (spread(n), spread(n + 1)))
                for half in range(NH):
                    queue_task(None, lambda half=half: less_maximum(half))
                for half in range(NH):
                    queue_task(None, lambda half=half: weigh(half))
                queue_task(None, gate)

            z_ready = [None] * HEADS
            for hd in range(HEADS):
                tv = []
                drain("v_t")

                def evac_v(h, cols, bank, t):
                    tv.append(S.do(lambda e: e.activation(v_t[:, cols], bank, ACT.Copy), t, used.get("v_t")))
                    return tv[-1]
                product(banks, h_hi, h_lo, h_ready, evac_v)
                turn_values(hd, tv)

                def evac_z(h, cols, bank, t, hd=hd):
                    z_ready[hd] = S.do(lambda e: e.activation(x[:, hd, cols], bank, ACT.Silu), t, t_park)
                    return z_ready[hd]
                product(banks, h_hi, h_lo, h_ready, evac_z)
                for g in range(G_RATES):
                    which = (hd * G_RATES + g) % 2
                    name = ("qk", which)
                    ready = []
                    drain(name)
                    for n in range(2):
                        dst = qk[:, which, n, :]
                        wait_for = name
                        ev = rope_evac(dst, g, ready)

                        def evac(h, cols, bank, t, ev=ev, wait_for=wait_for):
                            V.wait(used.get(wait_for))
                            return ev(h, cols, bank, t)
                        product(banks, h_hi, h_lo, h_ready, evac)
                        run_task()
                        j = 6 * hd + 2 * g + n
                        modulation(banks, KD, 6 * KD + j, par("ada_b_2", j))
                    attend(hd, g, qk[:, which, 0, :], qk[:, which, 1, :], ready, name)
                combine(hd)
            y_ready = [[], []]
            t_h_free = PE.last
            todo = list(range(KD))
            S.wait(t_h_free)

            def split_y():
                k = todo.pop(0)
                split_halves(h_hi[:, k, :], h_lo[:, k, :], x[:, k, :], y_ready, [y_done[k]] * NH)
                x_ready[k] = [dma(f"x{k}", x[:, k, :], x_park[:, k, :], y_ready[0][-1], y_ready[1][-1], t_park)]
            while tasks:
                run_task()
                if len(todo) > 1 and y_done[todo[0]]:
                    split_y()
            while todo:
                split_y()
            out_projection(banks, h_hi, h_lo, y_ready, 5 * KD, x_ready, (None, "final_g"), everything())


        def stage_between():
            banks = Banks(all_banks)
            t_gain = gains(2 * KD, 7 * KD, "g_mix_2", 0, V.last)
            g_all = col["final_g"][0][:, col["final_g"][1]:col["final_g"][1] + KD]
            t_gain = V.do(lambda e: e.tensor_tensor(gain[:, 2 * KD:3 * KD], gain[:, 2 * KD:3 * KD], g_all, ALU.mult), t_gain)
            h_ready = []
            sums = [[token_sums(banks, which, h) for which in range(2)] for h in range(NH)]

            def norm_both(h):
                f0, f1, f2 = (factor[:, i, 4 * h:4 * h + 4] for i in range(3))
                t_r = inverse_root(banks, sums[h][0], h, D, 0)
                b, bank, t = sums[h][1]
                t = V.do(lambda e: e.tensor_tensor(f1, bank[:, 0:4], f0, ALU.mult), t, t_r)
                banks.release(b, t)
                t = V.do(lambda e: e.tensor_tensor(f1, f1, f0, ALU.mult), t)
                t = S.do(lambda e: e.activation(f1, f1, ACT.Sqrt, bias=eps[:, 0:1], scale=1.0 / D), t)
                t = V.do(lambda e: e.reciprocal(f1, f1), t)
                t = V.do(lambda e: e.tensor_tensor(f2, f1, f0, ALU.mult), t)
                h_ready.append(norm_half(banks, h, 2 * KD, 6 * KD, x_ready, 2, t, t_gain))
                return t_r

            def first_norm(h, t_r):
                cols = slice(h * HALF, (h + 1) * HALF)
                b, r, t = spread(banks, h, 0, wide[:, h, 1, :], t_r, wide_free[h])
                for k in range(KD):
                    t_x = V.do(lambda e, k=k: e.scalar_tensor_tensor(
                        out=x[:, k, cols], in0=x[:, k, cols], scalar=par("final_g", k), in1=r,
                        op0=ALU.mult, op1=ALU.mult), t, x_ready[k], h_ready[h])
                    ends[k].append(t_x)
                banks.release(b, t_x)
                wide_free[h] = t_x

            ends = [[] for _ in range(KD)]
            t_r = [norm_both(h) for h in range(NH)]
            for h in range(NH):
                first_norm(h, t_r[h])
            for k in range(KD):
                x_ready[k] = ends[k]
            return h_ready

        KQ, KC = Q_RANK // P, KV_RANK // P
        I_KIDX, I_WIDX = Q_RANK + KV_RANK, Q_RANK + KV_RANK + IDX_DIM

        def latent_items():
            w_in = ins["a_w_in_2"][0]
            kcols = w_in.rearrange("(k p) n -> p k n", p=P)[:, :, I_KIDX:I_WIDX]
            return ([item(w_in, n) for n in range(KQ + KC)] + [([(0, IDX_DIM, kcols), (IDX_DIM, P, kcols)], KD, True)] +
                    [item(ins["a_w_qi_2"][0], n) for n in range(IDX_HEADS * IDX_DIM // P)] +
                    [item(ins["a_w_uq_2"][0], n) for n in range(HEADS)] +
                    [item(ins["a_w_o_2"][0], d) for d in range(KD)])

        def stage_latent(release, h_ready):
            w_in = ins["a_w_in_2"][0]
            banks = Banks(all_banks)
            area = Area(STAGE_AT, STAGE_SIZE)
            ckv_t = area.sb("ckv_t", [P, KC, T])
            ckv_tok = area.sb("ckv_tok", [P, NT, KV_RANK])
            k_idx = area.sb("k_idx", [P, T])
            w_idx = area.sb("w_idx", [P, NT, IDX_HEADS])
            q_idx = area.sb("q_idx", [P, IDX_HEADS * IDX_DIM // P, T])
            bias = area.sb("bias", [P, HEADS, 2 * P])
            causal = area.sb("causal", [P, P])
            top8 = area.sb("top8", [P, 8])
            early = Area(area.at, NORM_AT - area.at)
            cq_hi, cq_lo = early.sb("cq_hi", [P, KQ, T], F32R), early.sb("cq_lo", [P, KQ, T], F32R)
            wi = early.sb("wi", [P, KD, IDX_HEADS])
            wi_hi, wi_lo = early.sb("wi_hi", [P, KD, IDX_HEADS], F32R), early.sb("wi_lo", [P, KD, IDX_HEADS], F32R)
            rel, hot = early.sb("rel", [NUM_BUCKETS, IDX_HEADS]), early.sb("hot", [NUM_BUCKETS, 3 * P])
            late = Area(area.at, area.rest())
            near = late.sb("near", [P, 2, 2 * P])
            RING = 3
            prob = late.sb("prob", [P, RING, T])
            prob_t = late.sb("prob_t", [P, 2, NT, P])
            o_lat = late.sb("o_lat", [P, 2, KC, P])
            q_lat = late.sb("q_lat", [P, 2, KC, P])
            stat = late.sb("stat", [P, RING, 5])
            in_h = Area(H_AT, STAGE_AT - H_AT)
            q = in_h.sb("q", [P, HEADS, T])
            w_uk, w_uv = in_h.sb("w_uk", [P, HEADS, KV_RANK]), in_h.sb("w_uv", [P, HEADS, KC, P])
            work = in_h.sb("work", [P, T])
            relu = in_h.sb("relu", [P, 2, HALF])
            keep = in_h.sb("keep", [P, 2, T])

            change_rooms(release, h_ready[0], h_ready[1])
            t_rel = dma("rel", rel[:, :], ins["rel_bias_2"])
            t_hot = dma("hot", hot[:, :], ins["bucket_hot"])
            t_wi = dma("wi", wi[:, :, :], w_in.rearrange("(k p) n -> p k n", p=P)[:, :, I_WIDX:I_WIDX + IDX_HEADS])
            t_causal = dma("causal", causal[:, :], ins["causal_mask"])
            t_park = dma("park", x_park, x[:, :, :], x_ready)

            c_ready = [[None] * NH for _ in range(KQ + KC)]
            for n in range(KQ + KC):
                which, k = divmod(n, KQ)

                def evac(h, cols, bank, t, n=n, which=which, k=k):
                    c_ready[n][h] = S.do(lambda e: e.activation(x[:, n, cols], bank, ACT.Copy), t, t_park)
                    add_squares(x[:, n, cols], h, k == 0, which, None, c_ready[n][h])
                    return c_ready[n][h]
                product(banks, h_hi, h_lo, h_ready, evac)

            def normed(which, h, g_name, tiles, to, *after):
                cols = slice(h * HALF, (h + 1) * HALF)
                t = inverse_root(banks, token_sums(banks, which, h), h, KQ * P, which)
                b, r, t = spread(banks, h, which, wide[:, h, 1, :], t, wide_free[h])
                ts = [V.do(lambda e, k=k: e.scalar_tensor_tensor(
                    out=to[:, k, cols], in0=x[:, tiles + k, cols], scalar=par(g_name, k), in1=r,
                    op0=ALU.mult, op1=ALU.mult), t, c_ready[tiles + k][h], *after) for k in range(KQ)]
                banks.release(b, ts[-1])
                wide_free[h] = ts[-1]
                return ts

            t_k = [None] * NH

            def evac_k(h, cols, bank, t):
                t_k[h] = S.do(lambda e: e.activation(k_idx[:, cols], bank, ACT.Copy), t)
                return t_k[h]
            queue_task(None, lambda: None)
            cq_t = [None] * NH
            kv_t = [None] * NH

            def cq_task(h):
                cq_t[h] = normed(0, h, "a_g_cq_2", 0, x)
                for k in range(KQ):
                    cols = slice(h * HALF, (h + 1) * HALF)
                    t = S.do(lambda e, k=k: e.activation(cq_hi[:, k, cols], x[:, k, cols], ACT.Copy), cq_t[h][k])
                    cq_ready[h].append(G.do(lambda e, k=k: e.tensor_tensor(
                        cq_lo[:, k, cols], x[:, k, cols], cq_hi[:, k, cols].bitcast(F32), ALU.subtract), t))

            def kv_task(h):
                kv_t[h] = normed(1, h, "a_g_ckv_2", KQ, ckv_t)
            cq_ready = [[], []]
            queue_task(None, lambda: cq_task(0))
            queue_task(None, lambda: cq_task(1))
            product(banks, h_hi, h_lo, h_ready, evac_k)
            while tasks:
                run_task()
            t_lo = []
            t_hi = S.do(lambda e: e.activation(wi_hi[:, :, :], wi[:, :, :], ACT.Copy), t_wi)
            t_wi = G.do(lambda e: e.tensor_tensor(wi_lo[:, :, :], wi[:, :, :], wi_hi[:, :, :].bitcast(F32), ALU.subtract), t_hi)
            b, bank = banks.take()
            PE.wait(t_wi)
            for i in range(NT):
                for k in range(KD):
                    for n, (hp, wp) in enumerate(((h_hi, wi_hi), (h_hi, wi_lo), (h_lo, wi_hi))):
                        first, end = k == 0 and n == 0, k == KD - 1 and n == 2
                        t = PE.do(lambda e, o=bank[:, 8 * i:8 * i + 8], l=hp[:, k, i * P:(i + 1) * P], r=wp[:, k, :], f=first, z=end:
                                  e.matmul(o, l, r, start=f, stop=z), mark=end)
            t_h_free = t
            w_scale = float(IDX_HEADS) ** -0.5 * float(IDX_DIM) ** -0.5
            t_widx = V.do(lambda e, bank=bank: e.tensor_scalar(w_idx[:, :, :].rearrange("p a b -> p (a b)"), bank[:, 0:NT * IDX_HEADS],
                                                               w_scale, None, ALU.mult), t)
            banks.release(b, t_widx)
            for line in (V, S, SP):
                line.wait(t_h_free)
            t_uk = dma("w_uk", w_uk[:, :, :], ins["a_w_uk_2"][0].rearrange("h d c -> d h c"))
            t_uv = dma("w_uv", w_uv[:, :, :, :].rearrange("p h k v -> p (h k) v"),
                       ins["a_w_uv_2"][0].rearrange("h (k p) v -> p (h k) v", p=P))
            for h in range(NH):
                kv_task(h)

            def bias_part(part):
                b, bank = banks.take()
                PE.wait(t_rel, t_hot)
                for n in range(64):
                    a = 2 * P - 1 - (64 * part + n)
                    t = PE.do(lambda e, o=bank[:, 8 * n:8 * n + 8], l=hot[:, a:a + P]:
                              e.matmul(o, l, rel[:, :], start=True, stop=True), mark=(n == 63))
                t_bias[0] = V.do(lambda e, o=bias[:, :, 64 * part:64 * part + 64].rearrange("p h s -> p s h"),
                                 i=bank.rearrange("p (s h) -> p s h", h=HEADS): e.tensor_copy(o, i), t)
                banks.release(b, t_bias[0])

            def turn_ckv(i):
                b, bank = banks.take()
                for u in range(2):
                    for k in range(KC):
                        c = (u * KC + k) * P
                        t = PE.do(lambda e, o=bank[:, c:c + P], s=ckv_t[:, k, (i + u) * P:(i + u + 1) * P]:
                                  e.transpose(o, s, ident[:, :]), kv_t[i // 4][k])
                t_tok[0] = S.do(lambda e, o=ckv_tok[:, i:i + 2, :].rearrange("p a b -> p (a b)"), s=bank:
                                e.activation(o, s, ACT.Copy), t)
                banks.release(b, t_tok[0])

            t_bias, t_tok = [None], [None]
            t_qi = [None]
            for n in range(IDX_HEADS * IDX_DIM // P):
                def evac(h, cols, bank, t, n=n):
                    t_qi[0] = V.do(lambda e: e.tensor_copy(q_idx[:, n, cols], bank), t)
                    return t_qi[0]
                product(banks, cq_hi, cq_lo, cq_ready, evac)
            for i in range(0, NT, 2):
                queue_task(None, lambda i=i: turn_ckv(i))
            for part in range(4):
                queue_task(None, lambda part=part: bias_part(part))
            t_q = [None]
            for hd in range(HEADS):
                def evac_q(h, cols, bank, t, hd=hd):
                    t_q[0] = V.do(lambda e: e.tensor_copy(q[:, hd, cols], bank), t)
                    return t_q[0]
                product(banks, cq_hi, cq_lo, cq_ready, evac_q)
            while tasks:
                run_task()
            change_rooms(everything())

            s_banks = Banks([(0, 1), (2, 3)])
            t_banks = Banks([(4,), (5,)], (4, P))
            o_banks = Banks([(6,)], (KC, P))
            y_banks = Banks([(7,)], (KC, P))
            used = {}
            keep_ready = [None, None]
            Q_SCALE = float(DH) ** -0.5

            def pick(i):
                n = P * (i + 1)
                room = keep[:, i % 2, :]

                def whole():
                    t = V.do(lambda e: e.tensor_copy(room[:, n - P:n], causal[:, :]), t_causal, used.get(("keep", i % 2)))
                    if n > P:
                        t = V.do(lambda e: e.memset(room[:, 0:n - P], 0.0))
                    keep_ready[i % 2] = t
                if n <= TOPK:
                    return [whole]
                last = [None]

                def score(hh):
                    rows = slice(64 * (hh % 2), 64 * (hh % 2) + 64)
                    b, flat = s_banks.take()
                    for a in range(0, n, HALF):
                        z = min(a + HALF, n)
                        t = PE.do(lambda e, o=flat[:, a:z], l=q_idx[rows, hh // 2, i * P:(i + 1) * P], r=k_idx[rows, a:z]:
                                  e.matmul(o, l, r, start=True, stop=True))
                    ends = []
                    for u, a in enumerate(range(0, n, HALF)):
                        z = min(a + HALF, n)
                        ta = S.do(lambda e, o=relu[:, u, 0:z - a], s=flat[:, a:z]: e.activation(o, s, ACT.Relu),
                                  t, used.get(("relu", u)))
                        wcol = w_idx[:, i, hh:hh + 1]
                        if hh == 0:
                            tv = V.do(lambda e, o=work[:, a:z], s=relu[:, u, 0:z - a]: e.tensor_scalar(o, s, wcol, None, ALU.mult),
                                      ta, used.get("work"))
                        else:
                            tv = V.do(lambda e, o=work[:, a:z], s=relu[:, u, 0:z - a]: e.scalar_tensor_tensor(
                                out=o, in0=s, scalar=wcol, in1=o, op0=ALU.mult, op1=ALU.add), ta, last[0])
                        used[("relu", u)] = tv
                        ends.append(tv)
                    s_banks.release(b, ta)
                    last[0] = ends

                def bound():
                    last[0] = V.do(lambda e: e.tensor_tensor(work[:, n - P:n], work[:, n - P:n], causal[:, :], ALU.add),
                                   last[0], t_causal)

                def take8():
                    t = V.do(lambda e: e.max(top8[:, :], work[:, 0:n]), last[0])
                    last[0] = V.do(lambda e: e.match_replace(work[:, 0:n], top8[:, :], work[:, 0:n], TAKEN), t)

                def finish():
                    t = V.do(lambda e: e.tensor_scalar(room[:, 0:n], work[:, 0:n], TAKEN / 2, MASKED, ALU.is_gt, ALU.mult),
                             last[0], used.get(("keep", i % 2)))
                    used["work"] = keep_ready[i % 2] = t
                steps = [lambda hh=hh: score(hh) for hh in range(IDX_HEADS)] + [bound]
                return steps + [take8] * (TOPK // 8) + [finish]

            order = [(i, hd) for i in range(NT) for hd in range(HEADS)]
            q_ready, p_ready, pt_ready, o_ready = {}, {}, {}, {}

            def latent_query(s):
                i, hd = order[s]
                b, bank = y_banks.take()
                PE.wait(t_uk)
                for ch in range(KC):
                    t = PE.do(lambda e, ch=ch: e.matmul(bank[:, ch, :], w_uk[:, hd, ch * P:(ch + 1) * P], q[:, hd, i * P:(i + 1) * P],
                                                        start=True, stop=True))
                q_ready[s] = S.do(lambda e: e.activation(q_lat[:, s % 2, :, :], bank, ACT.Copy, scale=Q_SCALE),
                                  t, used.get(("q_lat", s % 2)))
                y_banks.release(b, q_ready[s])

            def logits(s):
                i, hd = order[s]
                n = P * (i + 1)
                i2, h2, r3 = i % 2, s % 2, s % RING
                m = min(n, 2 * P)
                t_near = G.do(lambda e: e.tensor_tensor(near[:, h2, 0:m], keep[:, i2, n - m:n], bias[:, hd, 2 * P - m:2 * P], ALU.add),
                              keep_ready[i2], used.get(("near", h2)))
                b, flat = s_banks.take()
                PE.wait(q_ready[s])
                for a in range(0, n, HALF):
                    z = min(a + HALF, n)
                    for k in range(KC):
                        t = PE.do(lambda e, o=flat[:, a:z], l=q_lat[:, h2, k, :], r=ckv_t[:, k, a:z], f=(k == 0), z_=(k == KC - 1):
                                  e.matmul(o, l, r, start=f, stop=z_), mark=(k == KC - 1))
                used[("q_lat", h2)] = t
                row = prob[:, r3, :]
                tm = [V.do(lambda e: e.tensor_tensor_reduce(row[:, n - m:n], flat[:, n - m:n], near[:, h2, 0:m], 1.0, LOWEST,
                                                            ALU.add, ALU.max, stat[:, r3, 0:1]),
                           t, t_near, used.get(("prob", r3)))]
                used[("near", h2)] = tm[0]
                if n > m:
                    tm.append(V.do(lambda e: e.tensor_tensor_reduce(row[:, 0:n - m], flat[:, 0:n - m], keep[:, i2, 0:n - m], 1.0, LOWEST,
                                                                    ALU.add, ALU.max, stat[:, r3, 1:2])))
                    t = V.do(lambda e: e.tensor_scalar(stat[:, r3, 2:3], stat[:, r3, 0:1], stat[:, r3, 1:2], -1.0, ALU.max, ALU.mult), tm)
                else:
                    t = V.do(lambda e: e.tensor_scalar(stat[:, r3, 2:3], stat[:, r3, 0:1], -1.0, None, ALU.mult), tm)
                used[("keep", i2)] = tm[-1]
                s_banks.release(b, tm[-1])
                p_ready[s] = S.do(lambda e: e.activation(row[:, 0:n], row[:, 0:n], ACT.Exp, bias=stat[:, r3, 2:3], accum_out=stat[:, r3, 3:4]), t)

            def normalise(s):
                i, hd = order[s]
                n, r3 = P * (i + 1), s % RING
                row = prob[:, r3, :]
                t = V.do(lambda e: e.reciprocal(stat[:, r3, 4:5], stat[:, r3, 3:4]), p_ready[s])
                p_ready[s] = G.do(lambda e: e.tensor_scalar(row[:, 0:n], row[:, 0:n], stat[:, r3, 4:5], None, ALU.mult), t)

            def turn(s):
                i, hd = order[s]
                h2, r3 = s % 2, s % RING
                ends = []
                for a in range(0, i + 1, 4):
                    z = min(a + 4, i + 1)
                    b, bank = t_banks.take()
                    PE.wait(p_ready[s])
                    for j in range(a, z):
                        t = PE.do(lambda e, o=bank[:, j - a, :], s_=prob[:, r3, j * P:(j + 1) * P]: e.transpose(o, s_, ident[:, :]),
                                  mark=(j == z - 1))
                    te = S.do(lambda e, o=prob_t[:, h2, a:z, :], s_=bank[:, 0:z - a, :]: e.activation(o, s_, ACT.Copy),
                              t, used.get(("prob_t", h2)))
                    t_banks.release(b, te)
                    ends.append(te)
                used[("prob", r3)] = t
                pt_ready[s] = ends

            def gather(s):
                i, hd = order[s]
                h2 = s % 2
                b, bank = o_banks.take()
                PE.wait(pt_ready[s])
                for k in range(KC):
                    for j in range(i + 1):
                        t = PE.do(lambda e, o=bank[:, k, :], l=ckv_tok[:, j, k * P:(k + 1) * P], r=prob_t[:, h2, j, :], f=(j == 0), z=(j == i):
                                  e.matmul(o, l, r, start=f, stop=z), mark=(j == i))
                used[("prob_t", h2)] = t
                o_ready[s] = S.do(lambda e: e.activation(o_lat[:, h2, :, :], bank, ACT.Copy), t, used.get(("o_lat", h2)))
                o_banks.release(b, o_ready[s])

            def values(s):
                i, hd = order[s]
                h2 = s % 2
                b, bank = y_banks.take()
                PE.wait(o_ready[s], t_uv)
                for k in range(KC):
                    t = PE.do(lambda e, k=k: e.matmul(bank[:, 0, :], w_uv[:, hd, k, :], o_lat[:, h2, k, :],
                                                      start=(k == 0), stop=(k == KC - 1)), mark=(k == KC - 1))
                used[("o_lat", h2)] = t
                y_done[hd][i // 4] = S.do(lambda e: e.activation(x[:, hd, i * P:(i + 1) * P], bank[:, 0, :], ACT.Copy), t)
                y_banks.release(b, y_done[hd][i // 4])

            y_done = [[None] * NH for _ in range(HEADS)]
            for step in pick(0) + pick(1):
                step()
            latent_query(0)
            ahead = []
            for s in range(len(order) + 3):
                if s < len(order) and order[s][1] == 0:
                    assert not ahead
                    i = order[s][0]
                    ahead = pick(i + 1) if 1 <= i < NT - 1 else []
                    per = -(-len(ahead) // HEADS)
                part, ahead = ahead[:per], ahead[per:]
                if s >= 3:
                    values(s - 3)
                if s < len(order):
                    logits(s)
                for step in part[:per // 2]:
                    step()
                if s < len(order):
                    normalise(s)
                if 2 <= s < len(order) + 2:
                    gather(s - 2)
                if s + 1 < len(order):
                    latent_query(s + 1)
                if 1 <= s < len(order) + 1:
                    turn(s - 1)
                for step in part[per // 2:]:
                    step()

            y_ready = [[], []]
            change_rooms(PE.last)
            for k in range(KD):
                split_halves(h_hi[:, k, :], h_lo[:, k, :], x[:, k, :], y_ready, y_done[k])
                x_ready[k] = [dma(f"x{k}", x[:, k, :], x_park[:, k, :], y_ready[0][-1], y_ready[1][-1], t_park)]
            out_projection(banks, h_hi, h_lo, y_ready, 8 * KD, x_ready, (None,), everything())
            return gains(3 * KD, 10 * KD, "g_ffn_2", 0, V.last)

        FFN_GROUPS = [range(0, 6), range(6, 12), range(12, 17), range(17, KF)]

        def ffn_items():
            w_in, w_out = ins["f_w_in_2"][0], ins["f_w_out_2"][0]
            items = []
            for grp in FFN_GROUPS:
                for n in grp:
                    items += [item(w_in, n), item(w_in, KF + n)]
                items += [item(w_out[grp[0] * P:(grp[-1] + 1) * P, :], d) for d in range(KD)]
            return items

        def stage_ffn(t_gain):
            banks = Banks(all_banks)
            area = Area(STAGE_AT, NORM_AT - STAGE_AT)
            release = everything()
            h_ready = modulated_norm(banks, 3 * KD, 9 * KD, x_ready, t_gain)
            change_rooms(release)
            y_hi, y_lo = area.sb("f_hi", [P, 6, T], F32R), area.sb("f_lo", [P, 6, T], F32R)
            u_pad, cv, yv = area.sb("u_pad", [P, T + 2]), area.sb("f_cv", [P, T]), area.sb("f_yv", [P, T])
            t_edge = V.do(lambda e: e.memset(u_pad[:, 0:2], 0.0))
            y_free = u_free = cv_free = None
            yv_free = [None, None]
            for grp in FFN_GROUPS:
                y_ready = [[], []]
                for i, n in enumerate(grp):
                    tu, ty = [], []

                    def evac_u(h, cols, bank, t):
                        a = 2 + h * HALF
                        tu.append(S.do(lambda e: e.activation(u_pad[:, a:a + HALF], bank, ACT.Copy), t, u_free))
                        return tu[-1]
                    product(banks, h_hi, h_lo, h_ready, evac_u)
                    t0 = V.do(lambda e, n=n: e.tensor_scalar(cv[:, :], u_pad[:, 0:T], par("f_conv_w_2", n), None, ALU.mult),
                              tu, t_edge, cv_free)
                    for tap in (1, 2):
                        t0 = V.do(lambda e, n=n, tap=tap: e.scalar_tensor_tensor(
                            out=cv[:, :], in0=u_pad[:, tap:tap + T], scalar=par("f_conv_w_2", tap * KF + n),
                            in1=cv[:, :], op0=ALU.mult, op1=ALU.add), t0)
                    u_free = t0
                    tg = S.do(lambda e, n=n: e.activation(cv[:, :], cv[:, :], ACT.Gelu, bias=par("f_conv_b_2", n)), t0)

                    def evac_v(h, cols, bank, t):
                        ty.append(V.do(lambda e: e.tensor_tensor(yv[:, cols], bank, cv[:, cols], ALU.mult), t, tg, yv_free[h]))
                        return ty[-1]
                    product(banks, h_hi, h_lo, h_ready, evac_v)
                    cv_free = ty[-1]
                    S.wait(y_free)
                    split_halves(y_hi[:, i, :], y_lo[:, i, :], yv, y_ready, ty)
                    yv_free = [y_ready[0][-1], y_ready[1][-1]]
                out_projection(banks, y_hi, y_lo, y_ready, 11 * KD, x_ready, (None,) if grp is FFN_GROUPS[-1] else ())
                y_free = PE.last

        def stage_end():
            banks = Banks(all_banks)
            area = Area(H_AT, 4 * NT * D)
            o_rows = area.sb("o_rows", [P, NT, D])
            change_rooms(PE.last, x_ready)
            for h in range(NH):
                cols = slice(h * HALF, (h + 1) * HALF)
                ends = x_ready
                t = inverse_root(banks, token_sums(banks, 0, h), h, D, 0)
                b, r, t = spread(banks, h, 0, wide[:, h, 1, :], t, wide_free[h])
                ends = [V.do(lambda e, k=k, r=r, cols=cols: e.scalar_tensor_tensor(
                    out=x[:, k, cols], in0=x[:, k, cols], scalar=par("g_final_2", k), in1=r,
                    op0=ALU.mult, op1=ALU.mult), t, x_ready[k]) for k in range(KD)]
                banks.release(b, ends[-1])
                for i in range(4 * h, 4 * h + 4):
                    moved = []
                    for q in range(2):
                        b, bank = banks.take()
                        for k in range(4):
                            t = PE.do(lambda e, i=i, k=k, q=q, bank=bank: e.transpose(
                                bank[:, k * P:(k + 1) * P], x[:, 4 * q + k, i * P:(i + 1) * P], ident[:, :]),
                                ends[4 * q + k], mark=(k == 3))
                        dst = o_rows[:, i, 4 * q * P:(4 * q + 4) * P]
                        if q:
                            t = S.do(lambda e, dst=dst, bank=bank: e.activation(dst, bank, ACT.Copy), t)
                        else:
                            t = V.do(lambda e, dst=dst, bank=bank: e.tensor_copy(dst, bank), t)
                        banks.release(b, t)
                        moved.append(t)
                    t_out = dma("out", out[0, i * P:(i + 1) * P, :], o_rows[:, i, :], moved)
            SP.wait(t_out)

        w.items += conv_items()
        w.items += dilated_items()
        w.items += latent_items()
        w.items += ffn_items()
        t = stage_setup()
        t = stage_conv(t)
        stage_dilated(t)
        release = everything()
        h_ready = stage_between()
        t = stage_latent(release, h_ready)
        stage_ffn(t)
        stage_end()

        block = ctx.enter_context(nc.Block())

        @block.tensor
        def _(e):
            for step in PE.steps:
                step(e)

        @block.vector
        def _(e):
            for step in V.steps:
                step(e)

        @block.scalar
        def _(e):
            for step in S.steps:
                step(e)

        @block.gpsimd
        def _(e):
            for step in G.steps:
                step(e)

        @block.sync
        def _(e):
            for step in SP.steps:
                step(e)


_INS = ["x", "c", "norm_g", "w_mod", "b_mod", "conv_w_in", "conv_k", "conv_w_out", "dil_w_in", "dil_w_out",
        "final_g", "c_2", "rel_bias_2", "a_w_in_2", "a_g_cq_2", "a_g_ckv_2", "a_w_uq_2", "a_w_uk_2",
        "a_w_uv_2", "a_w_qi_2", "a_w_o_2", "ada_w_2", "ada_b_2", "g_mix_2", "g_ffn_2", "f_w_in_2",
        "f_conv_w_2", "f_conv_b_2", "f_w_out_2", "g_final_2"]


def kernel(**inputs):
    import concourse.bacc as bacc
    from concourse.bass_utils import run_bass_kernel_spmd

    nc = bacc.Bacc("TRN2", target_bir_lowering=False, num_devices=1)
    arrays = {f"in_{n}": np.ascontiguousarray(inputs[n]) for n in _INS}
    arrays.update({f"in_{n}": a for n, a in shape_constants().items()})
    aps = {n[3:]: nc.dram_tensor(n, a.shape, F32, kind="ExternalInput").ap() for n, a in arrays.items()}
    out = nc.dram_tensor("out_x", (1, T, D), F32, kind="ExternalOutput").ap()
    build(nc, aps, out)
    r = run_bass_kernel_spmd(nc, [arrays], core_ids=[0])
    return r.results[0]["out_x"]
```

```python
from contextlib import ExitStack

import numpy as np

import concourse.bass as bass
from concourse import mybir

P = 128
F32 = mybir.dt.float32
F32R = mybir.dt.float32r
ALU = mybir.AluOpType
ACT = mybir.ActivationFunctionType
AX = mybir.AxisListType

T = 1024
D = 1024
KD = D // P
NT = T // P
HALF = 512
NH = T // HALF
CONV_TAPS = 3
HEADS = 8
DH = D // HEADS
RATES = (1, 4, 16)
STRIDES = (1, 4, 8)
REACH = 64
Q_RANK = 256
KV_RANK = 256
IDX_HEADS = 8
IDX_DIM = 64
TOPK = 256
NUM_BUCKETS = 32
MAX_DISTANCE = 128
D_FF = 2816
KF = D_FF // P
EPS = 1e-6
MASKED = -1e30
TAKEN = -3e38
LOWEST = -3.4e38

PACK_A = [("c", KD), ("c_2", KD), ("norm_g", 2 * KD), ("final_g", KD), ("conv_k", CONV_TAPS * KD),
          ("b_mod", 2 * 3 * KD), ("g_mix_2", KD), ("g_ffn_2", KD)]
PACK_B = [("ada_b_2", 6 * KD), ("f_conv_w_2", CONV_TAPS * KF), ("g_final_2", KD),
          ("a_g_cq_2", Q_RANK // P), ("a_g_ckv_2", KV_RANK // P)]
PACK_C = [("f_conv_b_2", KF)]


def shape_constants():
    f = np.float32
    half = DH // 2
    inv = (f(10000.0) ** (-np.arange(0, DH, 2, dtype=f) / f(DH))).astype(f)
    angle = (np.arange(T, dtype=f)[:, None] * inv[None, :]).astype(f)
    cos, sin = np.cos(angle).astype(f).T, np.sin(angle).astype(f).T
    p = np.arange(P)[:, None]
    j = np.arange(3 * P)[None, :]
    band = np.where(np.abs(j - P - p) <= REACH, 0.0, MASKED).astype(f)
    k = np.arange(P)[None, :]
    pair = np.where(p % 2 == k % 2, 0.0, MASKED).astype(f)
    causal = np.where(k <= p, 0.0, MASKED).astype(f)
    dist = np.arange(-127, 256)
    n = np.maximum(dist, 0)
    exact = NUM_BUCKETS // 2
    ratio = np.log(np.maximum(n, 1).astype(f) / f(exact)) / f(np.log(MAX_DISTANCE / exact))
    large = exact + (ratio * f(NUM_BUCKETS - exact)).astype(np.int32)
    bucket = np.where(n < exact, n, np.minimum(large, NUM_BUCKETS - 1))
    assert (bucket[dist >= P] == NUM_BUCKETS - 1).all()
    hot = np.zeros((NUM_BUCKETS, dist.size + 1), f)
    hot[bucket, np.arange(dist.size)] = 1.0
    hot[NUM_BUCKETS - 1, :dist.size] -= 1.0
    hot[:, :dist.size][:, dist < 0] = 0.0
    return {
        "rope_cos": np.ascontiguousarray(np.concatenate([cos, cos], 0)),
        "rope_sin": np.ascontiguousarray(np.concatenate([-sin, sin], 0)),
        "band_mask": band, "pair_mask": pair, "causal_mask": causal,
        "bucket_hot": np.ascontiguousarray(hot[:, ::-1]), "identity": np.eye(P, dtype=f),
        "reversal": np.ascontiguousarray(np.eye(P, dtype=f)[::-1]),
    }


class Line:

    def __init__(self, name, sem):
        self.name, self.sem, self.count, self.steps, self.seen = name, sem, 0, [], {}

    def wait(self, *tokens):
        for token in tokens:
            if isinstance(token, list):
                self.wait(*token)
            elif token is not None:
                sem, value = token
                if self.seen.get(sem, 0) < value:
                    self.seen[sem] = value
                    self.steps.append(lambda e, s=sem, v=value: e.wait_ge(s, v))

    def do(self, emit, *after, mark=True):
        self.wait(*after)
        if not mark:
            self.steps.append(emit)
            return None
        self.count += 1
        self.steps.append(lambda e: emit(e).then_inc(self.sem, 1))
        return (self.sem, self.count)

    @property
    def last(self):
        return (self.sem, self.count) if self.count else None


class DmaSlot:

    def __init__(self, sem):
        self.sem, self.count = sem, 0


def build(nc, ins, out):
    ctx = ExitStack()
    with ctx:
        named = {}

        class Area:

            def __init__(self, start, size):
                self.at, self.end = start, start + size

            def sb(self, name, shape, dt=F32):
                size = 4 * int(np.prod(shape[1:]))
                assert self.at + size <= self.end, (name, self.at, size, self.end)
                named[name] = named.get(name, 0) + 1
                tile = nc.alloc_sbuf_tensor_at(f"{name}_{named[name]}", shape, dt, offset=self.at)
                self.at += -(-size // 32) * 32
                return tile

            def rest(self):
                return self.end - self.at

        def sem(name):
            return ctx.enter_context(nc.semaphore(name))

        PE, V, S, G = (Line(n, sem("done_" + n)) for n in ("pe", "dve", "act", "pool"))
        SP = Line("sp", sem("done_sp"))
        LINES = (PE, V, S, G, SP)
        slots = {}

        def dma(name, dst, src, *after):
            if name not in slots:
                slots[name] = DmaSlot(sem("dma_" + name))
            slot = slots[name]
            SP.wait(*after)
            slot.count += 16
            SP.steps.append(lambda e: e.dma_start(dst, src).then_inc(slot.sem, 16))
            return (slot.sem, slot.count)

        def everything():
            return [line.last for line in LINES] + [(s.sem, s.count) for s in slots.values()]

        def change_rooms(*after):
            for line in (V, S, G, SP):
                line.wait(*after)

        base = -(-nc.sbuf_base // 32) * 32
        whole = Area(base, nc.sbuf_usable_end - base)
        x = whole.sb("x", [P, KD, T])
        ident = whole.sb("ident", [P, P])
        ones = whole.sb("ones", [P, P])
        eps = whole.sb("eps", [P, 1])
        par_a = whole.sb("par_a", [P, P])
        par_b = whole.sb("par_b", [P, P])
        par_c = whole.sb("par_c", [P, sum(n for _, n in PACK_C)])
        silu_c = whole.sb("silu_c", [P, 2 * KD])
        mod = whole.sb("mod", [P, 12 * KD])
        gain = whole.sb("gain", [P, 4 * KD])
        factor = whole.sb("factor", [P, 3, NT])
        mod_acc = whole.sb("mod_acc", [P, 2, P])
        RAW, SPLIT = 3, 2
        w_raw = whole.sb("w_raw", [P, RAW, KD, P])
        w_hi = whole.sb("w_hi", [P, SPLIT, KD, P], F32R)
        w_lo = whole.sb("w_lo", [P, SPLIT, KD, P], F32R)
        H_AT = whole.at
        h_hi = whole.sb("h_hi", [P, KD, T], F32R)
        h_lo = whole.sb("h_lo", [P, KD, T], F32R)
        STAGE_AT, STAGE_SIZE = whole.at, whole.rest()
        NORM_SIZE = 4 * 4 * T
        NORM_AT = (STAGE_AT + STAGE_SIZE - NORM_SIZE) // 32 * 32
        norm_area = Area(NORM_AT, NORM_SIZE)
        acc = norm_area.sb("norm_acc", [P, 2, T])
        wide = norm_area.sb("norm_wide", [P, 4, HALF])
        x_park = nc.dram_tensor("x_park", (P, KD, T), F32).ap()
        bias_dram = nc.dram_tensor("bias_by_distance", (HEADS, 3 * P), F32)
        psum = ctx.enter_context(nc.psum_tensor("psum", [P, 8, HALF], F32))

        col = {}
        for tile, pack in ((par_a, PACK_A), (par_b, PACK_B), (par_c, PACK_C)):
            at = 0
            for name, rows in pack:
                col[name] = (tile, at, rows)
                at += rows

        def par(name, j):
            tile, a, _ = col[name]
            return tile[:, a + j:a + j + 1]

        bank_free = [None] * 8

        class Banks:

            def __init__(self, groups, shape=None):
                self.groups, self.shape, self.n = groups, shape, 0

            def take(self):
                group = self.groups[self.n % len(self.groups)]
                self.n += 1
                for b in group:
                    PE.wait(bank_free[b])
                tile = psum[:, group[0]:group[-1] + 1, :].rearrange("p a b -> p (a b)")
                if self.shape:
                    tile = tile[:, 0:self.shape[0] * self.shape[1]].rearrange("p (a b) -> p a b", a=self.shape[0])
                return group, tile

            def release(self, group, token):
                for b in group:
                    bank_free[b] = token

        class Weights:

            def __init__(self):
                self.items, self.room, self.hi, self.lo = [], w_raw, w_hi, w_lo
                self.raw_free, self.split_free = {}, [None] * SPLIT
                self.loaded, self.ready, self.taken, self.splits = {}, {}, 0, 0
                self.n_loaded = self.n_split = 0

            def load_next(self):
                n = self.n_loaded
                if n >= len(self.items) or (n >= RAW and n - RAW not in self.raw_free):
                    return False
                self.n_loaded += 1
                r = n % RAW
                parts, kt, _ = self.items[n]
                for a, b, src in parts:
                    self.loaded[n] = dma(f"w{r}", self.room[:, r, 0:kt, a:b], src, self.raw_free.get(n - RAW))
                return True

            def hand_on(self):
                n = self.n_split
                while n >= self.n_loaded:
                    assert self.load_next()
                self.n_split += 1
                r = n % RAW
                _, kt, split = self.items[n]
                if not split:
                    self.ready[n] = (None, r, self.loaded[n])
                    return
                s = self.splits % SPLIT
                self.splits += 1
                raw, hi, lo = self.room[:, r, 0:kt, :], self.hi[:, s, 0:kt, :], self.lo[:, s, 0:kt, :]
                t_hi = S.do(lambda e: e.activation(hi, raw, ACT.Copy), self.loaded[n], self.split_free[s])
                t_lo = G.do(lambda e: e.tensor_tensor(lo, raw, hi.bitcast(F32), ALU.subtract), t_hi)
                self.raw_free[n] = t_lo
                self.ready[n] = (s, r, t_lo)

            def take(self):
                n = self.taken
                self.taken += 1
                while self.n_split <= n:
                    self.hand_on()
                return (n,) + self.ready[n]

            def look_ahead(self):
                n = self.taken - 1
                while self.n_split < min(n + 3, len(self.items)) and not any(
                        self.items[m][2] for m in range(n + 1, self.n_split)):
                    self.hand_on()
                while self.load_next():
                    pass

        w = Weights()
        tasks = []

        def run_task():
            if tasks:
                tasks.pop(0)[1]()

        def queue_task(room, task):
            tasks.append((room, task))

        def drain(room):
            while any(name == room for name, _ in tasks):
                run_task()

        def passes(block, bank, a_hi, a_lo, a_ready, h, tiles):
            n, s, _, t_w = block
            kt = w.items[n][1]
            cols = slice(h * HALF, (h + 1) * HALF)
            PE.wait(t_w)
            for k in tiles:
                PE.wait(a_ready[h][k])
                for i, (wp, ap) in enumerate(((w.hi, a_hi), (w.hi, a_lo), (w.lo, a_hi))):
                    first, end = k == 0 and i == 0, k == kt - 1 and i == 2
                    t = PE.do(lambda e, l=wp[:, s, k, :], r=ap[:, k, cols], f=first, z=end:
                              e.matmul(bank, l, r, start=f, stop=z), mark=end)
            return t

        def product(banks, a_hi, a_lo, a_ready, evac):
            block = w.take()
            w.look_ahead()
            kt = w.items[block[0]][1]
            for h in range(NH):
                b, bank = banks.take()
                passes(block, bank, a_hi, a_lo, a_ready, h, range(kt // 2))
                run_task()
                t = passes(block, bank, a_hi, a_lo, a_ready, h, range(kt // 2, kt))
                banks.release(b, evac(h, slice(h * HALF, (h + 1) * HALF), bank, t))
                run_task()
            w.split_free[block[1]] = t

        def product_pair(banks, a_hi, a_lo, a_ready, evacs, late):
            blocks = [w.take() for _ in evacs]
            kt = w.items[blocks[0][0]][1]
            runs = [(h, n) for h in range(NH) for n in range(len(evacs))]
            got, ends = {}, {}
            if late:
                for h, n in runs:
                    got[h, n] = banks.take()
                    passes(blocks[n], got[h, n][1], a_hi, a_lo, a_ready, h, range(kt - 1))
            for h, n in runs:
                if not late:
                    got[h, n] = banks.take()
                ends[h, n] = passes(blocks[n], got[h, n][1], a_hi, a_lo, a_ready, h, range(kt - 1 if late else 0, kt))
            for n, evac in enumerate(evacs):
                w.split_free[blocks[n][1]] = ends[NH - 1, n]
                for h in range(NH):
                    b, bank = got[h, n]
                    banks.release(b, evac(h, slice(h * HALF, (h + 1) * HALF), bank, ends[h, n]))
                w.look_ahead()

        unfinished, acc_free = [], [None, None]

        def finish_modulation():
            if unfinished:
                unfinished.pop()()

        def modulation(banks, c_col, mod_col, bias_ap, line, own=None):
            if own:
                room, t_w = own
            else:
                n, _, r, t_w = w.take()
                w.look_ahead()
                room = w.room[:, r, :, :]
            if line is PE:
                b, bank = banks.take()
                PE.wait(t_w, t_silu[0])
                for k in range(KD):
                    t = PE.do(lambda e, k=k: e.matmul(bank[:, 0:1], room[:, k, :], silu_c[:, c_col + k:c_col + k + 1],
                                                      start=(k == 0), stop=(k == KD - 1)), mark=(k == KD - 1))
                if not own:
                    w.raw_free[n] = t
                banks.release(b, V.do(lambda e: e.tensor_tensor(mod[:, mod_col:mod_col + 1], bank[:, 0:1], bias_ap, ALU.add), t))
                return
            a = n_mods[0] % 2
            n_mods[0] += 1
            part = mod_acc[:, a, :]
            c_tiles = silu_c[:, c_col:c_col + KD].unsqueeze(2).to_broadcast([P, KD, P])
            t = line.do(lambda e: e.tensor_tensor(room, room, c_tiles, ALU.mult), t_w, t_silu[0])
            k = KD // 2
            while k > 1:
                t = line.do(lambda e, k=k: e.tensor_tensor(room[:, 0:k, :], room[:, 0:k, :], room[:, k:2 * k, :], ALU.add), t)
                k //= 2
            t = line.do(lambda e: e.tensor_tensor(part, room[:, 0, :], room[:, 1, :], ALU.add), t, acc_free[a])
            t_part = t
            if not own:
                w.raw_free[n] = t
            finish_modulation()

            def finish():
                b, bank = banks.take()
                t = acc_free[a] = PE.do(lambda e: e.matmul(bank[:, 0:1], part, ones[:, 0:1], start=True, stop=True), t_part)
                banks.release(b, V.do(lambda e: e.tensor_tensor(mod[:, mod_col:mod_col + 1], bank[:, 0:1], bias_ap, ALU.add), t))
            unfinished.append(finish)

        n_mods = [0]

        def gains(first, scale_col, g_name, g_first, *after):
            return V.do(lambda e: e.scalar_tensor_tensor(
                out=gain[:, first:first + KD], in0=mod[:, scale_col:scale_col + KD], scalar=1.0,
                in1=col[g_name][0][:, col[g_name][1] + g_first:col[g_name][1] + g_first + KD],
                op0=ALU.add, op1=ALU.mult), *after)

        acc_ready = [[None, None], [None, None]]
        wide_free, n_wide = [None] * 4, [0]

        def wide_room():
            i = n_wide[0] % 4
            n_wide[0] += 1
            return i, wide[:, i, :], wide_free[i]

        def add_squares(src, h, first, which=0, scale=None, *after):
            cols = slice(h * HALF, (h + 1) * HALF)
            kw = {} if scale is None else {"scale": scale}
            if first:
                acc_ready[which][h] = S.do(lambda e: e.activation(acc[:, which, cols], src, ACT.Square, **kw), *after)
                return
            i, sq, free = wide_room()
            t = S.do(lambda e: e.activation(sq, src, ACT.Square, **kw), *after, free)
            acc_ready[which][h] = wide_free[i] = V.do(
                lambda e: e.tensor_tensor(acc[:, which, cols], acc[:, which, cols], sq, ALU.add),
                t, acc_ready[which][h])

        def token_sums(banks, which, h):
            b, bank = banks.take()
            for j in range(4):
                a = h * HALF + j * P
                t = PE.do(lambda e, o=bank[:, j:j + 1], l=acc[:, which, a:a + P]: e.matmul(o, l, ones[:, 0:1], start=True, stop=True),
                          acc_ready[which][h], mark=(j == 3))
            return b, bank, t

        def inverse_root(banks, got, h, n_features, to):
            b, bank, t = got
            f = factor[:, to, 4 * h:4 * h + 4]
            t = S.do(lambda e: e.activation(f, bank[:, 0:4], ACT.Sqrt, bias=eps[:, 0:1], scale=1.0 / n_features), t)
            banks.release(b, t)
            return V.do(lambda e: e.reciprocal(f, f), t)

        def spread(banks, h, which, *after):
            f = factor[:, which, 4 * h:4 * h + 4].unsqueeze(2).to_broadcast([P, 4, P])
            eye = ident[:, :].unsqueeze(1).to_broadcast([P, 4, P])
            i, diag, free = wide_room()
            t = V.do(lambda e: e.tensor_tensor(diag.rearrange("p (a b) -> p a b", a=4), eye, f, ALU.mult), *after, free)
            b, bank = banks.take()
            t = wide_free[i] = PE.do(lambda e: e.matmul(bank, ones[:, :], diag, start=True, stop=True), t)
            return b, bank, t

        def norm_half(banks, h, gain_col, shift_col, x_ready, spread_factor, *after):
            cols = slice(h * HALF, (h + 1) * HALF)
            b, r, t_r = spread_factor
            ready = [None] * KD

            def low(k, i, xn, t_hi):
                shift = mod[:, shift_col + k:shift_col + k + 1]
                if k % 2:
                    t = G.do(lambda e: e.tensor_tensor(h_lo[:, k, cols], xn, h_hi[:, k, cols].bitcast(F32), ALU.subtract), t_hi)
                else:
                    t = V.do(lambda e: e.scalar_tensor_tensor(
                        out=h_lo[:, k, cols], in0=xn, scalar=shift, in1=h_hi[:, k, cols].bitcast(F32),
                        op0=ALU.add, op1=ALU.subtract), t_hi)
                ready[k] = wide_free[i] = t

            def high(k):
                i, xn, free = wide_room()
                shift = mod[:, shift_col + k:shift_col + k + 1]
                t = t_v = V.do(lambda e: e.scalar_tensor_tensor(
                    out=xn, in0=x[:, k, cols], scalar=gain[:, gain_col + k:gain_col + k + 1], in1=r,
                    op0=ALU.mult, op1=ALU.mult), t_r, free, x_ready[k], *after)
                if k % 2:
                    t = S.do(lambda e: e.activation(xn, xn, ACT.Identity, bias=shift), t)
                    t = S.do(lambda e: e.activation(h_hi[:, k, cols], xn, ACT.Copy), t)
                else:
                    t = S.do(lambda e: e.activation(h_hi[:, k, cols], xn, ACT.Identity, bias=shift), t)
                return (k, i, xn, t), t_v

            behind = None
            for k in range(KD):
                ahead, t_v = high(k)
                if behind:
                    low(*behind)
                behind = ahead
            low(*behind)
            banks.release(b, t_v)
            return ready

        def modulated_norm(banks, gain_col, shift_col, x_ready, *after):
            sums = [token_sums(banks, 0, h) for h in range(NH)]
            factors = [inverse_root(banks, sums[h], h, D, 0) for h in range(NH)]
            spreads = [spread(banks, h, 0, factors[h]) for h in range(NH)]
            return [norm_half(banks, h, gain_col, shift_col, x_ready, spreads[h], *after) for h in range(NH)]

        def split_halves(hi, lo, src, ready, after, line=None, halves=range(NH)):
            for h in halves:
                cols = slice(h * HALF, (h + 1) * HALF)
                t = S.do(lambda e, c=cols: e.activation(hi[:, c], src[:, c], ACT.Copy), after[h])
                ready[h].append((line or G).do(lambda e, c=cols: e.tensor_tensor(
                    lo[:, c], src[:, c], hi[:, c].bitcast(F32), ALU.subtract), t))

        def out_projection(banks, y_hi, y_lo, y_ready, gate_col, x_ready, squares=(), before_squares=(), pair=False, late=False):
            def evac_of(d):
                def evac(h, cols, bank, t):
                    t = V.do(lambda e: e.scalar_tensor_tensor(
                        out=x[:, d, cols], in0=bank, scalar=mod[:, gate_col + d:gate_col + d + 1],
                        in1=x[:, d, cols], op0=ALU.mult, op1=ALU.add), t, x_ready[d])
                    x_lasts[d][h] = t
                    for which, scale in enumerate(squares):
                        add_squares(x[:, d, cols], h, d == 0, which, scale and par(scale, d), t, *before_squares)
                    return t
                return evac
            if pair:
                product_pair(banks, y_hi, y_lo, y_ready, [evac_of(0), evac_of(1)], late)
            for d in range(2 if pair else 0, KD):
                product(banks, y_hi, y_lo, y_ready, evac_of(d))
            for d in range(KD):
                x_ready[d] = list(x_lasts[d])

        x_lasts = [[None, None] for _ in range(KD)]

        def block_of(w2d, n):
            return w2d.rearrange("(k p) n -> p k n", p=P)[:, :, n * P:(n + 1) * P]

        def item(w2d, n, split=True):
            src = block_of(w2d, n)
            return ([(0, P, src)], src.shape[1], split)

        w_mod, ada_w = ins["w_mod"], ins["ada_w_2"][0]
        x_ready = [[] for _ in range(KD)]
        t_silu = [None]
        all_banks = [(b,) for b in range(8)]

        def stage_setup():
            banks = Banks(all_banks)
            area = Area(H_AT, 4 * (3 * P + NT * D))
            x_rows = area.sb("x_rows", [P, NT, D])
            rows = area.sb("par_rows", [P, 3, P])
            t_id = dma("ident", ident[:, :], ins["identity"])
            t_par = []
            for p_i, pack in enumerate((PACK_A, PACK_B, PACK_C)):
                a = 0
                for name, n in pack:
                    flat = ins[name]
                    names = " ".join("abcd"[:len(flat.shape)])
                    flat = flat.rearrange(f"{names} -> ({names})") if len(flat.shape) > 1 else flat
                    t_par.append(dma("par", rows[a:a + n, p_i, :], flat.rearrange("(j p) -> j p", p=P)))
                    a += n
            own_area = Area(STAGE_AT, NORM_AT - STAGE_AT)
            own_rooms = [own_area.sb("w_own", [P, KD, P]) for _ in range(2 * KD)]

            def load_own(js):
                for j in js:
                    own.append((own_rooms[j][:, :, :], dma(f"own{j}", own_rooms[j][:, :, :], block_of(w_mod[0], j))))
            own = []
            load_own(range(0, 2))
            t_x = [dma(f"x{i}", x_rows[:, i, :], ins["x"][0, i * P:(i + 1) * P, :]) for i in range(NT)]
            load_own(range(2, 2 * KD))
            while w.load_next():
                pass
            t_ones = V.do(lambda e: e.memset(ones[:, :], 1.0))
            V.do(lambda e: e.memset(eps[:, :], EPS))
            for p_i, (tile, pack) in enumerate(((par_a, PACK_A), (par_b, PACK_B), (par_c, PACK_C))):
                n = sum(r for _, r in pack)
                b, bank = banks.take()
                t = PE.do(lambda e, n=n, p_i=p_i, bank=bank: e.transpose(bank[:, 0:n], rows[0:n, p_i, :], ident[0:n, 0:n]),
                          t_id, t_par[-1])
                t = V.do(lambda e, n=n, tile=tile, bank=bank: e.tensor_copy(tile[:, 0:n], bank[:, 0:n]), t)
                banks.release(b, t)
            t_silu[0] = S.do(lambda e: e.activation(silu_c[:, :], par_a[:, 0:2 * KD], ACT.Silu), t)
            PE.wait(t_ones)

            def turn_x(i):
                h = i // 4
                for q in range(2):
                    b, bank = banks.take()
                    PE.wait(t_x[i])
                    for k in range(4):
                        t = PE.do(lambda e, k=k, q=q, bank=bank: e.transpose(
                            bank[:, k * P:(k + 1) * P], x_rows[:, i, (4 * q + k) * P:(4 * q + k + 1) * P], ident[:, :]),
                            mark=(k == 3))
                    dst = x[:, 4 * q:4 * q + 4, i * P:(i + 1) * P]
                    src = bank.rearrange("p (k n) -> p k n", k=4)
                    t = S.do(lambda e, dst=dst, src=src: e.activation(dst, src, ACT.Copy), t)
                    banks.release(b, t)
                    for k in range(4):
                        got[h][4 * q + k].append(t)
                        x_ready[4 * q + k].append(t)
                if i % 4 == 3:
                    for k in range(KD):
                        add_squares(x[:, k, h * HALF:(h + 1) * HALF], h, k == 0, 0, None, got[h][k])

            got = [[[] for _ in range(KD)] for _ in range(NH)]
            for j in range(2 * KD):
                modulation(banks, 0, j, par("b_mod", j), (PE, V, PE, G, PE)[j % 5], own[j])
                if 2 <= j < 2 + NT:
                    turn_x(j - 2)
            finish_modulation()
            return gains(0, KD, "norm_g", 0, V.last)

        GROUP = 4

        def conv_items():
            w_in, w_out = ins["conv_w_in"][0], ins["conv_w_out"][0]
            items = []
            mods = [item(w_mod[0], j, False) for j in range(2 * KD, 3 * KD)] + [item(w_mod[1], j, False) for j in range(3 * KD)]
            for g in range(KD // GROUP):
                for e_ in range(GROUP * g, GROUP * (g + 1)):
                    c, xin, z, b = (item(w_in, KD * part + e_) for part in (1, 2, 3, 0))
                    items += [c, xin, mods.pop(0), mods.pop(0)] if e_ == 0 else [c, mods.pop(0), xin, mods.pop(0)]
                    items += [z, mods.pop(0), b, mods.pop(0)]
                items += [item(w_out[GROUP * g * P:GROUP * (g + 1) * P, :], d) for d in range(KD)]
            assert not mods
            return items

        def stage_conv(t_gain):
            banks = Banks(all_banks)
            area = Area(STAGE_AT, NORM_AT - STAGE_AT)
            y_hi, y_lo = area.sb("y_hi", [P, GROUP, T], F32R), area.sb("y_lo", [P, GROUP, T], F32R)
            c_sb, cv, zs = area.sb("c_sb", [P, T]), area.sb("cv", [P, T]), area.sb("zs", [P, T])
            t_pad, yv = area.sb("t_pad", [P, T + 2]), area.sb("yv", [P, T])
            change_rooms(x_ready, everything())
            w.hand_on()
            w.hand_on()
            h_ready = modulated_norm(banks, 0, 0, x_ready, t_gain)
            V.do(lambda e: e.memset(t_pad[:, 0:1], 0.0))
            t_edge = V.do(lambda e: e.memset(t_pad[:, T + 1:T + 2], 0.0))
            y_free = t_cfree = t_tfree = t_cvfree = None
            t_yfree = [None, None]
            todo = list(range(2 * KD, 6 * KD))

            def one_modulation():
                j = todo.pop(0)
                modulation(banks, 0, j, par("b_mod", j), V)

            for g in range(KD // GROUP):
                y_ready = [[], []]
                for e_ in range(GROUP * g, GROUP * (g + 1)):
                    tk, tc, tz, ty = [None] * NH, [None] * NH, [None] * NH, [None] * NH

                    def evac_c(h, cols, bank, t):
                        tc[h] = S.do(lambda e: e.activation(c_sb[:, cols], bank, ACT.Copy), t, t_cfree)
                        return tc[h]

                    def evac_x(h, cols, bank, t):
                        a = 1 + h * HALF
                        tk[h] = V.do(lambda e: e.tensor_tensor(t_pad[:, a:a + HALF], bank, c_sb[:, cols], ALU.mult),
                                     t, tc[h], t_tfree)
                        return tk[h]
                    if e_ == 0:
                        product_pair(banks, h_hi, h_lo, h_ready, [evac_c, evac_x], False)
                        one_modulation()
                    else:
                        product(banks, h_hi, h_lo, h_ready, evac_c)
                        one_modulation()
                        product(banks, h_hi, h_lo, h_ready, evac_x)
                    one_modulation()
                    t_cfree = tk[1]
                    t0 = V.do(lambda e, e_=e_: e.tensor_scalar(cv[:, :], t_pad[:, 0:T], par("conv_k", e_), None, ALU.mult),
                              tk, t_edge, t_cvfree)
                    for tap in (1, 2):
                        t0 = V.do(lambda e, e_=e_, tap=tap: e.scalar_tensor_tensor(
                            out=cv[:, :], in0=t_pad[:, tap:tap + T], scalar=par("conv_k", tap * KD + e_),
                            in1=cv[:, :], op0=ALU.mult, op1=ALU.add), t0)
                    t_tfree = t_cv = t0

                    def evac_z(h, cols, bank, t):
                        t1 = S.do(lambda e: e.activation(zs[:, cols], bank, ACT.Silu), t, t_cvfree)
                        tz[h] = V.do(lambda e: e.tensor_tensor(cv[:, cols], cv[:, cols], zs[:, cols], ALU.mult), t1, t_cv)
                        return t1
                    product(banks, h_hi, h_lo, h_ready, evac_z)
                    one_modulation()

                    def evac_b(h, cols, bank, t):
                        ty[h] = V.do(lambda e: e.tensor_tensor(yv[:, cols], bank, cv[:, cols], ALU.mult),
                                     t, tz[h], t_yfree)
                        return ty[h]
                    product(banks, h_hi, h_lo, h_ready, evac_b)
                    one_modulation()
                    t_cvfree = ty[1]
                    i = e_ - GROUP * g
                    S.wait(y_free)
                    split_halves(y_hi[:, i, :], y_lo[:, i, :], yv, y_ready, ty)
                    t_yfree = [y_ready[0][-1], y_ready[1][-1]]
                finish_modulation()
                V.wait(V.last)
                out_projection(banks, y_hi, y_lo, y_ready, 2 * KD, x_ready, (None,) if g else ())
                y_free = PE.last
            return gains(KD, 4 * KD, "norm_g", KD, V.last)

        def dilated_items():
            w_in, w_out = ins["dil_w_in"][0], ins["dil_w_out"][0]
            n_g, items = len(RATES), []
            for hd in range(HEADS):
                items += [item(w_in, 2 * n_g * HEADS + hd), item(w_in, (2 * n_g + 1) * HEADS + hd)]
                for g in range(n_g):
                    for n, block in enumerate((g * HEADS + hd, (n_g + g) * HEADS + hd)):
                        items += [item(w_in, block), item(ada_w, 6 * hd + 2 * g + n, False)]
            return items + [item(w_out, d) for d in range(KD)]

        def stage_dilated(t_gain):
            SCALE = float(DH) ** -0.5
            G_RATES = len(RATES)
            banks = Banks([(0,), (1,), (2,)])
            s_banks = Banks([(3,), (4,)], (2, 256))
            t_banks = Banks([(5,), (6,)], (4, P))
            o_banks = Banks([(7,)], (4, P))
            area = Area(STAGE_AT, STAGE_SIZE)
            release = everything()
            w.hand_on()
            wide_banks = Banks(all_banks)
            h_ready = modulated_norm(wide_banks, KD, 3 * KD, x_ready, t_gain)
            while w.load_next():
                pass
            change_rooms(release, h_ready[0], h_ready[1])
            t_park = dma("park", x_park, x[:, :, :], x_ready)
            cos, sin = area.sb("cos", [P, T]), area.sb("sin", [P, T])
            band, pair_m = area.sb("band", [P, 3 * P]), area.sb("pair_m", [P, P])
            dma("tables", cos[:, :], ins["rope_cos"])
            dma("tables", sin[:, :], ins["rope_sin"])
            dma("tables", band[:, :], ins["band_mask"])
            t_tab = dma("tables", pair_m[:, :], ins["pair_mask"])
            qk = area.sb("qk", [P, 2, 2, T])
            v_t = area.sb("v_t", [P, T])
            v_tok = [area.sb(f"v_tok{g}", [P, NT + (g == 0), P]) for g in range(G_RATES)]
            o_g = [area.sb(f"o_g{g}", [P, T]) for g in range(G_RATES)]
            l_g = [area.sb(f"l_g{g}", [P, T]) for g in range(G_RATES)]
            rot, swp = area.sb("rot", [P, HALF]), area.sb("swp", [P, HALF])
            prob = area.sb("prob", [P, 2, 2, 256])
            prob_t = area.sb("prob_t", [P, 2, 4, P])
            stat = area.sb("stat", [P, 2, 3, G_RATES * NT])
            used = {}
            y_done = [None] * HEADS

            def natural(ap, r):
                return ap.rearrange("p (i c) -> p i c", c=r)

            def rope_evac(dst, g, ready):
                r = STRIDES[g]

                def evac(h, cols, bank, t):
                    t1 = V.do(lambda e: e.tensor_tensor(rot[:, :], bank, cos[:, cols], ALU.mult), t, t_tab, used.get("rot"))
                    S.do(lambda e: e.activation(swp[0:DH // 2, :], bank[DH // 2:DH, :], ACT.Copy), t1, used.get("swp"))
                    t2 = S.do(lambda e: e.activation(swp[DH // 2:DH, :], bank[0:DH // 2, :], ACT.Copy))
                    t3 = V.do(lambda e: e.tensor_tensor(swp[:, :], swp[:, :], sin[:, cols], ALU.mult), t2)
                    per = HALF // r
                    to = dst.rearrange("p (c i) -> p i c", c=r)[:, h * per:(h + 1) * per, :]
                    t4 = V.do(lambda e: e.tensor_tensor(to, natural(rot[:, :], r), natural(swp[:, :], r), ALU.add), t3)
                    used["rot"] = used["swp"] = t4
                    ready.append(t4)
                    return t2
                return evac

            def tile_plan(g, t):
                if g == 0:
                    lo, hi = max(0, P * t - REACH), min(T, P * t + P + REACH)
                    off = lo - (P * t - REACH)
                    chunks = [(max(off, 0), P - off, t), (P, min(P, hi - P * t - REACH), t + 1)]
                    return lo, hi - lo, off, band[:, REACH + off:REACH + off + hi - lo], chunks
                if g == 1:
                    c, u = divmod(t, 2)
                    return 256 * c, 256, 0, band[:, P * (1 - u):P * (1 - u) + 256], [(0, P, 2 * c), (P, P, 2 * c + 1)]
                return P * t, P, 0, pair_m[:, :], [(0, P, t)]

            def turn_values(hd, t_v):
                plans = [[v_t[:, max(0, P * j - REACH):min(T, P * j + REACH)] for j in range(NT + 1)]]
                s4 = v_t[:, :].rearrange("p (i c) -> p c i", c=STRIDES[1])
                plans.append([s4[:, j // 2, P * (j % 2):P * (j % 2) + P] for j in range(NT)])
                s8 = v_t[:, :].rearrange("p (i c) -> p c i", c=STRIDES[2])
                plans.append([s8[:, j, :] for j in range(NT)])

                def turn(g, js):
                    b, bank = t_banks.take()
                    PE.wait(t_v)
                    t = None
                    for n, j in enumerate(js):
                        src = plans[g][j]
                        rows = src.free_size()
                        t = PE.do(lambda e, o=bank[0:rows, n, :], i=src: e.transpose(o, i, ident[:, :]), mark=True)
                    runs = []
                    for n, j in enumerate(js):
                        rows = plans[g][j].free_size()
                        if runs and runs[-1][2] == rows:
                            runs[-1][1] = n + 1
                        else:
                            runs.append([n, n + 1, rows])
                    for a, z, rows in runs:
                        te = S.do(lambda e, o=v_tok[g][0:rows, js[a]:js[a] + z - a, :], i=bank[0:rows, a:z, :]:
                                  e.activation(o, i, ACT.Copy), t, used.get(("v_tok", g)))
                    t_banks.release(b, te)
                    v_ready[g] = te
                    used["v_t"] = t

                turns = []
                for g in range(G_RATES):
                    n = len(plans[g])
                    todo = [list(range(a, min(a + 4, n))) for a in range(0, n, 4)]
                    turns += [lambda g=g, js=js: turn(g, js) for js in todo]
                held = []
                while tasks and tasks[-1][0] == "combine":
                    held.insert(0, tasks.pop())
                while len(held) > 6:
                    tasks.append(held.pop(0))
                while held or turns:
                    if held:
                        tasks.append(held.pop(0))
                    if turns:
                        queue_task("v_t", turns.pop(0))

            v_ready = [None] * G_RATES

            def attend(hd, g, q, k, qk_ready, qk_name):
                par_ = hd % 2
                keep = {}

                def scores(p):
                    b, bank = s_banks.take()
                    PE.wait(qk_ready)
                    i = p % 2
                    room = prob[:, i, :, :]
                    ts = []
                    for u in range(2):
                        t = 2 * p + u
                        lo, n, off, mask, _ = tile_plan(g, t)
                        tt = PE.do(lambda e, o=bank[:, u, off:off + n], l=q[:, P * t:P * t + P], r=k[:, lo:lo + n]:
                                   e.matmul(o, l, r, start=True, stop=True))
                    for u in range(2):
                        t = 2 * p + u
                        lo, n, off, mask, _ = tile_plan(g, t)
                        c = g * NT + t
                        ts.append(V.do(lambda e, o=room[:, u, off:off + n], a=bank[:, u, off:off + n], m=mask, c=c:
                                       e.tensor_tensor_reduce(o, a, m, 1.0, LOWEST, ALU.add, ALU.max, stat[:, par_, 0, c:c + 1]),
                                       tt, used.get(("prob", i)), used.get(("stat", par_))))
                    used[qk_name] = tt
                    s_banks.release(b, ts[-1])
                    c = g * NT + 2 * p
                    t1 = V.do(lambda e: e.tensor_scalar(stat[:, par_, 1, c:c + 2], stat[:, par_, 0, c:c + 2], -SCALE, None, ALU.mult), ts)
                    te = []
                    for u in range(2):
                        _, n, off, _, _ = tile_plan(g, 2 * p + u)
                        te.append(S.do(lambda e, a=room[:, u, off:off + n], c=c + u: e.activation(
                            a, a, ACT.Exp, bias=stat[:, par_, 1, c:c + 1], scale=SCALE, accum_out=stat[:, par_, 2, c:c + 1]), t1))
                    t2 = V.do(lambda e: e.reciprocal(stat[:, par_, 1, c:c + 2], stat[:, par_, 2, c:c + 2]), te)
                    for u in range(2):
                        _, n, off, _, _ = tile_plan(g, 2 * p + u)
                        t3 = V.do(lambda e, a=room[:, u, off:off + n], c=c + u: e.tensor_scalar(
                            a, a, stat[:, par_, 1, c:c + 1], None, ALU.mult), t2)
                    keep[p] = [t3, None]

                def turn(p):
                    b, bank = t_banks.take()
                    i = p % 2
                    PE.wait(keep[p][0])
                    slots_ = []
                    n_ = 0
                    for u in range(2):
                        for (a, n, ch) in tile_plan(g, 2 * p + u)[4]:
                            tt = PE.do(lambda e, o=bank[0:n, n_, :], s=prob[:, i, u, a:a + n]: e.transpose(o, s, ident[:, :]))
                            slots_.append((u, n_, n, ch))
                            n_ += 1
                    used[("prob", i)] = tt
                    runs = []
                    for (_, s_, n, _) in slots_:
                        if runs and runs[-1][2] == n:
                            runs[-1][1] = s_ + 1
                        else:
                            runs.append([s_, s_ + 1, n])
                    for a, z, n in runs:
                        te = S.do(lambda e, o=prob_t[0:n, i, a:z, :], s=bank[0:n, a:z, :]: e.activation(o, s, ACT.Copy),
                                  tt, used.get(("prob_t", i)))
                    t_banks.release(b, te)
                    keep[p] = [te, slots_]

                def values(p):
                    i = p % 2
                    if i == 0:
                        keep["o"] = o_banks.take()
                    b, bank = keep["o"]
                    te, slots_ = keep[p]
                    PE.wait(te, v_ready[g])
                    for n_, (u, s_, n, ch) in enumerate(slots_):
                        first = n_ == 0 or slots_[n_ - 1][0] != u
                        last = n_ == len(slots_) - 1 or slots_[n_ + 1][0] != u
                        tt = PE.do(lambda e, o=bank[:, 2 * i + u, :], l=v_tok[g][0:n, ch, :], r=prob_t[0:n, i, s_, :], f=first, z=last:
                                   e.matmul(o, l, r, start=f, stop=z))
                    used[("prob_t", i)] = used[("v_tok", g)] = tt
                    if i == 1:
                        r = STRIDES[g]
                        half = p // 2
                        src = bank.rearrange("p a b -> p (a b)")
                        if r == 1:
                            src, to = src, o_g[g][:, half * HALF:(half + 1) * HALF]
                        else:
                            src = src.rearrange("p (c i) -> p c i", i=T // r)
                            to = o_g[g][:, :].rearrange("p (i c) -> p c i", c=r)[:, half * r // 2:(half + 1) * r // 2, :]
                        t = S.do(lambda e: e.activation(to, src, ACT.Copy), tt, used.get(("o_g", g)))
                        o_banks.release(b, t)
                        o_ready[g] = t

                queue_task(qk_name, lambda: scores(0))
                queue_task(qk_name, lambda: scores(1))
                queue_task(qk_name, lambda: (turn(0), scores(2)))
                queue_task(qk_name, lambda: (turn(1), scores(3)))
                queue_task(None, lambda: (values(0), turn(2)))
                queue_task(None, lambda: (values(1), turn(3)))
                queue_task(None, lambda: values(2))
                queue_task(None, lambda: values(3))

            o_ready = [None] * G_RATES

            def combine(hd):
                par_ = hd % 2
                l_ready = [[None] * NH for _ in range(G_RATES)]

                eye = ident[:, :].unsqueeze(1).to_broadcast([P, 4, P])
                t_diag = [None] * (G_RATES * NH)

                def diagonal(n):
                    c = 4 * n
                    lse = stat[:, par_, 1, c:c + 4].unsqueeze(2).to_broadcast([P, 4, P])
                    room = prob[:, n % 2, :, :].rearrange("p a (b c) -> p (a b) c", c=P)
                    t_diag[n] = used[("stat", par_)] = used[("lse", par_)] = G.do(
                        lambda e: e.tensor_tensor(room, eye, lse, ALU.mult), t_lse[0], used.get(("prob", n % 2)))

                def spread(n):
                    g, half = divmod(n, NH)
                    b, bank = t_banks.take()
                    flat = bank.rearrange("p a b -> p (a b)")
                    room = prob[:, n % 2, :, :].rearrange("p a b -> p (a b)")
                    tt = used[("prob", n % 2)] = PE.do(lambda e: e.matmul(flat, ones[:, :], room, start=True, stop=True), t_diag[n])
                    if n + 2 < G_RATES * NH:
                        diagonal(n + 2)
                    r = STRIDES[g]
                    if r == 1:
                        src, to = flat, l_g[g][:, half * HALF:(half + 1) * HALF]
                    else:
                        src = flat.rearrange("p (c i) -> p c i", i=T // r)
                        to = l_g[g][:, :].rearrange("p (i c) -> p c i", c=r)[:, half * r // 2:(half + 1) * r // 2, :]
                    t = S.do(lambda e: e.activation(to, src, ACT.Copy), tt, used.get(("l_g", g)))
                    t_banks.release(b, t)
                    l_ready[g][half] = t

                t_lse = [None]

                def start():
                    t = S.do(lambda e: e.activation(stat[:, par_, 1, :], stat[:, par_, 2, :], ACT.Ln), used.get(("lse", par_)), o_ready)
                    t_lse[0] = V.do(lambda e: e.scalar_tensor_tensor(
                        out=stat[:, par_, 1, :], in0=stat[:, par_, 0, :], scalar=SCALE, in1=stat[:, par_, 1, :],
                        op0=ALU.mult, op1=ALU.add), t)
                    diagonal(0)
                    diagonal(1)

                t_sub, t_exp, t_sum, t_o = {}, {}, {}, {}
                halves = [slice(half * HALF, (half + 1) * HALF) for half in range(NH)]

                def less_maximum(half):
                    for cols in (halves[half],):
                        L = [l[:, cols] for l in l_g]
                        mx = rot[:, :]
                        t = V.do(lambda e, L=L: e.tensor_tensor(mx, L[0], L[1], ALU.max), l_ready, used.get("rot"))
                        t = V.do(lambda e, L=L: e.tensor_tensor(mx, mx, L[2], ALU.max), t)
                        for g in range(G_RATES):
                            used["rot"] = t_sub[half, g] = V.do(lambda e, l=L[g]: e.tensor_tensor(l, l, mx, ALU.subtract), t)

                def weigh(half):
                    for cols in (halves[half],):
                        L, O = [l[:, cols] for l in l_g], [o[:, cols] for o in o_g]
                        for g in range(G_RATES):
                            te = S.do(lambda e, l=L[g]: e.activation(l, l, ACT.Exp), t_sub[half, g])
                            t_exp[g] = V.do(lambda e, o=O[g], l=L[g]: e.tensor_tensor(o, o, l, ALU.mult), te, o_ready[g])
                        t = V.do(lambda e, L=L: e.tensor_tensor(L[0], L[0], L[1], ALU.add), te, t_exp[0])
                        t_sum[half] = V.do(lambda e, L=L: e.tensor_tensor(L[0], L[0], L[2], ALU.add), t)
                        t = V.do(lambda e, O=O: e.tensor_tensor(O[0], O[0], O[1], ALU.add), t_exp[1])
                        t_o[half] = V.do(lambda e, O=O: e.tensor_tensor(O[0], O[0], O[2], ALU.add), t, t_exp[2])

                t_r = []

                def invert():
                    total = l_g[0][:, :]
                    t = S.do(lambda e: e.activation(total, total, ACT.Ln), t_sum[0], t_sum[1])
                    t_r.append(S.do(lambda e: e.activation(total, total, ACT.Exp, scale=-1.0), t))

                def gate():
                    for half, cols in enumerate(halves):
                        l, o, y = l_g[0][:, cols], o_g[0][:, cols], x[:, hd, cols]
                        t = V.do(lambda e, l=l, o=o: e.tensor_tensor(o, o, l, ALU.mult), t_r, t_o[half])
                        t = V.do(lambda e, y=y, o=o: e.tensor_tensor(y, o, y, ALU.mult), t, z_ready[hd])
                    for g in range(G_RATES):
                        used[("l_g", g)] = used[("o_g", g)] = t
                    y_done[hd] = t

                last_task = tasks.pop()
                queue_task(last_task[0], lambda: (last_task[1](), start()))
                for n in range(0, G_RATES * NH, 2):
                    queue_task("combine", lambda n=n: (spread(n), spread(n + 1)))
                for half in range(NH):
                    queue_task("combine", lambda half=half: less_maximum(half))
                for half in range(NH):
                    queue_task("combine", lambda half=half: weigh(half))
                queue_task("combine", invert)
                queue_task("combine", gate)

            z_ready = [None] * HEADS
            for hd in range(HEADS):
                tv = []
                drain("v_t")

                def evac_v(h, cols, bank, t):
                    tv.append(S.do(lambda e: e.activation(v_t[:, cols], bank, ACT.Copy), t, used.get("v_t")))
                    return tv[-1]

                def evac_z(h, cols, bank, t, hd=hd):
                    z_ready[hd] = S.do(lambda e: e.activation(x[:, hd, cols], bank, ACT.Silu), t, t_park)
                    return z_ready[hd]
                if hd == 0:
                    product_pair(wide_banks, h_hi, h_lo, h_ready, [evac_v, evac_z], False)
                    turn_values(hd, tv)
                else:
                    product(banks, h_hi, h_lo, h_ready, evac_v)
                    turn_values(hd, tv)
                    product(banks, h_hi, h_lo, h_ready, evac_z)
                for g in range(G_RATES):
                    which = (hd * G_RATES + g) % 2
                    name = ("qk", which)
                    ready = []
                    drain(name)
                    for n in range(2):
                        dst = qk[:, which, n, :]
                        wait_for = name
                        ev = rope_evac(dst, g, ready)

                        def evac(h, cols, bank, t, ev=ev, wait_for=wait_for):
                            V.wait(used.get(wait_for))
                            return ev(h, cols, bank, t)
                        product(banks, h_hi, h_lo, h_ready, evac)
                        run_task()
                        j = 6 * hd + 2 * g + n
                        modulation(banks, KD, 6 * KD + j, par("ada_b_2", j), G)
                    attend(hd, g, qk[:, which, 0, :], qk[:, which, 1, :], ready, name)
                combine(hd)
            finish_modulation()
            V.wait(V.last)
            y_ready = [[], []]
            t_h_free = PE.last
            todo = list(range(KD))
            w.hand_on()
            S.wait(t_h_free)

            def split_y():
                k = todo.pop(0)
                split_halves(h_hi[:, k, :], h_lo[:, k, :], x[:, k, :], y_ready, [y_done[k]] * NH, G if todo else V)
                x_ready[k] = [dma(f"x{k}", x[:, k, :], x_park[:, k, :], y_ready[0][-1], y_ready[1][-1], t_park)]
            while tasks:
                run_task()
                if len(todo) > 1 and y_done[todo[0]]:
                    split_y()
            while todo:
                split_y()
            out_projection(Banks(all_banks), h_hi, h_lo, y_ready, 5 * KD, x_ready, (None, "final_g"), everything(), pair=True, late=True)


        def stage_between():
            banks = Banks(all_banks)
            t_gain = gains(2 * KD, 7 * KD, "g_mix_2", 0, V.last)
            g_all = col["final_g"][0][:, col["final_g"][1]:col["final_g"][1] + KD]
            t_gain = V.do(lambda e: e.tensor_tensor(gain[:, 2 * KD:3 * KD], gain[:, 2 * KD:3 * KD], g_all, ALU.mult), t_gain)
            w.hand_on()
            sums = [[token_sums(banks, which, h) for which in range(2)] for h in range(NH)]

            def second_factor(h, t_r):
                f0, f1, f2 = (factor[:, i, 4 * h:4 * h + 4] for i in range(3))
                b, bank, t = sums[h][1]
                t = V.do(lambda e: e.tensor_tensor(f1, bank[:, 0:4], f0, ALU.mult), t, t_r)
                banks.release(b, t)
                t = V.do(lambda e: e.tensor_tensor(f1, f1, f0, ALU.mult), t)
                t = S.do(lambda e: e.activation(f1, f1, ACT.Sqrt, bias=eps[:, 0:1], scale=1.0 / D), t)
                t = V.do(lambda e: e.reciprocal(f1, f1), t)
                return V.do(lambda e: e.tensor_tensor(f2, f1, f0, ALU.mult), t)

            def first_norm(h, spread_factor):
                cols = slice(h * HALF, (h + 1) * HALF)
                b, r, t = spread_factor
                for k in range(KD):
                    t_x = V.do(lambda e, k=k: e.scalar_tensor_tensor(
                        out=x[:, k, cols], in0=x[:, k, cols], scalar=par("final_g", k), in1=r,
                        op0=ALU.mult, op1=ALU.mult), t, x_ready[k], h_ready[h])
                    ends[k].append(t_x)
                banks.release(b, t_x)

            ends = [[] for _ in range(KD)]
            t_r = [inverse_root(banks, sums[h][0], h, D, 0) for h in range(NH)]
            t_f = [second_factor(h, t_r[h]) for h in range(NH)]
            spreads = [spread(banks, h, 2, t_f[h]) for h in range(NH)]
            spreads_r = [spread(banks, h, 0, t_r[h]) for h in range(NH)]
            h_ready = [norm_half(banks, h, 2 * KD, 6 * KD, x_ready, spreads[h], t_gain) for h in range(NH)]
            for h in range(NH):
                first_norm(h, spreads_r[h])
            for k in range(KD):
                x_ready[k] = ends[k]
            return h_ready

        KQ, KC = Q_RANK // P, KV_RANK // P
        I_KIDX, I_WIDX = Q_RANK + KV_RANK, Q_RANK + KV_RANK + IDX_DIM

        def latent_items():
            w_in = ins["a_w_in_2"][0]
            kcols = w_in.rearrange("(k p) n -> p k n", p=P)[:, :, I_KIDX:I_WIDX]
            return ([item(w_in, n) for n in range(KQ + KC)] + [([(0, IDX_DIM, kcols), (IDX_DIM, P, kcols)], KD, True)] +
                    [item(ins["a_w_qi_2"][0], n) for n in range(IDX_HEADS * IDX_DIM // P)] +
                    [item(ins["a_w_uq_2"][0], n) for n in range(HEADS)] +
                    [item(ins["a_w_o_2"][0], d) for d in range(KD)])

        def stage_latent(release, h_ready):
            w_in = ins["a_w_in_2"][0]
            banks = Banks(all_banks)
            area = Area(STAGE_AT, STAGE_SIZE)
            ckv_t = area.sb("ckv_t", [P, KC, T])
            ckv_tok = area.sb("ckv_tok", [P, NT, KV_RANK])
            k_idx = area.sb("k_idx", [P, T])
            w_idx = area.sb("w_idx", [P, NT, IDX_HEADS])
            q_idx = area.sb("q_idx", [P, IDX_HEADS * IDX_DIM // P, T])
            c_raw = q_idx
            bias = area.sb("bias", [P, HEADS, 2 * P])
            causal = area.sb("causal", [P, P])
            top8 = area.sb("top8", [P, 8])
            early = Area(area.at, NORM_AT - area.at)
            cq_hi, cq_lo = early.sb("cq_hi", [P, KQ, T], F32R), early.sb("cq_lo", [P, KQ, T], F32R)
            wi = early.sb("wi", [P, KD, IDX_HEADS])
            wi_hi, wi_lo = early.sb("wi_hi", [P, KD, IDX_HEADS], F32R), early.sb("wi_lo", [P, KD, IDX_HEADS], F32R)
            rel = early.sb("rel", [NUM_BUCKETS, IDX_HEADS])
            late = Area(area.at, NORM_AT - area.at)
            near = late.sb("near", [P, 2, 2 * P])
            RING = 3
            prob = late.sb("prob", [P, RING, T])
            o_lat = late.sb("o_lat", [P, 2, KC, P])
            q_lat = late.sb("q_lat", [P, 2, KC, P])
            stat = late.sb("stat", [P, RING, 5])
            in_h = Area(H_AT, STAGE_AT - H_AT)
            q = in_h.sb("q", [P, HEADS, T])
            w_uk, w_uv = in_h.sb("w_uk", [P, HEADS, KV_RANK]), in_h.sb("w_uv", [P, HEADS, KC, P])
            work = in_h.sb("work", [P, 2, T])
            prob_t = in_h.sb("prob_t", [P, 2, NT, P])
            KEEP = 3
            in_norm = Area(NORM_AT, NORM_SIZE)
            keep = in_norm.sb("keep", [P, KEEP, T])
            relu = in_norm.sb("relu", [P, 2, HALF])
            w_idx_t, hot, bias_rows, flip = x[:, KQ + KC, :], x[:, KQ + KC + 1, 0:3 * P], x[:, KQ + KC + 1, 3 * P:6 * P], x[:, KQ + KC + 1, 6 * P:7 * P]
            bias_flipped = x[:, KQ + KC + 2:KQ + KC + 4, :].rearrange("p a b -> p (a b)")

            change_rooms(release, h_ready[0], h_ready[1])
            t_park, t_rel, t_hot = [], [], []

            def park():
                t_park.append(dma("park", x_park, x[:, :, :], x_ready))

            def load_tables():
                t_rel.append(dma("rel", rel[:, :], ins["rel_bias_2"], t_park))
                dma("hot", flip, ins["reversal"])
                t_hot.append(dma("hot", hot[0:NUM_BUCKETS, :], ins["bucket_hot"]))
            queue_task(None, load_tables)
            t_wi = dma("wi", wi[:, :, :], w_in.rearrange("(k p) n -> p k n", p=P)[:, :, I_WIDX:I_WIDX + IDX_HEADS])
            t_causal = dma("causal", causal[:, :], ins["causal_mask"])

            c_ready = [[None] * NH for _ in range(KQ + KC)]

            def evac_of(n):
                which, k = divmod(n, KQ)

                def evac(h, cols, bank, t):
                    c_ready[n][h] = S.do(lambda e: e.activation(c_raw[:, n, cols], bank, ACT.Copy), t)
                    add_squares(c_raw[:, n, cols], h, k == 0, which, None, c_ready[n][h])
                    return c_ready[n][h]
                return evac
            while w.load_next():
                pass
            park()
            product_pair(banks, h_hi, h_lo, h_ready, [evac_of(0), evac_of(1)], False)
            for n in range(2, KQ + KC):
                product(banks, h_hi, h_lo, h_ready, evac_of(n))

            def normed(which, h, g_name, tiles, to, *after):
                cols = slice(h * HALF, (h + 1) * HALF)
                t = inverse_root(banks, token_sums(banks, which, h), h, KQ * P, which)
                b, r, t = spread(banks, h, which, t)
                ts = [V.do(lambda e, k=k: e.scalar_tensor_tensor(
                    out=to[:, k, cols], in0=c_raw[:, tiles + k, cols], scalar=par(g_name, k), in1=r,
                    op0=ALU.mult, op1=ALU.mult), t, c_ready[tiles + k][h], *after) for k in range(KQ)]
                banks.release(b, ts[-1])
                return ts

            t_k = [None] * NH

            def evac_k(h, cols, bank, t):
                t_k[h] = S.do(lambda e: e.activation(k_idx[:, cols], bank, ACT.Copy), t)
                return t_k[h]
            cq_t = [None] * NH
            kv_t = [None] * NH

            def cq_task(h):
                cq_t[h] = normed(0, h, "a_g_cq_2", 0, c_raw)
                for k in range(KQ):
                    cols = slice(h * HALF, (h + 1) * HALF)
                    t = S.do(lambda e, k=k: e.activation(cq_hi[:, k, cols], c_raw[:, k, cols], ACT.Copy), cq_t[h][k])
                    cq_ready[h].append(G.do(lambda e, k=k: e.tensor_tensor(
                        cq_lo[:, k, cols], c_raw[:, k, cols], cq_hi[:, k, cols].bitcast(F32), ALU.subtract), t))

            def kv_task(h):
                kv_t[h] = normed(1, h, "a_g_ckv_2", KQ, ckv_t)
            cq_ready = [[], []]
            queue_task(None, lambda: cq_task(0))
            queue_task(None, lambda: cq_task(1))
            product(banks, h_hi, h_lo, h_ready, evac_k)
            while tasks:
                run_task()
            t_lo = []
            t_hi = S.do(lambda e: e.activation(wi_hi[:, :, :], wi[:, :, :], ACT.Copy), t_wi)
            t_wi = G.do(lambda e: e.tensor_tensor(wi_lo[:, :, :], wi[:, :, :], wi_hi[:, :, :].bitcast(F32), ALU.subtract), t_hi)
            t_wt = []
            for h in range(NH):
                cols = slice(h * HALF, (h + 1) * HALF)
                b, bank = banks.take()
                PE.wait(t_wi)
                for k in range(KD):
                    for n, (hp, wp) in enumerate(((h_hi, wi_hi), (h_hi, wi_lo), (h_lo, wi_hi))):
                        first, end = k == 0 and n == 0, k == KD - 1 and n == 2
                        t = PE.do(lambda e, o=bank[0:IDX_HEADS, :], l=wp[:, k, :], r=hp[:, k, cols], f=first, z=end:
                                  e.matmul(o, l, r, start=f, stop=z), mark=end)
                t_wt.append(S.do(lambda e, o=w_idx_t[0:IDX_HEADS, cols], s=bank[0:IDX_HEADS, :]: e.activation(o, s, ACT.Copy), t))
                banks.release(b, t_wt[-1])
            t_h_free = t
            w_scale = float(IDX_HEADS) ** -0.5 * float(IDX_DIM) ** -0.5

            def turn_w_idx():
                b, bank = banks.take()
                for i in range(NT):
                    t = PE.do(lambda e, i=i: e.transpose(bank[:, 8 * i:8 * i + 8], w_idx_t[0:IDX_HEADS, i * P:(i + 1) * P],
                                                         ident[0:IDX_HEADS, 0:IDX_HEADS]), t_wt)
                banks.release(b, V.do(lambda e: e.tensor_scalar(
                    w_idx[:, :, :].rearrange("p a b -> p (a b)"), bank[:, 0:NT * IDX_HEADS], w_scale, None, ALU.mult), t))
            for line in (V, S, SP):
                line.wait(t_h_free)
            t_uk = dma("w_uk", w_uk[:, :, :], ins["a_w_uk_2"][0].rearrange("h d c -> d h c"))
            t_uv = dma("w_uv", w_uv[:, :, :, :].rearrange("p h k v -> p (h k) v"),
                       ins["a_w_uv_2"][0].rearrange("h (k p) v -> p (h k) v", p=P))
            for h in range(NH):
                kv_task(h)

            def bias_by_distance():
                b, bank = banks.take()
                t = PE.do(lambda e: e.matmul(bank[0:HEADS, 0:3 * P], rel[:, :], hot[0:NUM_BUCKETS, :], start=True, stop=True), t_rel, t_hot)
                t = S.do(lambda e: e.activation(bias_rows[0:HEADS, :], bank[0:HEADS, 0:3 * P], ACT.Copy), t)
                banks.release(b, t)
                t = dma("bias", bias_dram.ap(), bias_rows[0:HEADS, :], t)
                shifted = bass.AP(bias_dram.ap().tensor, 1, [[1, P], [3 * P, HEADS], [1, 2 * P]])
                t_flipped.append(dma("bias", bias_flipped.rearrange("p (h s) -> p h s", h=HEADS), shifted, t))

            def flip_bias(n):
                b, bank = banks.take()
                cols = slice(n * HALF, (n + 1) * HALF)
                t = PE.do(lambda e: e.matmul(bank, flip, bias_flipped[:, cols], start=True, stop=True), t_flipped)
                t = S.do(lambda e: e.activation(bias[:, :, :].rearrange("p h s -> p (h s)")[:, cols], bank, ACT.Copy), t)
                banks.release(b, t)
                t_bias.append(t)
            t_flipped, t_bias = [], []

            def turn_ckv(i):
                b, bank = banks.take()
                for u in range(2):
                    for k in range(KC):
                        c = (u * KC + k) * P
                        t = PE.do(lambda e, o=bank[:, c:c + P], s=ckv_t[:, k, (i + u) * P:(i + u + 1) * P]:
                                  e.transpose(o, s, ident[:, :]), kv_t[i // 4][k])
                t_tok[0] = S.do(lambda e, o=ckv_tok[:, i:i + 2, :].rearrange("p a b -> p (a b)"), s=bank:
                                e.activation(o, s, ACT.Copy), t)
                banks.release(b, t_tok[0])

            t_tok, t_qi, t_q = [None], [], [None]
            turn_w_idx()
            S.wait(V.last, G.last)
            for n in range(IDX_HEADS * IDX_DIM // P):
                def evac(h, cols, bank, t, n=n):
                    t_qi.append(S.do(lambda e: e.activation(q_idx[:, n, cols], bank, ACT.Copy), t))
                    return t_qi[-1]
                product(banks, cq_hi, cq_lo, cq_ready, evac)
            bias_by_distance()
            V.wait(everything())
            S.wait(G.last)
            s_banks = Banks([(0, 1), (2, 3)])
            banks = Banks([(4,), (5,), (6,), (7,)])
            t_banks = Banks([(4,), (5,)], (4, P))
            o_banks = Banks([(6,)], (KC, P))
            y_banks = Banks([(7,)], (KC, P))
            used = {}
            keep_ready = {}
            Q_SCALE = float(DH) ** -0.5

            def pick(i):
                n = P * (i + 1)
                room = keep[:, i % KEEP, :]
                scores = work[:, i % 2, :]
                work_name = ("work", i % 2)

                def whole():
                    t = V.do(lambda e: e.tensor_copy(room[:, n - P:n], causal[:, :]), t_causal, used.get(("keep", i % KEEP)))
                    if n > P:
                        t = V.do(lambda e: e.memset(room[:, 0:n - P], 0.0))
                    keep_ready[i] = t
                if n <= TOPK:
                    return [], [(0, whole)]
                last = [None]

                def score(hh):
                    rows = slice(64 * (hh % 2), 64 * (hh % 2) + 64)
                    ends = []
                    for u, a in enumerate(range(0, n, HALF)):
                        z = min(a + HALF, n)
                        b, bank = t_banks.take()
                        flat = bank.rearrange("p a b -> p (a b)")[:, 0:z - a]
                        t = PE.do(lambda e, o=flat, l=q_idx[rows, hh // 2, i * P:(i + 1) * P], r=k_idx[rows, a:z]:
                                  e.matmul(o, l, r, start=True, stop=True))
                        r = relu[:, u, 0:z - a]
                        ta = S.do(lambda e, r=r, s=flat: e.activation(r, s, ACT.Relu), t, used.get(("relu", u)))
                        t_banks.release(b, ta)
                        wcol = w_idx[:, i, hh:hh + 1]
                        o = scores[:, a:z]
                        if hh == 0:
                            tg = S.do(lambda e, o=o, r=r: e.activation(o, r, ACT.Copy, scale=wcol), ta, used.get(work_name))
                        else:
                            ta = S.do(lambda e, r=r: e.activation(r, r, ACT.Copy, scale=wcol), ta)
                            tg = G.do(lambda e, o=o, r=r: e.tensor_tensor(o, o, r, ALU.add), ta, last[0])
                        used[("relu", u)] = tg
                        ends.append(tg)
                    last[0] = ends

                def bound():
                    last[0] = V.do(lambda e: e.tensor_tensor(scores[:, n - P:n], scores[:, n - P:n], causal[:, :], ALU.add),
                                   last[0], t_causal)

                def take8():
                    t = V.do(lambda e: e.max(top8[:, :], scores[:, 0:n]), last[0])
                    last[0] = V.do(lambda e: e.match_replace(scores[:, 0:n], top8[:, :], scores[:, 0:n], TAKEN), t)

                def finish():
                    t = V.do(lambda e: e.tensor_scalar(room[:, 0:n], scores[:, 0:n], TAKEN / 2, MASKED, ALU.is_gt, ALU.mult),
                             last[0], used.get(("keep", i % KEEP)))
                    used[work_name] = keep_ready[i] = t
                price = n / 960 + 0.13
                return ([lambda hh=hh: score(hh) for hh in range(IDX_HEADS)],
                        [(0, bound)] + [(2 * price, take8)] * (TOPK // 8) + [(price, finish)])

            score_steps, round_steps = [], []
            for i in range(NT):
                first, then = pick(i)
                score_steps += [(i, step) for step in first]
                round_steps += [(i, price, step) for price, step in then]
            owed = [0.0]
            PUSH = 1.3

            def pick_ahead(tile, time, n_scores=1):
                for _ in range(n_scores):
                    if score_steps and round_steps and score_steps[0][0] <= round_steps[0][0] + 1:
                        score_steps.pop(0)[1]()
                owed[0] += time
                while round_steps and owed[0] > 0:
                    i, price, step = round_steps[0]
                    if (score_steps and score_steps[0][0] <= i) or i >= tile + KEEP:
                        owed[0] = 0.0
                        break
                    round_steps.pop(0)
                    owed[0] -= price
                    step()

            def pick_all(tile):
                while score_steps and score_steps[0][0] <= tile:
                    score_steps.pop(0)[1]()
                while round_steps and round_steps[0][0] <= tile:
                    round_steps.pop(0)[2]()

            for i in range(0, NT, 2):
                queue_task(None, lambda i=i: turn_ckv(i))
            for n in range(4):
                queue_task(None, lambda n=n: flip_bias(n))
            for hd in range(HEADS):
                def evac_q(h, cols, bank, t, hd=hd):
                    t_q[0] = S.do(lambda e: e.activation(q[:, hd, cols], bank, ACT.Copy), t)
                    return t_q[0]
                product(banks, cq_hi, cq_lo, cq_ready, evac_q)
                pick_ahead(0, 3.0, 2)
            while tasks:
                run_task()
            t_early = everything()
            for line in (PE, S, G, SP):
                line.wait(t_early)

            order = [(i, hd) for i in range(NT) for hd in range(HEADS)]
            q_ready, l_ready, p_ready, pt_ready, o_ready = {}, {}, {}, {}, {}

            def latent_query(s):
                i, hd = order[s]
                b, bank = y_banks.take()
                PE.wait(t_uk)
                for ch in range(KC):
                    t = PE.do(lambda e, ch=ch: e.matmul(bank[:, ch, :], w_uk[:, hd, ch * P:(ch + 1) * P], q[:, hd, i * P:(i + 1) * P],
                                                        start=True, stop=True))
                q_ready[s] = S.do(lambda e: e.activation(q_lat[:, s % 2, :, :], bank, ACT.Copy, scale=Q_SCALE),
                                  t, used.get(("q_lat", s % 2)))
                y_banks.release(b, q_ready[s])

            def logits(s):
                i, hd = order[s]
                n = P * (i + 1)
                b, flat = s_banks.take()
                PE.wait(q_ready[s])
                for a in range(0, n, HALF):
                    z = min(a + HALF, n)
                    for k in range(KC):
                        t = PE.do(lambda e, o=flat[:, a:z], l=q_lat[:, s % 2, k, :], r=ckv_t[:, k, a:z], f=(k == 0), z_=(k == KC - 1):
                                  e.matmul(o, l, r, start=f, stop=z_), mark=(k == KC - 1))
                used[("q_lat", s % 2)] = t
                l_ready[s] = (b, flat, t)

            def weigh(s):
                i, hd = order[s]
                n = P * (i + 1)
                i3, h2, r3 = i % KEEP, s % 2, s % RING
                m = min(n, 2 * P)
                t_near = G.do(lambda e: e.tensor_tensor(near[:, h2, 0:m], keep[:, i3, n - m:n], bias[:, hd, 2 * P - m:2 * P], ALU.add),
                              keep_ready[i], t_bias, used.get(("near", h2)))
                b, flat, t = l_ready[s]
                row = prob[:, r3, :]
                tm = [V.do(lambda e: e.tensor_tensor_reduce(row[:, n - m:n], flat[:, n - m:n], near[:, h2, 0:m], 1.0, LOWEST,
                                                            ALU.add, ALU.max, stat[:, r3, 0:1]),
                           t, t_near, used.get(("prob", r3)))]
                used[("near", h2)] = tm[0]
                if n > m:
                    tm.append(V.do(lambda e: e.tensor_tensor_reduce(row[:, 0:n - m], flat[:, 0:n - m], keep[:, i3, 0:n - m], 1.0, LOWEST,
                                                                    ALU.add, ALU.max, stat[:, r3, 1:2])))
                    t = V.do(lambda e: e.tensor_scalar(stat[:, r3, 2:3], stat[:, r3, 0:1], stat[:, r3, 1:2], -1.0, ALU.max, ALU.mult), tm)
                else:
                    t = V.do(lambda e: e.tensor_scalar(stat[:, r3, 2:3], stat[:, r3, 0:1], -1.0, None, ALU.mult), tm)
                used[("keep", i3)] = tm[-1]
                s_banks.release(b, tm[-1])
                p_ready[s] = S.do(lambda e: e.activation(row[:, 0:n], row[:, 0:n], ACT.Exp, bias=stat[:, r3, 2:3], accum_out=stat[:, r3, 3:4]), t)

            def normalise(s):
                i, hd = order[s]
                n, r3 = P * (i + 1), s % RING
                row = prob[:, r3, :]
                t = V.do(lambda e: e.reciprocal(stat[:, r3, 4:5], stat[:, r3, 3:4]), p_ready[s])
                p_ready[s] = S.do(lambda e: e.activation(row[:, 0:n], row[:, 0:n], ACT.Copy, scale=stat[:, r3, 4:5]), t)

            def turn(s):
                i, hd = order[s]
                h2, r3 = s % 2, s % RING
                ends = []
                for a in range(0, i + 1, 4):
                    z = min(a + 4, i + 1)
                    b, bank = t_banks.take()
                    PE.wait(p_ready[s])
                    for j in range(a, z):
                        t = PE.do(lambda e, o=bank[:, j - a, :], s_=prob[:, r3, j * P:(j + 1) * P]: e.transpose(o, s_, ident[:, :]),
                                  mark=(j == z - 1))
                    te = S.do(lambda e, o=prob_t[:, h2, a:z, :], s_=bank[:, 0:z - a, :]: e.activation(o, s_, ACT.Copy),
                              t, used.get(("prob_t", h2)))
                    t_banks.release(b, te)
                    ends.append(te)
                used[("prob", r3)] = t
                pt_ready[s] = ends

            def gather(s):
                i, hd = order[s]
                h2 = s % 2
                b, bank = o_banks.take()
                PE.wait(pt_ready[s])
                for k in range(KC):
                    for j in range(i + 1):
                        t = PE.do(lambda e, o=bank[:, k, :], l=ckv_tok[:, j, k * P:(k + 1) * P], r=prob_t[:, h2, j, :], f=(j == 0), z=(j == i):
                                  e.matmul(o, l, r, start=f, stop=z), mark=(j == i))
                used[("prob_t", h2)] = t
                o_ready[s] = S.do(lambda e: e.activation(o_lat[:, h2, :, :], bank, ACT.Copy), t, used.get(("o_lat", h2)))
                o_banks.release(b, o_ready[s])

            def values(s):
                i, hd = order[s]
                h2 = s % 2
                b, bank = y_banks.take()
                PE.wait(o_ready[s], t_uv)
                for k in range(KC):
                    t = PE.do(lambda e, k=k: e.matmul(bank[:, 0, :], w_uv[:, hd, k, :], o_lat[:, h2, k, :],
                                                      start=(k == 0), stop=(k == KC - 1)), mark=(k == KC - 1))
                used[("o_lat", h2)] = t
                y_done[hd][i // 4] = S.do(lambda e: e.activation(x[:, hd, i * P:(i + 1) * P], bank[:, 0, :], ACT.Copy), t)
                y_banks.release(b, y_done[hd][i // 4])

            y_done = [[None] * NH for _ in range(HEADS)]
            latent_query(0)
            latent_query(1)
            logits(0)
            for s in range(len(order) + 4):
                i = order[s][0] if s < len(order) else NT
                time = 1.07 * (i + 1) + 0.85 - (0.133 * (i + 1) + 0.3)
                if s < len(order) and order[s][1] == 0:
                    pick_all(i)
                if s >= 4:
                    values(s - 4)
                if s < len(order):
                    if s + 1 < len(order):
                        logits(s + 1)
                    weigh(s)
                    pick_ahead(i, 2.0)
                    normalise(s)
                if 3 <= s < len(order) + 3:
                    gather(s - 3)
                if s + 2 < len(order):
                    latent_query(s + 2)
                if 2 <= s < len(order) + 2:
                    turn(s - 2)
                pick_ahead(i, PUSH * time - 2.0, 0)

            y_ready = [[], []]
            change_rooms(PE.last)
            banks = Banks(all_banks)
            w.hand_on()
            for h in range(NH):
                for k in range(KD):
                    split_halves(h_hi[:, k, :], h_lo[:, k, :], x[:, k, :], y_ready, y_done[k], (V, G)[k % 2], [h])
            for k in range(KD):
                x_ready[k] = [dma(f"x{k}", x[:, k, :], x_park[:, k, :], y_ready[0][k], y_ready[1][k], t_park)]
            out_projection(banks, h_hi, h_lo, y_ready, 8 * KD, x_ready, (None,), everything(), pair=True)
            return gains(3 * KD, 10 * KD, "g_ffn_2", 0, V.last)

        FFN_GROUPS = [range(0, 6), range(6, 12), range(12, 17), range(17, KF)]

        def ffn_items():
            w_in, w_out = ins["f_w_in_2"][0], ins["f_w_out_2"][0]
            items = []
            for grp in FFN_GROUPS:
                for n in grp:
                    items += [item(w_in, n), item(w_in, KF + n)]
                items += [item(w_out[grp[0] * P:(grp[-1] + 1) * P, :], d) for d in range(KD)]
            return items

        def stage_ffn(t_gain):
            banks = Banks(all_banks)
            area = Area(STAGE_AT, NORM_AT - STAGE_AT)
            release = everything()
            w.hand_on()
            h_ready = modulated_norm(banks, 3 * KD, 9 * KD, x_ready, t_gain)
            change_rooms(release)
            y_hi, y_lo = area.sb("f_hi", [P, 6, T], F32R), area.sb("f_lo", [P, 6, T], F32R)
            u_pad, cv, yv = area.sb("u_pad", [P, T + 2]), area.sb("f_cv", [P, T]), area.sb("f_yv", [P, T])
            t_edge = V.do(lambda e: e.memset(u_pad[:, 0:2], 0.0))
            y_free = u_free = cv_free = None
            yv_free = [None, None]
            for grp in FFN_GROUPS:
                y_ready = [[], []]
                for i, n in enumerate(grp):
                    tu, ty = [], []

                    def evac_u(h, cols, bank, t):
                        a = 2 + h * HALF
                        tu.append(S.do(lambda e: e.activation(u_pad[:, a:a + HALF], bank, ACT.Copy), t, u_free))
                        return tu[-1]

                    def convolve(n=n):
                        t = V.do(lambda e: e.tensor_scalar(cv[:, :], u_pad[:, 0:T], par("f_conv_w_2", n), None, ALU.mult),
                                 tu, t_edge, cv_free)
                        for tap in (1, 2):
                            t = V.do(lambda e, tap=tap: e.scalar_tensor_tensor(
                                out=cv[:, :], in0=u_pad[:, tap:tap + T], scalar=par("f_conv_w_2", tap * KF + n),
                                in1=cv[:, :], op0=ALU.mult, op1=ALU.add), t)
                        return t, S.do(lambda e: e.activation(cv[:, :], cv[:, :], ACT.Gelu, bias=par("f_conv_b_2", n)), t)

                    def evac_v(h, cols, bank, t):
                        if not conv:
                            conv.extend(convolve())
                        ty.append(V.do(lambda e: e.tensor_tensor(yv[:, cols], bank, cv[:, cols], ALU.mult), t, conv[1], yv_free[h]))
                        return ty[-1]
                    conv = []
                    if n == 0:
                        product_pair(banks, h_hi, h_lo, h_ready, [evac_u, evac_v], False)
                    else:
                        product(banks, h_hi, h_lo, h_ready, evac_u)
                        conv.extend(convolve())
                        product(banks, h_hi, h_lo, h_ready, evac_v)
                    u_free = conv[0]
                    cv_free = ty[-1]
                    S.wait(y_free)
                    split_halves(y_hi[:, i, :], y_lo[:, i, :], yv, y_ready, ty)
                    yv_free = [y_ready[0][-1], y_ready[1][-1]]
                out_projection(banks, y_hi, y_lo, y_ready, 11 * KD, x_ready, (None,) if grp is FFN_GROUPS[-1] else ())
                y_free = PE.last

        def stage_end():
            banks = Banks(all_banks)
            area = Area(H_AT, 4 * NT * D)
            o_rows = area.sb("o_rows", [P, NT, D])
            change_rooms(PE.last, x_ready)
            for h in range(NH):
                cols = slice(h * HALF, (h + 1) * HALF)
                ends = x_ready
                t = inverse_root(banks, token_sums(banks, 0, h), h, D, 0)
                b, r, t = spread(banks, h, 0, t)
                ends = [V.do(lambda e, k=k, r=r, cols=cols: e.scalar_tensor_tensor(
                    out=x[:, k, cols], in0=x[:, k, cols], scalar=par("g_final_2", k), in1=r,
                    op0=ALU.mult, op1=ALU.mult), t, x_ready[k]) for k in range(KD)]
                banks.release(b, ends[-1])
                for i in range(4 * h, 4 * h + 4):
                    moved = []
                    for q in range(2):
                        b, bank = banks.take()
                        for k in range(4):
                            t = PE.do(lambda e, i=i, k=k, q=q, bank=bank: e.transpose(
                                bank[:, k * P:(k + 1) * P], x[:, 4 * q + k, i * P:(i + 1) * P], ident[:, :]),
                                ends[4 * q + k], mark=(k == 3))
                        dst = o_rows[:, i, 4 * q * P:(4 * q + 4) * P]
                        if q:
                            t = S.do(lambda e, dst=dst, bank=bank: e.activation(dst, bank, ACT.Copy), t)
                        else:
                            t = V.do(lambda e, dst=dst, bank=bank: e.tensor_copy(dst, bank), t)
                        banks.release(b, t)
                        moved.append(t)
                    t_out = dma("out", out[0, i * P:(i + 1) * P, :], o_rows[:, i, :], moved)
            SP.wait(t_out)

        w.items += conv_items()
        w.items += dilated_items()
        w.items += latent_items()
        w.items += ffn_items()
        t = stage_setup()
        t = stage_conv(t)
        stage_dilated(t)
        release = everything()
        h_ready = stage_between()
        t = stage_latent(release, h_ready)
        stage_ffn(t)
        stage_end()

        block = ctx.enter_context(nc.Block())

        @block.tensor
        def _(e):
            for step in PE.steps:
                step(e)

        @block.vector
        def _(e):
            for step in V.steps:
                step(e)

        @block.scalar
        def _(e):
            for step in S.steps:
                step(e)

        @block.gpsimd
        def _(e):
            for step in G.steps:
                step(e)

        @block.sync
        def _(e):
            for step in SP.steps:
                step(e)


_INS = ["x", "c", "norm_g", "w_mod", "b_mod", "conv_w_in", "conv_k", "conv_w_out", "dil_w_in", "dil_w_out",
        "final_g", "c_2", "rel_bias_2", "a_w_in_2", "a_g_cq_2", "a_g_ckv_2", "a_w_uq_2", "a_w_uk_2",
        "a_w_uv_2", "a_w_qi_2", "a_w_o_2", "ada_w_2", "ada_b_2", "g_mix_2", "g_ffn_2", "f_w_in_2",
        "f_conv_w_2", "f_conv_b_2", "f_w_out_2", "g_final_2"]


def kernel(**inputs):
    import concourse.bacc as bacc
    from concourse.bass_utils import run_bass_kernel_spmd

    nc = bacc.Bacc("TRN2", target_bir_lowering=False, num_devices=1)
    arrays = {f"in_{n}": np.ascontiguousarray(inputs[n]) for n in _INS}
    arrays.update({f"in_{n}": a for n, a in shape_constants().items()})
    aps = {n[3:]: nc.dram_tensor(n, a.shape, F32, kind="ExternalInput").ap() for n, a in arrays.items()}
    out = nc.dram_tensor("out_x", (1, T, D), F32, kind="ExternalOutput").ap()
    build(nc, aps, out)
    r = run_bass_kernel_spmd(nc, [arrays], core_ids=[0])
    return r.results[0]["out_x"]
```
